# Optimizing a Trainium2 kernel written in Bass

```python
import math
import jax
import jax.numpy as jnp
from jax import lax
import numpy as np

D_MODEL = 1024
BATCH = 1
SEQ = 256
DEPTH = 1

N_HEADS = 16
N_KV_GROUPS = 4
HEADS_PER_GROUP = N_HEADS // N_KV_GROUPS
D_QK = 96
D_V = 64
CMP_BLOCK = 32
CMP_STRIDE = 16
CMP_HIDDEN = 256
SLC_BLOCK = 64
SLC_TOPN = 16
SLC_QUERY_BLOCK = 64
WINDOW = 512
WIN_QUERY_BLOCK = 128
ATTN_SCALE = D_QK ** -0.5
FORCE_BONUS = 1e6
N_BUCKETS = 32
MAX_DISTANCE = 128
CONV_CHANNELS = D_MODEL
CONV_WIDTH = 31
PEER_HEADS = 8
PEER_NKEYS = 128
PEER_EXPERTS = PEER_NKEYS * PEER_NKEYS
PEER_DQ = 256
PEER_TOPK = 16
PEER_TOKEN_BLOCK = 128
Q_COLS = N_HEADS * D_QK
K_COLS = N_KV_GROUPS * D_QK
V_COLS = N_KV_GROUPS * D_V
NSA_GATE_COLS = 3 * N_HEADS
GLU_COLS = 2 * CONV_CHANNELS
MERGE_COLS = 2 * D_MODEL
IN_SPLITS = (Q_COLS, K_COLS, K_COLS, K_COLS, V_COLS, V_COLS, V_COLS, NSA_GATE_COLS, GLU_COLS, MERGE_COLS)
IN_COLS = sum(IN_SPLITS)
NORM_EPS = 1e-6
NEG_INF = -1e30

kernel_name = 'hybrid_nsa_conformer_peer_block'

def rmsnorm(x, g):
    xf = x.astype(jnp.float32)
    y = xf * lax.rsqrt(jnp.mean(xf * xf, axis=-1, keepdims=True) + NORM_EPS)
    return (y * g).astype(x.dtype)

def layernorm(x, g, b):
    xf = x.astype(jnp.float32)
    xc = xf - jnp.mean(xf, axis=-1, keepdims=True)
    y = xc * lax.rsqrt(jnp.mean(xc * xc, axis=-1, keepdims=True) + NORM_EPS)
    return (y * g + b).astype(x.dtype)

def t5_bucket(dist):
    n = jnp.maximum(dist, 0)
    max_exact = N_BUCKETS // 2
    nf = jnp.maximum(n, 1).astype(jnp.float32)
    large = max_exact + (jnp.log(nf / max_exact) / math.log(MAX_DISTANCE / max_exact) * (N_BUCKETS - max_exact)).astype(jnp.int32)
    return jnp.where(n < max_exact, n, jnp.minimum(large, N_BUCKETS - 1))

def head_bias(rel_table, dist):
    b = jnp.moveaxis(rel_table[t5_bucket(dist)], -1, 0)
    return b.reshape((N_KV_GROUPS, HEADS_PER_GROUP) + dist.shape).astype(jnp.float32)

def masked_softmax(logits, mask):
    p = jax.nn.softmax(jnp.where(mask, logits, NEG_INF), axis=-1)
    return jnp.where(mask, p, 0.0)

def compress_kv(kv, w1, w2, pos_emb):
    B, G, S, d = kv.shape
    n_sub = CMP_BLOCK // CMP_STRIDE
    n_chunk = S // CMP_STRIDE
    n_cmp = n_chunk - n_sub + 1
    chunks = kv.reshape(B, G, n_chunk, CMP_STRIDE, d)
    blocks = jnp.concatenate([chunks[:, :, i:i + n_cmp] for i in range(n_sub)], axis=3) + pos_emb
    return jax.nn.gelu(blocks.reshape(B, G, n_cmp, CMP_BLOCK * d) @ w1) @ w2

def nsa_attention(q, k_cmp, k_slc, k_win, v_cmp, v_slc, v_win, gate_logits, rel_table, w1k, w2k, pos_k, w1v, w2v, pos_v):
    B, G, R, S, _ = q.shape
    t = jnp.arange(S)

    kc = compress_kv(k_cmp, w1k, w2k, pos_k)
    vc = compress_kv(v_cmp, w1v, w2v, pos_v)
    n_cmp = kc.shape[2]
    cmp_start = jnp.arange(n_cmp) * CMP_STRIDE
    cmp_end = cmp_start + CMP_BLOCK - 1
    dist_c = t[:, None] - cmp_end[None, :]
    logits = jnp.einsum('bgrsd,bgnd->bgrsn', q, kc).astype(jnp.float32) * ATTN_SCALE + head_bias(rel_table, dist_c)
    p_cmp = masked_softmax(logits, dist_c >= 0)
    o_cmp = jnp.einsum('bgrsn,bgnd->bgrsd', p_cmp.astype(vc.dtype), vc)

    n_slc = S // SLC_BLOCK
    n_sel = min(SLC_TOPN, n_slc)
    slc_start = jnp.arange(n_slc) * SLC_BLOCK
    overlap = ((cmp_start[:, None] <= slc_start[None, :] + SLC_BLOCK - 1) & (cmp_end[:, None] >= slc_start[None, :])).astype(jnp.float32)
    imp = jnp.einsum('bgsn,nj->bgsj', p_cmp.sum(axis=2), overlap)
    j = jnp.arange(n_slc)[None, :]
    cur = (t // SLC_BLOCK)[:, None]
    forced = (j == 0) | (j == cur) | (j == cur - 1)
    score = jnp.where(j <= cur, imp + jnp.where(forced, FORCE_BONUS, 0.0), NEG_INF)
    _, sel = lax.top_k(score, n_sel)

    ks_blocks = k_slc.reshape(B, G, n_slc, SLC_BLOCK, D_QK)
    vs_blocks = v_slc.reshape(B, G, n_slc, SLC_BLOCK, D_V)
    nqs = S // SLC_QUERY_BLOCK
    q_s = q.reshape(B, G, R, nqs, SLC_QUERY_BLOCK, D_QK).transpose(0, 3, 1, 2, 4, 5).reshape(B * nqs, G, R, SLC_QUERY_BLOCK, D_QK)
    sel_s = sel.reshape(B, G, nqs, SLC_QUERY_BLOCK, n_sel).transpose(0, 2, 1, 3, 4).reshape(B * nqs, G, SLC_QUERY_BLOCK, n_sel)
    b_ids = jnp.repeat(jnp.arange(B), nqs)
    s_ids = jnp.tile(jnp.arange(nqs) * SLC_QUERY_BLOCK, B)
    table_gr = rel_table.reshape(N_BUCKETS, G, R).transpose(1, 0, 2)
    in_blk = jnp.arange(SLC_BLOCK)
    q_off = jnp.arange(SLC_QUERY_BLOCK)
    n_keys = n_sel * SLC_BLOCK

    def selected_block(args):
        b, s0, qb, ib = args
        kg = jax.vmap(lambda kk, ii: kk[ii])(ks_blocks[b], ib).reshape(G, SLC_QUERY_BLOCK, n_keys, D_QK)
        vg = jax.vmap(lambda vv, ii: vv[ii])(vs_blocks[b], ib).reshape(G, SLC_QUERY_BLOCK, n_keys, D_V)
        kpos = (ib[..., None] * SLC_BLOCK + in_blk).reshape(G, SLC_QUERY_BLOCK, n_keys)
        dist = (s0 + q_off)[None, :, None] - kpos
        bias = jax.vmap(lambda tb, bk: jnp.take(tb, bk, axis=0))(table_gr, t5_bucket(dist))
        logits = jnp.einsum('grqd,gqkd->grqk', qb, kg).astype(jnp.float32) * ATTN_SCALE + bias.transpose(0, 3, 1, 2).astype(jnp.float32)
        p = masked_softmax(logits, (dist >= 0)[:, None])
        return jnp.einsum('grqk,gqkd->grqd', p.astype(vg.dtype), vg)

    o_slc = lax.map(selected_block, (b_ids, s_ids, q_s, sel_s))
    o_slc = o_slc.reshape(B, nqs, G, R, SLC_QUERY_BLOCK, D_V).transpose(0, 2, 3, 1, 4, 5).reshape(B, G, R, S, D_V)

    span = WIN_QUERY_BLOCK + WINDOW
    pad = ((0, 0), (0, 0), (WINDOW, 0), (0, 0))
    kp = jnp.pad(k_win, pad)
    vp = jnp.pad(v_win, pad)
    qi = jnp.arange(WIN_QUERY_BLOCK)[:, None]
    kj = jnp.arange(span)[None, :]
    dist_w = WINDOW + qi - kj
    band = (dist_w >= 0) & (dist_w < WINDOW)
    bias_w = head_bias(rel_table, dist_w)
    nqw = S // WIN_QUERY_BLOCK
    q_w = q.reshape(B, G, R, nqw, WIN_QUERY_BLOCK, D_QK).transpose(3, 0, 1, 2, 4, 5)

    def window_block(args):
        qb, s0 = args
        kb = lax.dynamic_slice_in_dim(kp, s0, span, axis=2)
        vb = lax.dynamic_slice_in_dim(vp, s0, span, axis=2)
        logits = jnp.einsum('bgrqd,bgkd->bgrqk', qb, kb).astype(jnp.float32) * ATTN_SCALE + bias_w
        p = masked_softmax(logits, band & (kj >= WINDOW - s0))
        return jnp.einsum('bgrqk,bgkd->bgrqd', p.astype(vb.dtype), vb)

    o_win = lax.map(window_block, (q_w, jnp.arange(nqw) * WIN_QUERY_BLOCK))
    o_win = o_win.transpose(1, 2, 3, 0, 4, 5).reshape(B, G, R, S, D_V)

    g = jax.nn.sigmoid(gate_logits.astype(jnp.float32)).reshape(B, S, 3, G, R).transpose(2, 0, 3, 4, 1)[..., None]
    o = g[0] * o_cmp + g[1] * o_slc + g[2] * o_win
    return o.transpose(0, 3, 1, 2, 4).reshape(B, S, N_HEADS * D_V).astype(q.dtype)

def conformer_conv(glu_in, w_dw, b_dw, ln_g, ln_b):
    a, gate = jnp.split(glu_in, 2, axis=-1)
    u = a * jax.nn.sigmoid(gate)
    y = lax.conv_general_dilated(u, w_dw, window_strides=(1,), padding=[(CONV_WIDTH - 1, 0)],
                                 dimension_numbers=('NWC', 'WIO', 'NWC'), feature_group_count=CONV_CHANNELS) + b_dw
    return jax.nn.silu(layernorm(y, ln_g, ln_b))

def to_groups(z, d):
    B, S, _ = z.shape
    return z.reshape(B, S, N_KV_GROUPS, d).transpose(0, 2, 1, 3)

def token_mixer(h, w_in, rel_table, w1k, w2k, pos_k, w1v, w2v, pos_v, w_attn_out, conv_w, conv_b, conv_ln_g, conv_ln_b, w_conv_out, w_out):
    B, S, _ = h.shape
    offsets = [int(o) for o in np.cumsum(IN_SPLITS)[:-1]]
    q, k_c, k_s, k_w, v_c, v_s, v_w, g_nsa, glu_in, g_merge = jnp.split(h @ w_in, offsets, axis=-1)
    q = q.reshape(B, S, N_KV_GROUPS, HEADS_PER_GROUP, D_QK).transpose(0, 2, 3, 1, 4)
    attn = nsa_attention(q, to_groups(k_c, D_QK), to_groups(k_s, D_QK), to_groups(k_w, D_QK),
                         to_groups(v_c, D_V), to_groups(v_s, D_V), to_groups(v_w, D_V), g_nsa,
                         rel_table, w1k, w2k, pos_k, w1v, w2v, pos_v)
    y_a = attn @ w_attn_out
    y_b = conformer_conv(glu_in, conv_w, conv_b, conv_ln_g, conv_ln_b) @ w_conv_out
    g_a, g_b = jnp.split(g_merge, 2, axis=-1)
    y = jax.nn.sigmoid(g_a) * y_a + jax.nn.sigmoid(g_b) * y_b
    return y @ w_out

def peer_ffn(h, w_q, sub_keys, u, v):
    B, S, D = h.shape
    T = B * S
    hf = h.reshape(T, D)
    q = (hf @ w_q).reshape(T, PEER_HEADS, 2, PEER_DQ // 2)
    s = jnp.einsum('thcd,hckd->thck', q, sub_keys).astype(jnp.float32)
    s1, i1 = lax.top_k(s[:, :, 0], PEER_TOPK)
    s2, i2 = lax.top_k(s[:, :, 1], PEER_TOPK)
    cand = (s1[..., :, None] + s2[..., None, :]).reshape(T, PEER_HEADS, PEER_TOPK * PEER_TOPK)
    cand_idx = (i1[..., :, None] * PEER_NKEYS + i2[..., None, :]).reshape(T, PEER_HEADS, PEER_TOPK * PEER_TOPK)
    top_s, pos = lax.top_k(cand, PEER_TOPK)
    expert_idx = jnp.take_along_axis(cand_idx, pos, axis=-1)
    weights = jax.nn.softmax(top_s, axis=-1)
    n_blk = T // PEER_TOKEN_BLOCK
    n_e = PEER_HEADS * PEER_TOPK
    xs = (hf.reshape(n_blk, PEER_TOKEN_BLOCK, D),
          expert_idx.reshape(n_blk, PEER_TOKEN_BLOCK, n_e),
          weights.reshape(n_blk, PEER_TOKEN_BLOCK, n_e))

    def token_block(args):
        hc, ec, wc = args
        act = jax.nn.gelu(jnp.einsum('cd,ced->ce', hc, u[ec]))
        coef = (act.astype(jnp.float32) * wc).astype(hc.dtype)
        return jnp.einsum('ce,ced->cd', coef, v[ec])

    return lax.map(token_block, xs).reshape(B, S, D)

def setup_inputs(seed: int = 0) -> dict:
    key = jax.random.key(seed)
    ks = jax.random.split(key, 27)
    f32 = jnp.float32
    L = DEPTH
    D = D_MODEL

    def nrm(k, shape, scale):
        return jax.random.normal(k, shape, f32) * scale

    return {
        'x': nrm(ks[0], (BATCH, SEQ, D), 1.0),
        'c': nrm(ks[1], (BATCH, D), 1.0),
        'w_ada': nrm(ks[2], (L, D, 6 * D), 0.5 * D ** -0.5),
        'b_ada': nrm(ks[3], (L, 6 * D), 0.01),
        'g_pre_mix': 1.0 + nrm(ks[4], (L, D), 0.01),
        'g_post_mix': 1.0 + nrm(ks[5], (L, D), 0.01),
        'g_pre_ffn': 1.0 + nrm(ks[6], (L, D), 0.01),
        'g_post_ffn': 1.0 + nrm(ks[7], (L, D), 0.01),
        'rel_table': nrm(ks[8], (N_BUCKETS, N_HEADS), 0.5),
        'w_in': nrm(ks[9], (L, D, IN_COLS), D ** -0.5),
        'cmp_w1k': nrm(ks[10], (L, CMP_BLOCK * D_QK, CMP_HIDDEN), (CMP_BLOCK * D_QK) ** -0.5),
        'cmp_w2k': nrm(ks[11], (L, CMP_HIDDEN, D_QK), CMP_HIDDEN ** -0.5),
        'cmp_pos_k': nrm(ks[12], (L, CMP_BLOCK, D_QK), 0.1),
        'cmp_w1v': nrm(ks[13], (L, CMP_BLOCK * D_V, CMP_HIDDEN), (CMP_BLOCK * D_V) ** -0.5),
        'cmp_w2v': nrm(ks[14], (L, CMP_HIDDEN, D_V), CMP_HIDDEN ** -0.5),
        'cmp_pos_v': nrm(ks[15], (L, CMP_BLOCK, D_V), 0.1),
        'w_attn_out': nrm(ks[16], (L, N_HEADS * D_V, D), (N_HEADS * D_V) ** -0.5),
        'conv_w': nrm(ks[17], (L, CONV_WIDTH, 1, CONV_CHANNELS), CONV_WIDTH ** -0.5),
        'conv_b': nrm(ks[18], (L, CONV_CHANNELS), 0.01),
        'conv_ln_g': 1.0 + nrm(ks[19], (L, CONV_CHANNELS), 0.01),
        'conv_ln_b': nrm(ks[20], (L, CONV_CHANNELS), 0.01),
        'w_conv_out': nrm(ks[21], (L, CONV_CHANNELS, D), CONV_CHANNELS ** -0.5),
        'w_out': nrm(ks[22], (L, D, D), D ** -0.5),
        'peer_wq': nrm(ks[23], (L, D, PEER_HEADS * PEER_DQ), D ** -0.5),
        'peer_subkeys': nrm(ks[24], (L, PEER_HEADS, 2, PEER_NKEYS, PEER_DQ // 2), (PEER_DQ // 2) ** -0.5),
        'peer_u': nrm(ks[25], (L, PEER_EXPERTS, D), D ** -0.5),
        'peer_v': nrm(ks[26], (L, PEER_EXPERTS, D), 1.0),
    }

def reference(x, c, w_ada, b_ada, g_pre_mix, g_post_mix, g_pre_ffn, g_post_ffn, rel_table, w_in,
              cmp_w1k, cmp_w2k, cmp_pos_k, cmp_w1v, cmp_w2v, cmp_pos_v, w_attn_out,
              conv_w, conv_b, conv_ln_g, conv_ln_b, w_conv_out, w_out,
              peer_wq, peer_subkeys, peer_u, peer_v):
    c_act = jax.nn.silu(c)
    for layer in range(DEPTH):
        mod = (c_act @ w_ada[layer] + b_ada[layer])[:, None, :]
        sh1, sc1, gt1, sh2, sc2, gt2 = jnp.split(mod, 6, axis=-1)
        h = rmsnorm(x, g_pre_mix[layer]) * (1.0 + sc1) + sh1
        y = token_mixer(h, w_in[layer], rel_table, cmp_w1k[layer], cmp_w2k[layer], cmp_pos_k[layer],
                        cmp_w1v[layer], cmp_w2v[layer], cmp_pos_v[layer], w_attn_out[layer],
                        conv_w[layer], conv_b[layer], conv_ln_g[layer], conv_ln_b[layer],
                        w_conv_out[layer], w_out[layer])
        x = x + gt1 * rmsnorm(y, g_post_mix[layer])
        h = rmsnorm(x, g_pre_ffn[layer]) * (1.0 + sc2) + sh2
        y = peer_ffn(h, peer_wq[layer], peer_subkeys[layer], peer_u[layer], peer_v[layer])
        x = x + gt2 * rmsnorm(y, g_post_ffn[layer])
    return x


_drawn_inputs = setup_inputs


def setup_inputs(seed=0):
    import zlib

    import numpy as np

    out = dict(_drawn_inputs(seed))
    spreads = {}
    factors = {'g_pre_mix': 3.059,
     'g_post_mix': 2.957,
     'g_post_ffn': 8.0,
     'cmp_pos_k': 3.898,
     'conv_b': 2.754,
     'conv_ln_g': 3.378,
     'conv_ln_b': 3.417}
    for name, (base, spread) in spreads.items():
        noise = np.random.default_rng([zlib.crc32(name.encode()), seed]).standard_normal(out[name].shape)
        drawn = base * np.exp(spread * noise) if base else spread * noise
        out[name] = jnp.asarray(drawn.astype(out[name].dtype))
    for name, factor in factors.items():
        out[name] = (out[name] * factor).astype(out[name].dtype)
    return out
```

```python
from contextlib import ExitStack

import numpy as np

import concourse.bass as bass
from concourse import mybir

F32 = mybir.dt.float32
I32 = mybir.dt.int32
U32 = mybir.dt.uint32
ALU = mybir.AluOpType
ACT = mybir.ActivationFunctionType
AX = mybir.AxisListType.X

P = 128
D = 1024
DT = D // P
SEQ = 256
TT = SEQ // P
HEADS = 16
GROUPS = 4
REP = HEADS // GROUPS
DQK = 96
DV = 64
CMP_L = 32
CMP_ST = 16
NCMP = SEQ // CMP_ST - 1
HID = 256
SCALE = DQK ** -0.5
BUCKETS = 32
MAXDIST = 128
TAPS = 31
PADT = TAPS - 1
PH = 8
NK = 128
TOPK = 16
NE = PH * TOPK
REV = 2 * SEQ - 1
EPS = 1e-6
NEG = -1e30

RING = 8
CH = 8
CPT = NE // CH
R_GLU, R_MERGE, R_GROUP, R_V, R_CO, R_AO, R_OUT, R_WQ, ROUNDS = 0, 2, 4, 8, 9, 10, 11, 12, 14

C_BADA, C_GPM, C_GOM, C_GPF, C_GOF, C_CB, C_LG, C_LB, C_CW = 0, 48, 56, 64, 72, 80, 88, 96, 104
NCOLS = C_CW + TAPS * DT


class Chain:

    def __init__(self, eng, sem):
        self.eng, self.sem, self.n, self.k = eng, sem, 0, 0

    def add(self, ins):
        ins.then_inc(self.sem, 1)
        self.k += 1
        return self.n + self.k

    def link(self, ins):
        self.eng.wait_ge(self.sem, self.add(ins))

    def enter(self, i, per):
        self.base, self.per = self.n + self.k, per
        self.n, self.k = self.base + i * per, 0

    def leave(self, times):
        assert self.k == self.per, self.k
        self.n, self.k = self.base + self.per * times, 0


def build(nc, a, out):
    ctx = ExitStack()
    with ctx:
        def sb(name, shape, dt=F32):
            return ctx.enter_context(nc.sbuf_tensor(name, shape, dt))

        def sem(name):
            return ctx.enter_context(nc.semaphore(name))

        arena = sb("arena", [P, 16, D])
        ring = arena[:, 0:8, :]
        adaw = arena[:, 8:16, :]
        w1 = arena[:, 8:16, :].rearrange("p a b -> p (a b)").rearrange("p (l n) -> p l n", n=HID)
        urow = arena[:, 0:8, :]
        vrow = arena[:, 8:16, :]
        x = sb("x", [P, TT, D])
        hT = sb("hT", [P, DT, SEQ])
        qT = sb("qT", [P, HEADS, SEQ])
        kT_ = sb("kT", [P, GROUPS * 3 * SEQ])
        kT = kT_[:, :].rearrange("p (g b t) -> p g b t", g=GROUPS, b=3)
        subk = kT_[:, 0:2 * PH * NK].rearrange("p (m k) -> p m k", k=NK)
        vcT = sb("vcT", [P, GROUPS, SEQ])
        V = sb("V", [P, TT, 2 * GROUPS * DV])
        gates = sb("gates", [P, TT, 3, HEADS])
        upad_ = sb("upad", [P, DT * (PADT + SEQ)])
        upad = upad_[:, :].rearrange("p (j t) -> p j t", j=DT)
        cand = upad_[:, 0:PH * TOPK * TOPK].rearrange("p (h c) -> p h c", h=PH)
        y = sb("y", [P, DT, SEQ])
        swork = y[:, :, :].rearrange("p a b -> p (a b)").rearrange("p (m k) -> p m k", k=NK)
        sig = sb("sig", [P, 2 * DT, SEQ])
        h2 = sig[:, 0:8, :].rearrange("p a b -> p (a b)").rearrange("p (t d) -> p t d", t=TT)
        tb = sb("tb", [P, HEADS, SEQ])
        tbf = tb[:, :, :].rearrange("p a b -> p (a b)")
        ohc = tbf[0:BUCKETS + 1, 0:NCMP * SEQ].rearrange("p (n t) -> p n t", n=NCMP)
        rows = tbf.rearrange("p (v d) -> p v d", v=4)
        sc = sb("sc", [P, 4096])
        xs = sc[:, 0:2048].rearrange("p (t d) -> p t d", t=TT)
        ohr = sc[0:BUCKETS + 1, 2048:2560]
        cact = sc[:, 3072:4096]
        kcA, kcB, vcA, vcB = (sc[:, 1024 * i:1024 * i + 1024].rearrange("p (g t) -> p g t", g=GROUPS)
                              for i in range(4))
        attn = xs
        attnT = sc[:, 2048:4096].rearrange("p (j t) -> p j t", j=DT)
        cwork = sc[:, 0:2048].rearrange("p (h c) -> p h c", h=PH)
        oneh = sc[:, 2048:4096].rearrange("p (e c) -> p e c", c=TOPK)
        S_ = sb("S", [P, 2 * 2 * SEQ])
        S = S_[:, :].rearrange("p (u b t) -> p u b t", u=2, b=2)
        revsb = S_[0:HEADS, 0:512]
        wide = S_[:, :].rearrange("p (j t) -> p j t", j=DT)
        junk = S_[:, :]
        PT = sb("PT", [P, 2, 512])
        tmp = PT[:, :, :].rearrange("p a b -> p (a b)")
        PcT = sb("PcT", [P, 512])
        cols = sb("cols", [P, NCOLS])
        mod = sb("mod", [P, 48])
        modst = sb("modst", [P, 8])
        A1 = sb("A1", [P, DT])
        vec4 = sb("vec4", [P, 4, DT])
        table = sb("table", [BUCKETS + 1, HEADS])
        posk = sb("posk", [DQK, CMP_L])
        posv = sb("posv", [DV, CMP_L])
        w2k = sb("w2k", [P, 2, DQK])
        w2v = sb("w2v", [P, 2, DV])
        hidk = sb("hidk", [P, 2, 64])
        hidv = sb("hidv", [P, 2, 64])
        kcT = sb("kcT", [DQK, GROUPS * NCMP])
        vcv = sb("vcv", [NCMP, GROUPS * DV])
        tbc = sb("tbc", [P, TT, HEADS, NCMP])
        Sc = sb("Sc", [P, REP, NCMP])
        nmc = sb("nmc", [P, REP])
        nm = sb("nm", [P, 2, 2])
        Z = sb("Z", [P, 2, REP, 3])
        rz = sb("rz", [P, REP, 3])
        coef = sb("coef", [P, REP, 3])
        otmp = sb("otmp", [P, 2, 2 * 3 * DV])
        ident = sb("ident", [P, P])
        ones = sb("ones", [P, P])
        iota16 = sb("iota16", [P, TOPK])
        rowok = sb("rowok", [P, 1])
        eps = sb("eps", [P, 1])
        ss = sb("ss", [P, 8])
        std = sb("std", [P, 8])
        rstd = sb("rstd", [P, 8])
        stdc = sb("stdc", [P, SEQ])
        Vf = V[:, :, :].rearrange("p a b -> p (a b)")
        v16 = Vf[:, 0:256].rearrange("p (m k) -> p m k", k=TOPK)
        i16 = Vf[:, 256:512].bitcast(U32).rearrange("p (m k) -> p m k", k=TOPK)
        i16f = Vf[:, 512:768].rearrange("p (m k) -> p m k", k=TOPK)
        t16 = Vf[:, 768:896].rearrange("p (m k) -> p m k", k=TOPK)
        p16 = Vf[:, 896:1024].bitcast(U32)
        spare = kT_[:, 2 * PH * NK:]
        pa = spare[:, 0:NE].bitcast(U32)
        paf = spare[:, NE:2 * NE]
        e1 = spare[:, 2 * NE:3 * NE]
        e2 = spare[:, 3 * NE:4 * NE]
        idx = sb("idx", [P, TT * CPT, CH], I32)
        wgt = sb("wgt", [P, TT * CPT, CH])
        wsum = sb("wsum", [P, PH])
        stage = sb("stage", [P, 2, CH], I32)
        dot = sb("dot", [P, 2, CH])
        gl = sb("gl", [P, 2, CH])
        cf = sb("cf", [P, 2, CH])
        diag = hT[:, :, :].rearrange("p a b -> p (a b)").rearrange("p (u s c) -> p u s c", u=2, s=CH)
        pb = ctx.enter_context(nc.psum_tensor("pb", [P, 8, 512], F32))

        s_x, s_c, s_cols, s_tbl, s_oh, s_small = (sem(n) for n in
                                                  ("x_in", "c_in", "cols_in", "table_in", "onehot_in", "small_in"))
        ring_in = [sem(f"ring_in{i}") for i in range(RING)]
        ada_in = [sem(f"ada_in{i}") for i in range(8)]
        ada_more = [sem(f"ada_more{i}") for i in range(8)]
        rev_out, tb_in, w1_in, sub_in = sem("rev_out"), sem("tb_in"), sem("w1_in"), sem("sub_in")
        ring_used, ada_used = sem("ring_used"), sem("ada_used")
        g_const, g_rowok, g_chain = sem("g_const"), sem("g_rowok"), sem("g_chain")
        a_c, a_ss, a_std, a_rev, a_cmpb = (sem(n) for n in ("a_c", "a_ss", "a_std", "a_rev", "a_cmpb"))
        a_evac, a_v, a_hk, a_kc, a_hv, a_vc, a_stdc, a_z = (
            sem(n) for n in ("a_evac", "a_v", "a_hk", "a_kc", "a_hv", "a_vc", "a_stdc", "a_z"))
        a_cexp, a_exp, a_pt, a_pct, a_at, a_row, a_h2T, a_q, a_wexp = (
            sem(n) for n in ("a_cexp", "a_exp", "a_pt", "a_pct", "a_at", "a_row", "a_h2T", "a_q", "a_wexp"))
        a_turn, a_gl, a_dg = sem("a_turn"), sem("a_gl"), sem("a_dg")
        p_rev, p_cmpb, p_xT, p_proj, p_v, p_mean, p_var, p_hk, p_kc, p_hv, p_vc, p_co = (
            sem(n) for n in ("p_rev", "p_cmpb", "p_xT", "p_proj", "p_v", "p_mean", "p_var", "p_hk", "p_kc",
                             "p_hv", "p_vc", "p_co"))
        p_cs, p_s, p_t, p_ct, p_o, p_at, p_ao, p_row, p_out, p_h2T, p_q, p_sc = (
            sem(n) for n in ("p_cs", "p_s", "p_t", "p_ct", "p_o", "p_at", "p_ao", "p_row", "p_out", "p_h2T",
                             "p_q", "p_sc"))
        v_chain, v_xs, v_hT, v_y, v_vec, v_pos, v_yc, v_sq, v_yn, v_zb = (
            sem(n) for n in ("v_chain", "v_xs", "v_hT", "v_y", "v_vec", "v_pos", "v_yc", "v_sq", "v_yn", "v_zb"))
        v_cs, v_csub, v_st, v_mx, v_coef, v_o, v_at, v_m, v_row, v_x2, v_h2 = (
            sem(n) for n in ("v_cs", "v_csub", "v_st", "v_mx", "v_coef", "v_o", "v_at", "v_m", "v_row", "v_x2",
                             "v_h2"))
        v_idx, v_wsub, v_cf, v_out = sem("v_idx"), sem("v_wsub"), sem("v_cf"), sem("v_out")
        u_in = [sem(f"u_in{i}") for i in range(CH)]
        v_in = [sem(f"v_in{i}") for i in range(CH)]
        u_free, v_free, g_staged, g_turn = sem("u_free"), sem("v_free"), sem("g_staged"), sem("g_turn")
        o_done = sem("o_done")

        rev_dram = nc.dram_tensor("rev_scratch", (HEADS, P, REV), F32).ap()

        def unit_keys(n):
            tt, h = divmod(n, HEADS)
            return tt, h, h // REP, h % REP, P * (tt + 1)

        NU = TT * HEADS

        block = ctx.enter_context(nc.Block())

        @block.sync
        def _(sp):
            sp.dma_start(x[:, :, :], a["x"].rearrange("(t p) d -> p t d", p=P)).then_inc(s_x, 16)
            sp.dma_start(cact, a["c"].partition_broadcast(P)).then_inc(s_c, 16)
            for s in range(8):
                sp.dma_start(adaw[:, s, :], a["w_ada"][s]).then_inc(ada_in[s], 16)
            sp.dma_start(cols[:, :], a["cols"]).then_inc(s_cols, 16)
            sp.dma_start(table[0:BUCKETS, :], a["rel_table"]).then_inc(s_tbl, 16)
            sp.dma_start(ohr, a["onehot_rev"]).then_inc(s_oh, 16)
            sp.dma_start(ohc, a["onehot_cmp"]).then_inc(s_oh, 16)
            for s in range(8):
                sp.wait_ge(ada_used, s + 1)
                sp.dma_start(adaw[:, s, :], a["w_ada"][8 + s]).then_inc(ada_in[s], 16)
            for s in range(RING):
                sp.dma_start(ring[:, s, :], a["w_stream"][s]).then_inc(ring_in[s], 16)
            sp.dma_start(posk[:, :], a["pos_k"]).then_inc(s_small, 16)
            sp.dma_start(posv[:, :], a["pos_v"]).then_inc(s_small, 16)
            sp.dma_start(w2k[:, :, :], a["w2k"]).then_inc(s_small, 16)
            sp.dma_start(w2v[:, :, :], a["w2v"]).then_inc(s_small, 16)
            with sp.Fori(1, ROUNDS) as r:
                for s in range(RING):
                    sp.wait_ge(ring_used, (r - 1) * RING + s + 1)
                    sp.dma_start(ring[:, s, :], a["w_stream"][r * RING + s]).then_inc(ring_in[s], 16)
            for t in range(TT):
                sp.wait_ge(v_out, t + 1)
                sp.dma_start(out[t * P:(t + 1) * P, :], x[:, t, :]).then_inc(o_done, 16)
            sp.wait_ge(o_done, 16 * TT)

        @block.gpsimd
        def _(g):
            g_ch = Chain(g, g_chain)
            g_ch.link(nc.gpsimd.memset(table[BUCKETS:BUCKETS + 1, :], NEG))
            nc.gpsimd.memset(eps[:, :], EPS).then_inc(g_const, 1)
            nc.gpsimd.memset(ones[:, :], 1.0 / D).then_inc(g_const, 1)
            g_ch.link(nc.gpsimd.memset(ident[:, :], 0.0))
            nc.gpsimd.affine_select(out=ident[:, :], in_=ident[:, :], compare_op=ALU.not_equal, fill=1.0, base=0,
                                    pattern=[[-1, P]], channel_multiplier=1).then_inc(g_const, 1)
            nc.gpsimd.iota(iota16[:, :], pattern=[[1, TOPK]], base=0, channel_multiplier=0,
                           allow_small_or_imprecise_dtypes=True).then_inc(g_const, 1)
            g_ch.link(nc.gpsimd.memset(rowok[:, :], 1.0))
            nc.gpsimd.affine_select(out=rowok[:, :], in_=rowok[:, :], compare_op=ALU.is_ge, fill=0.0,
                                    base=-(CMP_L - 1), pattern=[[0, 1]], channel_multiplier=1).then_inc(g_rowok, 1)
            g.wait_ge(a_rev, 1)
            g.dma_start(rev_dram, revsb[:, 0:REV].unsqueeze(1).broadcast_to((HEADS, P, REV))).then_inc(rev_out, 16)
            g.wait_ge(rev_out, 16)
            g.wait_ge(p_cmpb, 1)
            g.dma_start(tb[:, :, :], bass.AP(rev_dram.tensor, P - 1, [[REV - 1, P], [P * REV, HEADS], [1, SEQ]])
                        ).then_inc(tb_in, 16)
            with g.Fori(2, 6) as i:
                for s in range(8):
                    g.wait_ge(ada_used, (i - 1) * 8 + s + 1)
                    g.sem_inc(g_turn, 1)
                    g.dma_start(adaw[:, s, :], a["w_ada"][i * 8 + s]).then_inc(ada_more[s], 16)
            g.wait_ge(ada_used, 48)
            g.dma_start(w1[0:DQK, :, :], a["w1k"]).then_inc(w1_in, 16)
            g.wait_ge(p_hk, 1)
            g.dma_start(w1[0:DV, :, :], a["w1v"]).then_inc(w1_in, 16)
            g.wait_ge(p_s, NU)
            g.dma_start(subk, a["subkeys"]).then_inc(sub_in, 16)
            g.wait_ge(ring_used, RING * ROUNDS)
            for t in range(TT):
                g.wait_ge(v_idx, t + 1)
                with g.Fori(0, CPT // 2) as i:
                    for b in range(2):
                        c = i * 2 + (CPT * t + b)
                        nc.gpsimd.tensor_copy(stage[:, b, :], idx[:, c, :]).then_inc(g_staged, 1)
                        g.wait_ge(g_staged, c + 1)
                        g.sem_inc(g_turn, 1)
                        for rowbuf, src, free, land in ((urow, a["peer_u"], u_free, u_in),
                                                        (vrow, a["peer_v"], v_free, v_in)):
                            for s in range(CH):
                                g.wait_ge(free, c * CH + (s + 1))
                                g.sem_inc(g_turn, 1)
                                nc.gpsimd.indirect_dma_start(
                                    out=rowbuf[:, s, :], out_offset=None, in_=src,
                                    in_offset=bass.IndirectOffsetOnAxis(ap=stage[:, b, s:s + 1], axis=0),
                                ).then_inc(land[s], 16)

        @block.tensor
        def _(pe):
            mm = nc.tensor.matmul
            v_free_start = CH
            pe.sem_inc(v_free, v_free_start)

            pe.wait_ge(s_tbl, 16)
            pe.wait_ge(g_const, 4)
            pe.wait_ge(s_oh, 32)
            mm(pb[0:HEADS, 0, :], table[:, :], ohr, start=True, stop=True).then_inc(p_rev, 1)
            for t in range(TT):
                for n in range(NCMP):
                    o = (t * NCMP + n) * HEADS
                    last = mm(pb[:, 1, o:o + HEADS], ohc[:, n, t * P:(t + 1) * P], table[:, :], start=True, stop=True)
            last.then_inc(p_cmpb, 1)

            pe.wait_ge(v_xs, TT)
            for j in range(DT):
                for t in range(TT):
                    o = (j % 2) * SEQ + t * P
                    last = nc.tensor.transpose(pb[:, 4 + j // 2, o:o + P], xs[:, t, j * P:(j + 1) * P], ident[:, :])
                if j % 2:
                    last.then_inc(p_xT, 1)

            def column_round(r, first=False):
                for s in range(RING):
                    pe.wait_ge(ring_in[s], (r + 1) * 16)
                    if not first or s >= 4:
                        pe.wait_ge(a_evac, r * RING + (s - 3))
                    for k in range(DT):
                        last = mm(pb[:, s % 4, 0:SEQ], ring[:, s, k * P:(k + 1) * P], hT[:, k, :],
                                  start=(k == 0), stop=(k == DT - 1))
                    last.then_inc(p_proj, 1)
                    pe.wait_ge(p_proj, r * RING + (s + 1))
                    pe.sem_inc(ring_used, 1)

            pe.wait_ge(v_hT, DT)
            pe.wait_ge(a_rev, 1)
            pe.wait_ge(a_cmpb, 1)
            column_round(0, first=True)
            with pe.Fori(1, R_V) as r:
                column_round(r)

            def used(last, extra=None):
                last.then_inc(ring_used, 1)

            pe.wait_ge(a_evac, RING * R_V)
            for k in range(DT):
                pe.wait_ge(ring_in[k], (R_V + 1) * 16)
                for t in range(TT):
                    h = hT[:, k, t * P:(t + 1) * P]
                    mm(pb[:, t, :], h, ring[:, k, 0:512], start=(k == 0), stop=(k == DT - 1))
                    last = mm(pb[:, 2 + t, 0:48], h, ring[:, k, 512:560], start=(k == 0), stop=(k == DT - 1))
                used(last)

            pe.wait_ge(v_y, 2)
            for k in range(DT):
                last = mm(pb[:, 4, 0:SEQ], ones[:, :], y[:, k, :], start=(k == 0), stop=(k == DT - 1))
            last.then_inc(p_mean, 1)

            def hidden(bank, dk, A, B):
                for hh in range(2):
                    for l in range(CMP_L):
                        src, o = (A, l) if l < CMP_ST else (B, l)
                        last = mm(pb[:, bank, hh * 64:hh * 64 + GROUPS * NCMP],
                                  w1[0:dk, l, hh * P:(hh + 1) * P],
                                  src[0:dk, :, o:o + (NCMP - 1) * CMP_ST + 1:CMP_ST],
                                  start=(l == 0), stop=(l == CMP_L - 1))
                return last

            pe.wait_ge(w1_in, 16)
            pe.wait_ge(v_pos, 4)
            hidden(5, DQK, kcA, kcB).then_inc(p_hk, 1)
            pe.wait_ge(v_sq, 1)
            for k in range(DT):
                last = mm(pb[:, 4, SEQ:2 * SEQ], ones[:, :], upad[:, k, 0:SEQ], start=(k == 0), stop=(k == DT - 1))
            last.then_inc(p_var, 1)
            pe.wait_ge(a_hk, 1)
            pe.wait_ge(s_small, 64)
            for k in range(2):
                last = mm(pb[0:DQK, 6, 0:GROUPS * NCMP], w2k[:, k, :], hidk[:, k, 0:GROUPS * NCMP],
                          start=(k == 0), stop=(k == 1))
            last.then_inc(p_kc, 1)
            pe.wait_ge(w1_in, 32)
            hidden(7, DV, vcA, vcB).then_inc(p_hv, 1)
            pe.wait_ge(a_hv, 1)
            for g in range(GROUPS):
                for k in range(2):
                    last = mm(pb[0:NCMP, 5, g * DV:(g + 1) * DV], hidv[:, k, g * NCMP:(g + 1) * NCMP], w2v[:, k, :],
                              start=(k == 0), stop=(k == 1))
            last.then_inc(p_vc, 1)

            pe.wait_ge(a_z, DT)
            pe.wait_ge(a_v, 4)
            for j in range(DT):
                pe.wait_ge(ring_in[j], (R_CO + 1) * 16)
                if j >= 4:
                    pe.wait_ge(v_zb, j - 3)
                for k in range(DT):
                    last = mm(pb[:, j % 4, 0:SEQ], ring[:, j, k * P:(k + 1) * P], y[:, k, :],
                              start=(k == 0), stop=(k == DT - 1))
                used(last)

            pe.wait_ge(a_kc, 1)
            pe.wait_ge(a_vc, 1)
            pe.wait_ge(v_zb, DT)
            pe.wait_ge(a_stdc, 1)

            def cmp_scores(gi):
                tt, g = divmod(gi, GROUPS)
                if gi >= 1:
                    pe.wait_ge(v_cs, gi)
                for hh in range(REP):
                    last = mm(pb[:, 4, hh * NCMP:(hh + 1) * NCMP], qT[0:DQK, g * REP + hh, tt * P:(tt + 1) * P],
                              kcT[:, g * NCMP:(g + 1) * NCMP], start=True, stop=True)
                last.then_inc(p_cs, 1)

            def cmp_transposes(gi):
                pe.wait_ge(a_cexp, gi + 1)
                if gi >= 1:
                    pe.wait_ge(a_pct, gi)
                for hh in range(REP):
                    last = nc.tensor.transpose(pb[0:NCMP, 5, hh * P:(hh + 1) * P], Sc[:, hh, :], ident[:, :])
                last.then_inc(p_ct, 1)

            def scores(n):
                tt, h, g, hh, keys = unit_keys(n)
                if n >= 2:
                    pe.wait_ge(v_st, n - 1)
                mm(pb[:, n % 2, 0:2 * keys], qT[0:DQK, h, tt * P:(tt + 1) * P], kT[0:DQK, g, 1:3, 0:keys],
                   start=True, stop=True).then_inc(p_s, 1)

            def transposes(n):
                tt, h, g, hh, keys = unit_keys(n)
                pe.wait_ge(a_exp, 2 * (n + 1))
                if n >= 2:
                    pe.wait_ge(a_pt, n - 1)
                for b in range(2):
                    for kb in range(tt + 1):
                        o = (b * (tt + 1) + kb) * P
                        last = nc.tensor.transpose(pb[:, 2 + n % 2, o:o + P], S[:, n % 2, b, kb * P:(kb + 1) * P],
                                                   ident[:, :])
                last.then_inc(p_t, 1)

            def values(n):
                tt, h, g, hh, keys = unit_keys(n)
                gi = n // REP
                pe.wait_ge(a_pt, n + 1)
                pe.wait_ge(a_pct, gi + 1)
                if gi >= 1 and hh % 2 == 0:
                    pe.wait_ge(v_o, 2 * (gi - 1) + hh // 2 + 1)
                o = (hh % 2) * 3 * DV
                bank = 6 + hh // 2
                mm(pb[:, bank, o:o + DV], PcT[0:NCMP, hh * P:(hh + 1) * P], vcv[:, g * DV:(g + 1) * DV],
                   start=True, stop=True)
                for b in range(2):
                    for kb in range(tt + 1):
                        last = mm(pb[:, bank, o + (1 + b) * DV:o + (2 + b) * DV],
                                  PT[:, n % 2, (b * (tt + 1) + kb) * P:(b * (tt + 1) + kb + 1) * P],
                                  V[:, kb, (b * GROUPS + g) * DV:(b * GROUPS + g + 1) * DV],
                                  start=(kb == 0), stop=(kb == tt))
                last.then_inc(p_o, 1)

            for n in range(NU + 2):
                if n < NU:
                    if n % REP == 0:
                        cmp_scores(n // REP)
                    scores(n)
                    if n % REP == 1:
                        cmp_transposes(n // REP)
                if 1 <= n <= NU:
                    transposes(n - 1)
                if n >= 2:
                    values(n - 2)

            pe.wait_ge(v_at, 2 * GROUPS * TT)
            pe.wait_ge(a_pt, NU)
            pe.wait_ge(a_pct, GROUPS * TT)
            for t in range(TT):
                for jj in range(2):
                    for j in range(4):
                        last = nc.tensor.transpose(pb[:, 2 + 2 * t + jj, j * P:(j + 1) * P],
                                                   attn[:, t, (4 * jj + j) * P:(4 * jj + j + 1) * P], ident[:, :])
                    last.then_inc(p_at, 1)

            wide_bank = (0, 1, 6, 7)
            pe.wait_ge(a_at, 4)
            pe.wait_ge(v_o, 2 * GROUPS * TT)
            for j in range(DT):
                pe.wait_ge(ring_in[j], (R_AO + 1) * 16)
                if j >= 4:
                    pe.wait_ge(v_m, j - 3)
                for k in range(DT):
                    last = mm(pb[:, wide_bank[j % 4], 0:SEQ], ring[:, j, k * P:(k + 1) * P], attnT[:, k, :],
                              start=(k == 0), stop=(k == DT - 1))
                used(last)

            for v in range(4):
                pe.wait_ge(v_row, v + 1)
                if v >= 2:
                    pe.wait_ge(a_row, v - 1)
                for j in range(DT):
                    last = mm(pb[:, 2 + 2 * (v % 2) + j // 4, (j % 4) * P:(j % 4 + 1) * P], wide[:, j, :], ident[:, :],
                              start=True, stop=True)
                last.then_inc(p_row, 1)

            pe.wait_ge(v_m, DT)
            for k in range(DT):
                pe.wait_ge(ring_in[k], (R_OUT + 1) * 16)
                for t in range(TT):
                    for hf in range(2):
                        last = mm(pb[:, 6 * t + hf, :], y[:, k, t * P:(t + 1) * P], ring[:, k, hf * 512:(hf + 1) * 512],
                                  start=(k == 0), stop=(k == DT - 1))
                used(last)

            pe.wait_ge(v_h2, TT)
            pe.wait_ge(a_row, 4)
            for j in range(DT):
                for t in range(TT):
                    o = (j % 2) * SEQ + t * P
                    last = nc.tensor.transpose(pb[:, 2 + j // 2, o:o + P], h2[:, t, j * P:(j + 1) * P], ident[:, :])
                if j % 2:
                    last.then_inc(p_h2T, 1)
            pe.wait_ge(a_h2T, 4)
            for m in range(2 * PH):
                pe.wait_ge(ring_in[m % RING], (R_WQ + m // RING + 1) * 16)
                if m >= 4:
                    pe.wait_ge(a_q, m - 3)
                for k in range(DT):
                    last = mm(pb[:, wide_bank[m % 4], 0:SEQ], ring[:, m % RING, k * P:(k + 1) * P], hT[:, k, :],
                              start=(k == 0), stop=(k == DT - 1))
                used(last)
            pe.wait_ge(a_q, 2 * PH)
            pe.wait_ge(sub_in, 16)
            for t in range(TT):
                for m in range(2 * PH):
                    bank = (2, 3, 4, 5)[m // 4] if t == 0 else wide_bank[m // 4]
                    last = mm(pb[:, bank, (m % 4) * NK:(m % 4 + 1) * NK], qT[:, m, t * P:(t + 1) * P], subk[:, m, :],
                              start=True, stop=True)
                last.then_inc(p_sc, 1)

            def expert_chunk(t, b, c, first=False):
                for s in range(CH):
                    pe.wait_ge(v_in[s], (c + 1) * 16)
                    pe.wait_ge(a_dg, c * CH + (s + 1))
                    for hf in range(2):
                        last = mm(pb[:, 2 + 2 * t + hf, :], diag[:, b, s, :], vrow[:, s, hf * 512:(hf + 1) * 512],
                                  start=(first and s == 0), stop=False, skip_group_check=True)
                    last.then_inc(v_free, 1)

            for t in range(TT):
                pe.wait_ge(v_idx, t + 1)
                for b in range(2):
                    expert_chunk(t, b, CPT * t + b, first=(b == 0))
                with pe.Fori(1, CPT // 2) as i:
                    for b in range(2):
                        expert_chunk(t, b, i * 2 + (CPT * t + b))

        @block.scalar
        def _(act):
            fn = nc.scalar.activation

            def turn():
                act.sem_inc(a_turn, 1)

            act.wait_ge(s_c, 16)
            fn(cact, cact, ACT.Silu).then_inc(a_c, 1)
            act.wait_ge(s_x, 16)
            for t in range(TT):
                fn(xs[:, t, :], x[:, t, :], ACT.Square, accum_out=ss[:, t:t + 1]).then_inc(a_ss, 1)
            act.wait_ge(a_ss, TT)
            act.wait_ge(g_const, 4)
            fn(std[:, 0:TT], ss[:, 0:TT], ACT.Sqrt, scale=1.0 / D, bias=eps[:, :]).then_inc(a_std, 1)
            act.wait_ge(p_rev, 1)
            fn(revsb, pb[0:HEADS, 0, :], ACT.Copy).then_inc(a_rev, 1)
            act.wait_ge(p_cmpb, 1)
            for t in range(TT):
                o = t * NCMP * HEADS
                last = fn(tbc[:, t, :, :],
                          pb[:, 1, o:o + NCMP * HEADS].rearrange("p (n h) -> p h n", n=NCMP), ACT.Copy)
            last.then_inc(a_cmpb, 1)

            def evac(r, s, dst, func, rows_=P):
                act.wait_ge(p_proj, r * RING + (s + 1))
                turn()
                fn(dst, pb[0:rows_, s % 4, 0:SEQ], func).then_inc(a_evac, 1)

            with act.Fori(0, 2) as r:
                for s in range(RING):
                    if s % 2 == 0:
                        evac(r, s, upad[:, r * 4 + s // 2, PADT:PADT + SEQ], ACT.Copy)
                    else:
                        evac(r, s, y[:, r * 4 + s // 2, :], ACT.Sigmoid)
            with act.Fori(0, 2) as r:
                for s in range(RING):
                    evac(r + R_MERGE, s, sig[:, r * RING + s, :], ACT.Sigmoid)
            with act.Fori(0, GROUPS) as g:
                for s in range(REP):
                    evac(g + R_GROUP, s, qT[0:DQK, g * REP + s, :], ACT.Copy, DQK)
                for s in range(REP, 7):
                    evac(g + R_GROUP, s, kT[0:DQK, g, s - REP, :], ACT.Copy, DQK)
                evac(g + R_GROUP, 7, vcT[0:DV, g, :], ACT.Copy, DV)
            act.wait_ge(ring_used, RING * (R_V + 1))
            for t in range(TT):
                fn(V[:, t, :], pb[:, t, :], ACT.Copy).then_inc(a_v, 1)
            for t in range(TT):
                fn(gates[:, t, :, :], pb[:, 2 + t, 0:48], ACT.Sigmoid).then_inc(a_v, 1)
            act.wait_ge(p_hk, 1)
            fn(hidk[:, :, 0:GROUPS * NCMP], pb[:, 5, 0:P].rearrange("p (a b) -> p a b", a=2)[:, :, 0:GROUPS * NCMP],
               ACT.Gelu_apprx_tanh).then_inc(a_hk, 1)
            act.wait_ge(p_kc, 1)
            fn(kcT[:, :], pb[0:DQK, 6, 0:GROUPS * NCMP], ACT.Copy).then_inc(a_kc, 1)
            act.wait_ge(p_var, 1)
            fn(stdc[:, :], pb[:, 4, SEQ:2 * SEQ], ACT.Sqrt, bias=eps[:, :]).then_inc(a_stdc, 1)
            act.wait_ge(p_hv, 1)
            fn(hidv[:, :, 0:GROUPS * NCMP], pb[:, 7, 0:P].rearrange("p (a b) -> p a b", a=2)[:, :, 0:GROUPS * NCMP],
               ACT.Gelu_apprx_tanh).then_inc(a_hv, 1)
            act.wait_ge(p_vc, 1)
            fn(vcv[:, :], pb[0:NCMP, 5, 0:GROUPS * DV], ACT.Copy).then_inc(a_vc, 1)
            act.wait_ge(v_yn, 1)
            for j in range(DT):
                fn(y[:, j, :], y[:, j, :], ACT.Silu, scale=cols[:, C_LG + j:C_LG + j + 1],
                   bias=cols[:, C_LB + j:C_LB + j + 1]).then_inc(a_z, 1)

            def exps(n):
                tt, h, g, hh, keys = unit_keys(n)
                gi = n // REP
                act.wait_ge(v_mx, n + 1)
                if gi >= 2 and hh == 0:
                    act.wait_ge(v_coef, gi - 1)
                for b in range(2):
                    fn(S[:, n % 2, b, 0:keys], S[:, n % 2, b, 0:keys], ACT.Exp, bias=nm[:, n % 2, b:b + 1],
                       accum_out=Z[:, gi % 2, hh, 1 + b:2 + b]).then_inc(a_exp, 1)

            for n in range(NU + 1):
                gi = n // REP
                if n < NU:
                    if n % REP == 0:
                        act.wait_ge(v_csub, gi + 1)
                        fn(Sc[:, :, :], Sc[:, :, :], ACT.Exp).then_inc(a_cexp, 1)
                    exps(n)
                if n >= 1:
                    u = n - 1
                    tt = u // HEADS
                    act.wait_ge(p_t, u + 1)
                    if u >= 2:
                        act.wait_ge(p_o, u - 1)
                    fn(PT[:, u % 2, 0:2 * P * (tt + 1)], pb[:, 2 + u % 2, 0:2 * P * (tt + 1)],
                       ACT.Copy).then_inc(a_pt, 1)
                if n < NU and n % REP == 1:
                    act.wait_ge(p_ct, gi + 1)
                    if gi >= 1:
                        act.wait_ge(p_o, gi * REP)
                    fn(PcT[0:NCMP, :], pb[0:NCMP, 5, :], ACT.Copy).then_inc(a_pct, 1)
            for t in range(TT):
                for jj in range(2):
                    act.wait_ge(p_at, 2 * t + jj + 1)
                    fn(attnT[:, 4 * jj:4 * jj + 4, t * P:(t + 1) * P],
                       pb[:, 2 + 2 * t + jj, :].rearrange("p (j t) -> p j t", j=4), ACT.Copy).then_inc(a_at, 1)
            for v in range(4):
                act.wait_ge(p_row, v + 1)
                fn(rows[:, v, :], pb[:, 2 + 2 * (v % 2):4 + 2 * (v % 2), :].rearrange("p a b -> p (a b)"),
                   ACT.Copy).then_inc(a_row, 1)
            act.wait_ge(ring_used, RING * (R_OUT + 1))
            act.wait_ge(p_row, 4)
            for t in range(TT):
                fn(junk, pb[:, 6 * t:6 * t + 2, :].rearrange("p a b -> p (a b)"), ACT.Square,
                   accum_out=ss[:, 2 + t:3 + t]).then_inc(a_ss, 1)
                act.wait_ge(a_ss, TT + t + 1)
            fn(std[:, 2:4], ss[:, 2:4], ACT.Sqrt, scale=1.0 / D, bias=eps[:, :]).then_inc(a_std, 1)
            for t in range(TT):
                act.wait_ge(v_x2, t + 1)
                fn(junk, x[:, t, :], ACT.Square, accum_out=ss[:, 4 + t:5 + t]).then_inc(a_ss, 1)
                act.wait_ge(a_ss, 2 * TT + t + 1)
            fn(std[:, 4:6], ss[:, 4:6], ACT.Sqrt, scale=1.0 / D, bias=eps[:, :]).then_inc(a_std, 1)
            for b in range(4):
                act.wait_ge(p_h2T, b + 1)
                fn(hT[:, 2 * b:2 * b + 2, :], pb[:, 2 + b, :].rearrange("p (a t) -> p a t", a=2),
                   ACT.Copy).then_inc(a_h2T, 1)
            wide_bank = (0, 1, 6, 7)
            for m in range(2 * PH):
                act.wait_ge(ring_used, RING * R_WQ + m + 1)
                fn(qT[:, m, :], pb[:, wide_bank[m % 4], 0:SEQ], ACT.Copy).then_inc(a_q, 1)
            for t in range(TT):
                act.wait_ge(v_wsub, t + 1)
                fn(wgt[:, CPT * t:CPT * (t + 1), :], wgt[:, CPT * t:CPT * (t + 1), :], ACT.Exp).then_inc(a_wexp, 1)

            for t in range(TT):
                with act.Fori(0, CPT // 2) as i:
                    for b in range(2):
                        c = i * 2 + (CPT * t + b)
                        act.wait_ge(u_free, c * CH + 2 * CH)
                        fn(gl[:, b, :], dot[:, b, :], ACT.Gelu_apprx_tanh).then_inc(a_gl, 1)
                        act.wait_ge(v_cf, c + 1)
                        for s in range(CH):
                            fn(diag[:, b, s, :], ident[:, :], ACT.Copy, scale=cf[:, b, s:s + 1]).then_inc(a_dg, 1)
            for t in range(TT):
                act.wait_ge(v_free, CH + NE * (t + 1))
                fn(junk, pb[:, 2 + 2 * t:4 + 2 * t, :].rearrange("p a b -> p (a b)"), ACT.Square,
                   accum_out=ss[:, 6 + t:7 + t]).then_inc(a_ss, 1)
                act.wait_ge(a_ss, 3 * TT + t + 1)
                fn(std[:, 6 + t:7 + t], ss[:, 6 + t:7 + t], ACT.Sqrt, scale=1.0 / D, bias=eps[:, :]).then_inc(a_std, 1)

        @block.vector
        def _(dve):
            V_ = nc.vector
            ch = Chain(dve, v_chain)
            dve.sem_inc(u_free, CH)

            ch.link(V_.memset(upad[:, :, 0:PADT], 0.0))

            def ada_part(i, landed, n):
                for s in range(8):
                    dve.wait_ge(landed[s], n * 16 + 16)
                    V_.tensor_tensor_reduce(out=adaw[:, s, :], in0=adaw[:, s, :], in1=cact, scale=1.0, scalar=0.0,
                                            op0=ALU.mult, op1=ALU.add, accum_out=modst[:, s:s + 1]
                                            ).then_inc(ada_used, 1)
                dve.wait_ge(ada_used, i * 8 + 8)
                ch.link(V_.tensor_tensor(mod[:, bass.ds(i * 8, 8)], modst[:, :], cols[:, bass.ds(i * 8 + C_BADA, 8)], ALU.add))

            dve.wait_ge(a_c, 1)
            dve.wait_ge(s_cols, 16)
            ada_part(0, ada_in, 0)
            dve.wait_ge(a_std, 1)
            ch.link(V_.reciprocal(rstd[:, 0:TT], std[:, 0:TT]))
            for t in range(TT):
                V_.tensor_scalar(xs[:, t, :], x[:, t, :], rstd[:, t:t + 1], None, ALU.mult).then_inc(v_xs, 1)
            ada_part(1, ada_in, 1)
            ch.link(V_.scalar_tensor_tensor(out=A1[:, :], in0=mod[:, 8:16], scalar=1.0, in1=cols[:, C_GPM:C_GPM + DT],
                                            op0=ALU.add, op1=ALU.mult))
            for j in range(DT):
                dve.wait_ge(p_xT, j // 2 + 1)
                o = (j % 2) * SEQ
                V_.tensor_scalar(hT[:, j, :], pb[:, 4 + j // 2, o:o + SEQ], A1[:, j:j + 1], mod[:, j:j + 1],
                                 ALU.mult, ALU.add).then_inc(v_hT, 1)

            with dve.Fori(0, 2) as r:
                ch.enter(r, 4 * TAPS + 4 - 4)
                for jj in range(4):
                    dve.wait_ge(a_evac, r * RING + (2 * jj + 2))
                    u = upad[:, r * 4 + jj, PADT:PADT + SEQ]
                    last = V_.tensor_tensor(u, u, y[:, r * 4 + jj, :], ALU.mult)
                    n = ch.add(last)
                dve.wait_ge(v_chain, n)
                for k in range(TAPS):
                    for jj in range(4):
                        j = r * 4 + jj
                        w = cols[:, bass.ds(j * TAPS + (C_CW + k), 1)]
                        if k == 0:
                            ins = V_.tensor_scalar(y[:, j, :], upad[:, j, 0:SEQ], w, cols[:, bass.ds(j + C_CB, 1)],
                                                   ALU.mult, ALU.add)
                        else:
                            dve.wait_ge(v_chain, n - 3 + (jj if k == TAPS - 1 else 0))
                            ins = V_.scalar_tensor_tensor(out=y[:, j, :], in0=upad[:, j, k:k + SEQ], scalar=w,
                                                          in1=y[:, j, :], op0=ALU.mult, op1=ALU.add)
                        if k < TAPS - 1:
                            n = ch.add(ins)
                        elif jj == 3:
                            ins.then_inc(v_y, 1)
                dve.wait_ge(v_y, r + 1)
            ch.leave(2)

            with dve.Fori(2, 6) as i:
                ch.enter(i - 2, 1)
                ada_part(i, ada_more, i - 2)
            ch.leave(4)
            ch.add(V_.tensor_tensor(vec4[:, 0, :], mod[:, 16:24], cols[:, C_GOM:C_GOM + DT], ALU.mult))
            ch.add(V_.scalar_tensor_tensor(out=vec4[:, 1, :], in0=mod[:, 32:40], scalar=1.0,
                                           in1=cols[:, C_GPF:C_GPF + DT], op0=ALU.add, op1=ALU.mult))
            ch.add(V_.tensor_copy(vec4[:, 2, :], mod[:, 24:32]))
            ch.link(V_.tensor_tensor(vec4[:, 3, :], mod[:, 40:48], cols[:, C_GOF:C_GOF + DT], ALU.mult))

            dve.wait_ge(a_evac, RING * R_V)
            dve.wait_ge(s_small, 64)
            dve.wait_ge(v_hT, DT)
            for dst, src, pos, dk, o in ((kcA, kT[0:DQK, :, 0, :], posk, DQK, 0), (kcB, kT[0:DQK, :, 0, :], posk, DQK, CMP_ST),
                                         (vcA, vcT[0:DV, :, :], posv, DV, 0), (vcB, vcT[0:DV, :, :], posv, DV, CMP_ST)):
                V_.tensor_tensor(
                    dst[0:dk].rearrange("p g (c l) -> p g c l", l=CMP_ST),
                    src.rearrange("p g (c l) -> p g c l", l=CMP_ST),
                    pos[:, o:o + CMP_ST].unsqueeze(1).unsqueeze(1).broadcast_to((dk, GROUPS, SEQ // CMP_ST, CMP_ST)),
                    ALU.add).then_inc(v_pos, 1)

            dve.wait_ge(p_mean, 1)
            ch.link(V_.tensor_tensor(y[:, :, :], y[:, :, :],
                                     pb[:, 4, 0:SEQ].unsqueeze(1).broadcast_to((P, DT, SEQ)), ALU.subtract))
            V_.tensor_tensor(upad[:, :, 0:SEQ], y[:, :, :], y[:, :, :], ALU.mult).then_inc(v_sq, 1)
            dve.wait_ge(a_stdc, 1)
            ch.link(V_.reciprocal(stdc[:, :], stdc[:, :]))
            dve.wait_ge(v_sq, 1)
            V_.tensor_tensor(y[:, :, :], y[:, :, :], stdc[:, :].unsqueeze(1).broadcast_to((P, DT, SEQ)),
                             ALU.mult).then_inc(v_yn, 1)
            dve.wait_ge(a_v, 4)
            dve.wait_ge(g_rowok, 1)
            ch.add(V_.tensor_scalar(gates[:, 0, 0, :], gates[:, 0, 0, :], rowok[:, :], None, ALU.mult))
            for j in range(DT):
                dve.wait_ge(ring_used, RING * R_CO + j + 1)
                V_.tensor_tensor(upad[:, j, 0:SEQ], pb[:, j % 4, 0:SEQ], sig[:, DT + j, :], ALU.mult).then_inc(v_zb, 1)

            dve.wait_ge(tb_in, 16)
            dve.wait_ge(a_cmpb, 1)
            dve.wait_ge(p_vc, 1)

            def cmp_logits(gi):
                tt, g = divmod(gi, GROUPS)
                dve.wait_ge(p_cs, gi + 1)
                if gi >= 1:
                    dve.wait_ge(p_ct, gi)
                V_.scalar_tensor_tensor(out=Sc[:, :, :],
                                        in0=pb[:, 4, 0:REP * NCMP].rearrange("p (h n) -> p h n", h=REP),
                                        scalar=SCALE, in1=tbc[:, tt, g * REP:(g + 1) * REP, :],
                                        op0=ALU.mult, op1=ALU.add).then_inc(v_cs, 1)
                dve.wait_ge(v_cs, gi + 1)
                ch.link(V_.tensor_reduce(nmc[:, :], Sc[:, :, :], AX, ALU.max))
                V_.tensor_tensor(Sc[:, :, :], Sc[:, :, :], nmc[:, :].unsqueeze(2).broadcast_to((P, REP, NCMP)),
                                 ALU.subtract).then_inc(v_csub, 1)

            def logits(n):
                tt, h, g, hh, keys = unit_keys(n)
                dve.wait_ge(p_s, n + 1)
                if n >= 2:
                    dve.wait_ge(p_t, n - 1)
                V_.scalar_tensor_tensor(out=S[:, n % 2, :, 0:keys],
                                        in0=pb[:, n % 2, 0:2 * keys].rearrange("p (b t) -> p b t", b=2),
                                        scalar=SCALE,
                                        in1=tb[:, h, SEQ - keys:SEQ].unsqueeze(1).broadcast_to((P, 2, keys)),
                                        op0=ALU.mult, op1=ALU.add).then_inc(v_st, 1)
                dve.wait_ge(v_st, n + 1)
                V_.tensor_reduce(nm[:, n % 2, :], S[:, n % 2, :, 0:keys], AX, ALU.max, negate=True).then_inc(v_mx, 1)

            def combine(gi):
                tt, g = divmod(gi, GROUPS)
                dve.wait_ge(a_exp, 2 * REP * (gi + 1))
                ch.link(V_.reciprocal(rz[:, :, :], Z[:, gi % 2, :, :]))
                V_.tensor_tensor(coef[:, :, :], rz[:, :, :],
                                 gates[:, tt, :, g * REP:(g + 1) * REP].rearrange("p b h -> p h b"),
                                 ALU.mult).then_inc(v_coef, 1)
                dve.wait_ge(v_coef, gi + 1)
                for pr in range(2):
                    dve.wait_ge(p_o, REP * gi + 2 * (pr + 1))
                    V_.tensor_tensor(otmp[:, pr, :].rearrange("p (c d) -> p c d", d=DV),
                                     pb[:, 6 + pr, 0:6 * DV].rearrange("p (c d) -> p c d", d=DV),
                                     coef[:, 2 * pr:2 * pr + 2, :].rearrange("p h b -> p (h b)").unsqueeze(2)
                                     .broadcast_to((P, 6, DV)), ALU.mult).then_inc(v_o, 1)
                for pr in range(2):
                    dve.wait_ge(v_o, 2 * gi + pr + 1)
                    o = (g * REP + 2 * pr) * DV
                    V_.tensor_reduce(attn[:, tt, o:o + 2 * DV].rearrange("p (h d) -> p h d", d=DV),
                                     otmp[:, pr, :].rearrange("p (h b d) -> p h d b", h=2, b=3),
                                     AX, ALU.add).then_inc(v_at, 1)
                dve.wait_ge(v_at, 2 * gi + 2)

            for n in range(NU + 2):
                gi = n // REP
                if n < NU:
                    if n % REP == 0:
                        cmp_logits(gi)
                    logits(n)
                    if n % REP == 1:
                        dve.wait_ge(a_cexp, gi + 1)
                        ch.add(V_.tensor_reduce(Z[:, gi % 2, :, 0], Sc[:, :, :], AX, ALU.add))
                if n % REP == 1 and n > REP:
                    combine(gi - 1)

            wide_bank = (0, 1, 6, 7)

            def row(v):
                if v:
                    dve.wait_ge(p_row, v)
                else:
                    dve.wait_ge(p_t, NU)
                V_.tensor_copy(wide, vec4[:, v, :].unsqueeze(2).broadcast_to((P, DT, P))).then_inc(v_row, 1)

            row(0)
            dve.wait_ge(p_o, NU)
            for j in range(DT):
                dve.wait_ge(ring_used, RING * R_AO + j + 1)
                ch.link(V_.tensor_tensor(tmp[:, 0:SEQ], pb[:, wide_bank[j % 4], 0:SEQ], sig[:, j, :], ALU.mult))
                V_.tensor_tensor(y[:, j, :], tmp[:, 0:SEQ], upad[:, j, 0:SEQ], ALU.add).then_inc(v_m, 1)
                dve.wait_ge(v_m, j + 1)
            for v in range(1, 4):
                row(v)

            dve.wait_ge(a_row, 4)
            dve.wait_ge(a_std, 2)
            ch.link(V_.reciprocal(rstd[:, 2:4], std[:, 2:4]))
            for t in range(TT):
                ch.link(V_.scalar_tensor_tensor(out=tmp, in0=pb[:, 6 * t:6 * t + 2, :].rearrange("p a b -> p (a b)"),
                                                scalar=rstd[:, 2 + t:3 + t], in1=rows[:, 0, :],
                                                op0=ALU.mult, op1=ALU.mult))
                V_.tensor_tensor(x[:, t, :], x[:, t, :], tmp, ALU.add).then_inc(v_x2, 1)
                dve.wait_ge(v_x2, t + 1)
            dve.wait_ge(a_std, 3)
            ch.link(V_.reciprocal(rstd[:, 4:6], std[:, 4:6]))
            for t in range(TT):
                ch.link(V_.scalar_tensor_tensor(out=h2[:, t, :], in0=x[:, t, :], scalar=rstd[:, 4 + t:5 + t],
                                                in1=rows[:, 1, :], op0=ALU.mult, op1=ALU.mult))
                V_.tensor_tensor(h2[:, t, :], h2[:, t, :], rows[:, 2, :], ALU.add).then_inc(v_h2, 1)
            dve.wait_ge(v_h2, TT)

            def top16(n_rows, src, work, vals, idxs):
                for m in range(n_rows):
                    n = ch.add(V_.max(vals(m)[:, 0:8], src(m)))
                dve.wait_ge(v_chain, n)
                for m in range(n_rows):
                    ch.add(V_.max_index(idxs(m)[:, 0:8], vals(m)[:, 0:8], src(m)))
                    n = ch.add(V_.match_replace(work(m), vals(m)[:, 0:8], src(m), -3.0e38))
                dve.wait_ge(v_chain, n)
                for m in range(n_rows):
                    n = ch.add(V_.max(vals(m)[:, 8:16], work(m)))
                dve.wait_ge(v_chain, n)
                for m in range(n_rows):
                    n = ch.add(V_.max_index(idxs(m)[:, 8:16], vals(m)[:, 8:16], work(m)))
                dve.wait_ge(v_chain, n)

            def retrieve(t):
                dve.wait_ge(p_sc, t + 1)
                banks = (2, 3, 4, 5) if t == 0 else wide_bank
                top16(2 * PH, lambda m: pb[:, banks[m // 4], (m % 4) * NK:(m % 4 + 1) * NK], lambda m: swork[:, m, :],
                      lambda m: v16[:, m, :], lambda m: i16[:, m, :])
                ch.add(V_.tensor_copy(i16f[:, :, :], i16[:, :, :]))
                pair = v16[:, :, :].rearrange("p (h c) k -> p h c k", c=2)
                for h in range(PH):
                    n = ch.add(V_.tensor_tensor(cand[:, h, :].rearrange("p (a b) -> p a b", a=TOPK),
                                                pair[:, h, 0, :].unsqueeze(2).broadcast_to((P, TOPK, TOPK)),
                                                pair[:, h, 1, :].unsqueeze(1).broadcast_to((P, TOPK, TOPK)), ALU.add))
                dve.wait_ge(v_chain, n)
                top16(PH, lambda h: cand[:, h, :], lambda h: cwork[:, h, :], lambda h: t16[:, h, :],
                      lambda h: p16[:, h * TOPK:(h + 1) * TOPK])
                for half, dst in ((0, e1), (1, e2)):
                    op, by = ((ALU.logical_shift_right, 4), (ALU.bitwise_and, TOPK - 1))[half]
                    ch.link(V_.tensor_single_scalar(pa[:, :], p16[:, :], by, op))
                    ch.link(V_.tensor_copy(paf[:, :], pa[:, :]))
                    ch.link(V_.tensor_tensor(oneh, iota16[:, :].unsqueeze(1).broadcast_to((P, NE, TOPK)),
                                             paf[:, :].unsqueeze(2).broadcast_to((P, NE, TOPK)), ALU.is_equal))
                    sub = i16f[:, :, :].rearrange("p (h c) k -> p h c k", c=2)
                    for h in range(PH):
                        o4 = oneh[:, h * TOPK:(h + 1) * TOPK, :]
                        n = ch.add(V_.tensor_tensor(o4, o4, sub[:, h, half, :].unsqueeze(1).broadcast_to((P, TOPK, TOPK)),
                                                    ALU.mult))
                    dve.wait_ge(v_chain, n)
                    ch.link(V_.tensor_reduce(dst[:, :], oneh, AX, ALU.add))
                V_.scalar_tensor_tensor(out=idx[:, CPT * t:CPT * (t + 1), :].rearrange("p a b -> p (a b)"),
                                        in0=e1[:, :], scalar=float(NK), in1=e2[:, :],
                                        op0=ALU.mult, op1=ALU.add).then_inc(v_idx, 1)
                dve.wait_ge(v_idx, t + 1)
                w = wgt[:, CPT * t:CPT * (t + 1), :].rearrange("p a b -> p (a b)").rearrange("p (h k) -> p h k", h=PH)
                V_.tensor_tensor(w, t16[:, :, :], t16[:, :, 0:1].broadcast_to((P, PH, TOPK)),
                                 ALU.subtract).then_inc(v_wsub, 1)
                dve.wait_ge(a_wexp, t + 1)
                ch.link(V_.tensor_reduce(wsum[:, :], w, AX, ALU.add))
                ch.link(V_.reciprocal(wsum[:, :], wsum[:, :]))
                ch.link(V_.tensor_tensor(w, w, wsum[:, :].unsqueeze(2).broadcast_to((P, PH, TOPK)), ALU.mult))

            dve.wait_ge(g_const, 4)
            for t in range(TT):
                retrieve(t)

            for t in range(TT):
                with dve.Fori(0, CPT // 2) as i:
                    for b in range(2):
                        c = i * 2 + (CPT * t + b)
                        for s in range(CH):
                            dve.wait_ge(u_in[s], c * 16 + 16)
                            V_.tensor_tensor_reduce(out=urow[:, s, :], in0=urow[:, s, :], in1=h2[:, t, :], scale=1.0,
                                                    scalar=0.0, op0=ALU.mult, op1=ALU.add,
                                                    accum_out=dot[:, b, s:s + 1]).then_inc(u_free, 1)
                        dve.wait_ge(a_gl, c + 1)
                        V_.tensor_tensor(cf[:, b, :], gl[:, b, :], wgt[:, c, :], ALU.mult).then_inc(v_cf, 1)

            for t in range(TT):
                dve.wait_ge(a_std, 4 + t)
                ch.link(V_.reciprocal(rstd[:, 6 + t:7 + t], std[:, 6 + t:7 + t]))
                ch.link(V_.scalar_tensor_tensor(out=tmp, in0=pb[:, 2 + 2 * t:4 + 2 * t, :].rearrange("p a b -> p (a b)"),
                                                scalar=rstd[:, 6 + t:7 + t], in1=rows[:, 3, :],
                                                op0=ALU.mult, op1=ALU.mult))
                V_.tensor_tensor(x[:, t, :], x[:, t, :], tmp, ALU.add).then_inc(v_out, 1)
                dve.wait_ge(v_out, t + 1)


def bucket(dist):
    exact = BUCKETS // 2
    nf = np.maximum(dist, 1).astype(np.float32)
    big = exact + (np.log(nf / np.float32(exact)) / np.float32(np.log(MAXDIST / exact)) * np.float32(BUCKETS - exact)).astype(np.int32)
    b = np.where(dist < exact, dist, np.minimum(big, BUCKETS - 1))
    return np.where(dist < 0, BUCKETS, b)


def onehot(dist):
    return (bucket(dist)[None] == np.arange(BUCKETS + 1).reshape((-1,) + (1,) * dist.ndim)).astype(np.float32)


def column_tiles(w, width):
    n = w.shape[1] // width
    t = np.zeros((n, P, DT, P), w.dtype)
    t[:, :, :, 0:width] = w.reshape(DT, P, n, width).transpose(2, 1, 0, 3)
    return t.reshape(n, P, D)


def kernel(**inputs):
    import concourse.bacc as _bacc
    from concourse.bass_utils import run_bass_kernel_spmd as _run

    f = {n: np.ascontiguousarray(v) for n, v in inputs.items()}
    w_in = f["w_in"][0]
    sizes = [HEADS * DQK] + [GROUPS * DQK] * 3 + [GROUPS * DV] * 3 + [3 * HEADS, 2 * D, 2 * D]
    at = np.cumsum([0] + sizes)
    q, kc, ks, kw, vc, vs, vw, gn, glu, gm = (w_in[:, at[i]:at[i + 1]] for i in range(10))
    glu_t = column_tiles(glu, P)
    q_t, kc_t, ks_t, kw_t, vc_t = column_tiles(q, DQK), column_tiles(kc, DQK), column_tiles(ks, DQK), column_tiles(kw, DQK), column_tiles(vc, DV)
    vtile = np.zeros((DT, P, D), w_in.dtype)
    vtile[:, :, 0:256] = vs.reshape(DT, P, 256)
    vtile[:, :, 256:512] = vw.reshape(DT, P, 256)
    vtile[:, :, 512:560] = gn.reshape(DT, P, 48)
    stream = [glu_t.reshape(2, DT, P, D).transpose(1, 0, 2, 3).reshape(2 * DT, P, D), column_tiles(gm, P)]
    for g in range(GROUPS):
        stream += [q_t[g * REP:(g + 1) * REP], kc_t[g:g + 1], ks_t[g:g + 1], kw_t[g:g + 1], vc_t[g:g + 1]]
    stream += [vtile, column_tiles(f["w_conv_out"][0], P), column_tiles(f["w_attn_out"][0], P),
               f["w_out"][0].reshape(DT, P, D), column_tiles(f["peer_wq"][0], P)]

    def col(v):
        return v.reshape(-1, P).T

    cols = np.concatenate([col(f[n][0]) for n in ("b_ada", "g_pre_mix", "g_post_mix", "g_pre_ffn", "g_post_ffn",
                                                  "conv_b", "conv_ln_g", "conv_ln_b")]
                          + [f["conv_w"][0, :, 0, :].reshape(TAPS, DT, P).transpose(2, 1, 0).reshape(P, -1)], axis=1)
    j = np.arange(512)
    n = np.arange(NCMP)
    t = np.arange(SEQ)
    arrays = {
        "x": f["x"][0], "c": f["c"][0],
        "w_ada": f["w_ada"][0].T.reshape(48, P, D),
        "w_stream": np.concatenate(stream, axis=0),
        "cols": cols,
        "rel_table": f["rel_table"],
        "onehot_rev": onehot(SEQ - 1 - j),
        "onehot_cmp": onehot(t[None, :] - (n[:, None] * CMP_ST + CMP_L - 1)),
        "w1k": f["cmp_w1k"][0].reshape(CMP_L, DQK, HID).transpose(1, 0, 2),
        "w1v": f["cmp_w1v"][0].reshape(CMP_L, DV, HID).transpose(1, 0, 2),
        "w2k": f["cmp_w2k"][0].reshape(2, P, DQK).transpose(1, 0, 2),
        "w2v": f["cmp_w2v"][0].reshape(2, P, DV).transpose(1, 0, 2),
        "pos_k": f["cmp_pos_k"][0].T, "pos_v": f["cmp_pos_v"][0].T,
        "subkeys": f["peer_subkeys"][0].reshape(2 * PH, NK, P).transpose(2, 0, 1),
        "peer_u": f["peer_u"][0], "peer_v": f["peer_v"][0],
    }
    nc = _bacc.Bacc("TRN2", target_bir_lowering=False, num_devices=1)
    feed, aps = {}, {}
    for name, v in arrays.items():
        v = np.ascontiguousarray(v)
        feed[f"in_{name}"] = v
        aps[name] = nc.dram_tensor(f"in_{name}", v.shape, mybir.dt.from_np(v.dtype), kind="ExternalInput").ap()
    o = nc.dram_tensor("out_y", (SEQ, D), F32, kind="ExternalOutput").ap()
    build(nc, aps, o)
    r = _run(nc, [feed], core_ids=[0])
    return r.results[0]["out_y"].reshape(1, SEQ, D)
```

```python
from contextlib import ExitStack

import numpy as np

import concourse.bass as bass
from concourse import mybir

F32 = mybir.dt.float32
I32 = mybir.dt.int32
U32 = mybir.dt.uint32
ALU = mybir.AluOpType
ACT = mybir.ActivationFunctionType
AX = mybir.AxisListType.X

P = 128
D = 1024
DT = D // P
SEQ = 256
TT = SEQ // P
HEADS = 16
GROUPS = 4
REP = HEADS // GROUPS
DQK = 96
DV = 64
CMP_L = 32
CMP_ST = 16
NCMP = SEQ // CMP_ST - 1
HID = 256
SCALE = DQK ** -0.5
BUCKETS = 32
MAXDIST = 128
TAPS = 31
PADT = TAPS - 1
PH = 8
NK = 128
TOPK = 16
NE = PH * TOPK
REV = 2 * SEQ - 1
EPS = 1e-6
NEG = -1e30

RING = 4
CH = 8
CPT = NE // CH
SEG = 4
UNITS = TT * CPT // SEG
T_GLU, T_MERGE, T_GROUP, T_V, T_CO, T_AO, T_OUT, T_WQ, TILES = 0, 16, 32, 64, 72, 80, 88, 96, 112

C_BADA, C_GPM, C_GOM, C_GPF, C_GOF, C_CB, C_LG, C_LB, C_CW = 0, 48, 56, 64, 72, 80, 88, 96, 104
NCOLS = C_CW + TAPS * DT


class Chain:

    def __init__(self, eng, sem):
        self.eng, self.sem, self.n, self.k = eng, sem, 0, 0

    def add(self, ins):
        ins.then_inc(self.sem, 1)
        self.k += 1
        return self.n + self.k

    def link(self, ins):
        self.eng.wait_ge(self.sem, self.add(ins))

    def enter(self, i, per):
        self.base, self.per = self.n + self.k, per
        self.n, self.k = self.base + i * per, 0

    def leave(self, times):
        assert self.k == self.per, self.k
        self.n, self.k = self.base + self.per * times, 0


def build(nc, a, out):
    ctx = ExitStack()
    with ctx:
        def sb(name, shape, dt=F32):
            return ctx.enter_context(nc.sbuf_tensor(name, shape, dt))

        def sem(name):
            return ctx.enter_context(nc.semaphore(name))

        arena = sb("arena", [P, 16, D])
        ring = arena[:, 0:RING, :]
        front = arena[:, 4:8, :].rearrange("p a b -> p (a b)")
        upad_ = front[:, 0:DT * (PADT + SEQ)]
        vcT = front[:, DT * (PADT + SEQ):DT * (PADT + SEQ) + GROUPS * SEQ].rearrange("p (g t) -> p g t", g=GROUPS)
        adaw = arena[:, 8:16, :]
        adaw1 = arena[:, 0:8, :]
        w1 = arena[:, 8:16, :].rearrange("p a b -> p (a b)").rearrange("p (l n) -> p l n", n=HID)
        urow = arena[:, 8:16, :]

        def vrow(s):
            return arena[:, (s + 4) % CH, :]

        x = sb("x", [P, TT, D])
        hT = sb("hT", [P, DT, SEQ])
        qT = sb("qT", [P, HEADS, SEQ])
        kT_ = sb("kT", [P, GROUPS * 3 * SEQ])
        kT = kT_[:, :].rearrange("p (g b t) -> p g b t", g=GROUPS, b=3)
        subk = kT_[:, 0:2 * PH * NK].rearrange("p (m k) -> p m k", k=NK)
        V = sb("V", [P, TT, 2 * GROUPS * DV])
        gates = sb("gates", [P, TT, 3, HEADS])
        upad = upad_.rearrange("p (j t) -> p j t", j=DT)
        y = sb("y", [P, DT, SEQ])
        yf = y[:, :, :].rearrange("p a b -> p (a b)")
        swork = yf[:, 0:512].rearrange("p (m k) -> p m k", k=NK)
        cand = yf[:, 512:1024].rearrange("p (h c) -> p h c", h=2)
        cwork = yf[:, 1024:1536].rearrange("p (h c) -> p h c", h=2)
        oneh = yf[:, 1536:2048].rearrange("p (e c) -> p e c", c=TOPK)
        sig = sb("sig", [P, 2 * DT, SEQ])
        h2 = sig[:, 0:8, :].rearrange("p a b -> p (a b)").rearrange("p (t d) -> p t d", t=TT)
        tb = sb("tb", [P, HEADS, SEQ])
        tbf = tb[:, :, :].rearrange("p a b -> p (a b)")
        ohc = tbf[0:BUCKETS + 1, 0:NCMP * SEQ].rearrange("p (n t) -> p n t", n=NCMP)
        rows = tbf.rearrange("p (v d) -> p v d", v=4)
        sc = sb("sc", [P, 4096])
        xs = sc[:, 0:2048].rearrange("p (t d) -> p t d", t=TT)
        ohr = sc[0:BUCKETS + 1, 2048:2560]
        cact = sc[:, 3072:4096]
        kcA, kcB, vcA, vcB = (sc[:, 1024 * i:1024 * i + 1024].rearrange("p (g t) -> p g t", g=GROUPS)
                              for i in range(4))
        attn = xs
        attnT = sc[:, 2048:4096].rearrange("p (j t) -> p j t", j=DT)
        ssb = sc[:, :].rearrange("p (t m k) -> p t m k", t=TT, k=NK)
        S_ = sb("S", [P, 2 * 2 * SEQ])
        S = S_[:, :].rearrange("p (u b t) -> p u b t", u=2, b=2)
        revsb = S_[0:HEADS, 0:512]
        wide = S_[:, :].rearrange("p (j t) -> p j t", j=DT)
        junk = S_[:, :]
        PT = sb("PT", [P, 2, 512])
        tmp = PT[:, :, :].rearrange("p a b -> p (a b)")
        PcT = sb("PcT", [P, 512])
        cols = sb("cols", [P, NCOLS])
        mod = sb("mod", [P, 48])
        modst = sb("modst", [P, 8])
        A1 = sb("A1", [P, DT])
        vec4 = sb("vec4", [P, 4, DT])
        table = sb("table", [BUCKETS + 1, HEADS])
        posk = sb("posk", [DQK, CMP_L])
        posv = sb("posv", [DV, CMP_L])
        w2k = sb("w2k", [P, 2, DQK])
        w2v = sb("w2v", [P, 2, DV])
        hidk = sb("hidk", [P, 2, 64])
        hidv = sb("hidv", [P, 2, 64])
        kcT = sb("kcT", [DQK, GROUPS * NCMP])
        vcv = sb("vcv", [NCMP, GROUPS * DV])
        tbc = sb("tbc", [P, TT, HEADS, NCMP])
        Sc = sb("Sc", [P, REP, NCMP])
        nmc = sb("nmc", [P, REP])
        nm = sb("nm", [P, 2, 2])
        Z = sb("Z", [P, 2, REP, 3])
        rz = sb("rz", [P, REP, 3])
        coef = sb("coef", [P, REP, 3])
        otmp = sb("otmp", [P, 2, 2 * 3 * DV])
        ident = sb("ident", [P, P])
        ones = sb("ones", [P, P])
        iota16 = sb("iota16", [P, TOPK])
        rowok = sb("rowok", [P, 1])
        eps = sb("eps", [P, 1])
        ss = sb("ss", [P, 8])
        std = sb("std", [P, 8])
        rstd = sb("rstd", [P, 8])
        stdc = sb("stdc", [P, SEQ])
        EU = SEG * CH
        v16 = sb("v16", [P, 4, TOPK])
        i16 = sb("i16", [P, 4, TOPK], U32)
        i16f = sb("i16f", [P, 4, TOPK])
        t16 = sb("t16", [P, 2, TOPK])
        p16 = sb("p16", [P, EU], U32)
        pa = sb("pa", [P, EU], U32)
        paf = sb("paf", [P, EU])
        e1 = sb("e1", [P, EU])
        e2 = sb("e2", [P, EU])
        idx = sb("idx", [P, TT * CPT, CH], I32)
        wgt = sb("wgt", [P, TT * CPT, CH])
        wsum = sb("wsum", [P, 2])
        stage = sb("stage", [P, SEG, CH], I32)
        dot = sb("dot", [P, 2, CH])
        gl = sb("gl", [P, 2, CH])
        cf = sb("cf", [P, 2, CH])
        diag = sig[:, 8:16, :].rearrange("p a b -> p (a b)").rearrange("p (u s c) -> p u s c", u=2, s=CH)
        pb = ctx.enter_context(nc.psum_tensor("pb", [P, 8, 512], F32))

        s_x, s_c, s_cols, s_tbl, s_oh, s_small = (sem(n) for n in
                                                  ("x_in", "c_in", "cols_in", "table_in", "onehot_in", "small_in"))
        ring_in = [sem(f"ring_in{i}") for i in range(RING)]
        ada_in1 = [sem(f"ada_in1_{i}") for i in range(8)]
        ada_in = [sem(f"ada_in{i}") for i in range(8)]
        ada_more = [sem(f"ada_more{i}") for i in range(8)]
        rev_out, tb_in, w1_in, sub_in = sem("rev_out"), sem("tb_in"), sem("w1_in"), sem("sub_in")
        ring_used, ada_used = sem("ring_used"), sem("ada_used")
        g_const, g_rowok, g_chain = sem("g_const"), sem("g_rowok"), sem("g_chain")
        a_c, a_ss, a_std, a_rev, a_cmpb = (sem(n) for n in ("a_c", "a_ss", "a_std", "a_rev", "a_cmpb"))
        a_evac, a_v, a_hk, a_kc, a_hv, a_vc, a_stdc, a_z = (
            sem(n) for n in ("a_evac", "a_v", "a_hk", "a_kc", "a_hv", "a_vc", "a_stdc", "a_z"))
        a_cexp, a_exp, a_pt, a_pct, a_at, a_row, a_h2T, a_q, a_wexp = (
            sem(n) for n in ("a_cexp", "a_exp", "a_pt", "a_pct", "a_at", "a_row", "a_h2T", "a_q", "a_wexp"))
        a_s = sem("a_s")
        a_turn, a_gl, a_dg = sem("a_turn"), sem("a_gl"), sem("a_dg")
        p_rev, p_cmpb, p_xT, p_mean, p_var, p_hk, p_kc, p_hv, p_vc = (
            sem(n) for n in ("p_rev", "p_cmpb", "p_xT", "p_mean", "p_var", "p_hk", "p_kc",
                             "p_hv", "p_vc"))
        p_cs, p_s, p_t, p_ct, p_o, p_at, p_ao, p_row, p_out, p_h2T, p_q, p_sc = (
            sem(n) for n in ("p_cs", "p_s", "p_t", "p_ct", "p_o", "p_at", "p_ao", "p_row", "p_out", "p_h2T",
                             "p_q", "p_sc"))
        v_chain, v_xs, v_hT, v_y, v_vec, v_pos, v_yc, v_sq, v_yn, v_zb = (
            sem(n) for n in ("v_chain", "v_xs", "v_hT", "v_y", "v_vec", "v_pos", "v_yc", "v_sq", "v_yn", "v_zb"))
        v_cs, v_csub, v_st, v_mx, v_coef, v_o, v_at, v_m, v_row, v_x2, v_h2 = (
            sem(n) for n in ("v_cs", "v_csub", "v_st", "v_mx", "v_coef", "v_o", "v_at", "v_m", "v_row", "v_x2",
                             "v_h2"))
        v_idx, v_wsub, v_cf, v_out = sem("v_idx"), sem("v_wsub"), sem("v_cf"), sem("v_out")
        u_in = [sem(f"u_in{i}") for i in range(CH)]
        v_in = [sem(f"v_in{i}") for i in range(CH)]
        u_free, v_free, g_staged, g_turn = sem("u_free"), sem("v_free"), sem("g_staged"), sem("g_turn")
        o_done = sem("o_done")

        rev_dram = nc.dram_tensor("rev_scratch", (HEADS, P, REV), F32).ap()

        def unit_keys(n):
            tt, h = divmod(n, HEADS)
            return tt, h, h // REP, h % REP, P * (tt + 1)

        NU = TT * HEADS

        block = ctx.enter_context(nc.Block())

        @block.sync
        def _(sp):
            sp.dma_start(cact, a["c"].partition_broadcast(P)).then_inc(s_c, 16)
            for s in range(8):
                sp.dma_start(adaw[:, s, :], a["w_ada"][s]).then_inc(ada_in[s], 16)
            sp.dma_start(cols[:, :], a["cols"]).then_inc(s_cols, 16)
            sp.dma_start(x[:, :, :], a["x"].rearrange("(t p) d -> p t d", p=P)).then_inc(s_x, 16)
            for s in range(8):
                sp.dma_start(adaw1[:, s, :], a["w_ada"][8 + s]).then_inc(ada_in1[s], 16)
            sp.dma_start(table[0:BUCKETS, :], a["rel_table"]).then_inc(s_tbl, 16)
            for s in range(RING):
                sp.wait_ge(ada_used, 8 + s + 1)
                sp.dma_start(ring[:, s, :], a["w_stream"][s]).then_inc(ring_in[s], 16)
            sp.dma_start(ohr, a["onehot_rev"]).then_inc(s_oh, 16)
            sp.dma_start(ohc, a["onehot_cmp"]).then_inc(s_oh, 16)
            sp.dma_start(posk[:, :], a["pos_k"]).then_inc(s_small, 16)
            sp.dma_start(posv[:, :], a["pos_v"]).then_inc(s_small, 16)
            sp.dma_start(w2k[:, :, :], a["w2k"]).then_inc(s_small, 16)
            sp.dma_start(w2v[:, :, :], a["w2v"]).then_inc(s_small, 16)
            with sp.Fori(1, TILES // RING) as r:
                for s in range(RING):
                    sp.wait_ge(ring_used, (r - 1) * RING + s + 1)
                    sp.dma_start(ring[:, s, :], a["w_stream"][r * RING + s]).then_inc(ring_in[s], 16)
            for t in range(TT):
                sp.wait_ge(v_out, t + 1)
                sp.dma_start(out[t * P:(t + 1) * P, :], x[:, t, :]).then_inc(o_done, 16)
            sp.wait_ge(o_done, 16 * TT)

        @block.gpsimd
        def _(g):
            g_ch = Chain(g, g_chain)
            g_ch.link(nc.gpsimd.memset(table[BUCKETS:BUCKETS + 1, :], NEG))
            nc.gpsimd.memset(eps[:, :], EPS).then_inc(g_const, 1)
            nc.gpsimd.memset(ones[:, :], 1.0 / D).then_inc(g_const, 1)
            g_ch.link(nc.gpsimd.memset(ident[:, :], 0.0))
            nc.gpsimd.affine_select(out=ident[:, :], in_=ident[:, :], compare_op=ALU.not_equal, fill=1.0, base=0,
                                    pattern=[[-1, P]], channel_multiplier=1).then_inc(g_const, 1)
            nc.gpsimd.iota(iota16[:, :], pattern=[[1, TOPK]], base=0, channel_multiplier=0,
                           allow_small_or_imprecise_dtypes=True).then_inc(g_const, 1)
            g_ch.link(nc.gpsimd.memset(rowok[:, :], 1.0))
            nc.gpsimd.affine_select(out=rowok[:, :], in_=rowok[:, :], compare_op=ALU.is_ge, fill=0.0,
                                    base=-(CMP_L - 1), pattern=[[0, 1]], channel_multiplier=1).then_inc(g_rowok, 1)
            g.wait_ge(a_rev, 1)
            g.dma_start(rev_dram, revsb[:, 0:REV].unsqueeze(1).broadcast_to((HEADS, P, REV))).then_inc(rev_out, 16)
            g.wait_ge(rev_out, 16)
            g.wait_ge(p_cmpb, 1)
            g.dma_start(tb[:, :, :], bass.AP(rev_dram.tensor, P - 1, [[REV - 1, P], [P * REV, HEADS], [1, SEQ]])
                        ).then_inc(tb_in, 16)
            with g.Fori(2, 6) as i:
                for s in range(8):
                    g.wait_ge(ada_used, (i - 1) * 8 + s + 1)
                    g.sem_inc(g_turn, 1)
                    g.dma_start(adaw[:, s, :], a["w_ada"][i * 8 + s]).then_inc(ada_more[s], 16)
            g.wait_ge(ada_used, 48)
            g.dma_start(w1[0:DQK, :, :], a["w1k"]).then_inc(w1_in, 16)
            g.wait_ge(p_hk, 1)
            g.dma_start(w1[0:DV, :, :], a["w1v"]).then_inc(w1_in, 16)
            g.wait_ge(p_s, NU)
            g.dma_start(subk, a["subkeys"]).then_inc(sub_in, 16)
            g.wait_ge(p_hv, 1)
            g.wait_ge(v_m, DT)
            with g.Fori(0, UNITS) as k:
                g.wait_ge(v_idx, k + 1)
                g.sem_inc(g_turn, 1)
                for b in range(SEG):
                    c = k * SEG + b
                    nc.gpsimd.tensor_copy(stage[:, b, :], idx[:, c, :]).then_inc(g_staged, 1)
                    g.wait_ge(g_staged, c + 1)
                    g.sem_inc(g_turn, 1)
                    for s in range(CH):
                        g.wait_ge(u_free, c * CH + (s + 1))
                        g.sem_inc(g_turn, 1)
                        nc.gpsimd.indirect_dma_start(
                            out=urow[:, s, :], out_offset=None, in_=a["peer_u"],
                            in_offset=bass.IndirectOffsetOnAxis(ap=stage[:, b, s:s + 1], axis=0),
                        ).then_inc(u_in[s], 16)
                    for s in range(CH):
                        g.wait_ge(v_free, c * CH + (s + 1))
                        g.sem_inc(g_turn, 1)
                        nc.gpsimd.indirect_dma_start(
                            out=vrow(s), out_offset=None, in_=a["peer_v"],
                            in_offset=bass.IndirectOffsetOnAxis(ap=stage[:, b, s:s + 1], axis=0),
                        ).then_inc(v_in[s], 16)

        @block.tensor
        def _(pe):
            mm = nc.tensor.matmul
            pe.sem_inc(v_free, CH // 2)

            pe.wait_ge(g_const, 4)
            pe.wait_ge(v_xs, TT)
            for j in range(DT):
                for t in range(TT):
                    o = (j % 2) * SEQ + t * P
                    last = nc.tensor.transpose(pb[:, 4 + j // 2, o:o + P], xs[:, t, j * P:(j + 1) * P], ident[:, :])
                if j % 2:
                    last.then_inc(p_xT, 1)

            def landed(tile):
                pe.wait_ge(ring_in[tile % RING], 16 * (tile // RING + 1))

            def column_tile(bank, slot, src):
                for k in range(DT):
                    last = mm(pb[:, bank, 0:SEQ], ring[:, slot, k * P:(k + 1) * P], src[:, k, :],
                              start=(k == 0), stop=(k == DT - 1))
                last.then_inc(ring_used, 1)

            def column_round(r, first=False):
                for s in range(RING):
                    pe.wait_ge(ring_in[s], r * 16 + 16)
                    if not first:
                        pe.wait_ge(a_evac, (r - 1) * RING + (s + 1))
                    column_tile(s, s, hT)

            pe.wait_ge(v_hT, DT)
            column_round(0, first=True)
            with pe.Fori(1, T_MERGE // RING) as r:
                column_round(r)

            pe.wait_ge(s_tbl, 16)
            pe.wait_ge(s_oh, 32)
            mm(pb[0:HEADS, 4, :], table[:, :], ohr, start=True, stop=True).then_inc(p_rev, 1)
            for t in range(TT):
                for n in range(NCMP):
                    o = (t * NCMP + n) * HEADS
                    last = mm(pb[:, 5, o:o + HEADS], ohc[:, n, t * P:(t + 1) * P], table[:, :], start=True, stop=True)
            last.then_inc(p_cmpb, 1)

            with pe.Fori(T_MERGE // RING, T_V // RING) as r:
                column_round(r)

            pe.wait_ge(a_evac, T_V)
            for k in range(DT):
                landed(T_V + k)
                for t in range(TT):
                    h = hT[:, k, t * P:(t + 1) * P]
                    mm(pb[:, t, :], h, ring[:, k % RING, 0:512], start=(k == 0), stop=(k == DT - 1))
                    last = mm(pb[:, 2 + t, 0:48], h, ring[:, k % RING, 512:560], start=(k == 0), stop=(k == DT - 1))
                last.then_inc(ring_used, 1)

            pe.wait_ge(v_y, 2)
            for k in range(DT):
                last = mm(pb[:, 4, 0:SEQ], ones[:, :], y[:, k, :], start=(k == 0), stop=(k == DT - 1))
            last.then_inc(p_mean, 1)

            def hidden(bank, dk, A, B):
                for hh in range(2):
                    for l in range(CMP_L):
                        src, o = (A, l) if l < CMP_ST else (B, l)
                        last = mm(pb[:, bank, hh * 64:hh * 64 + GROUPS * NCMP],
                                  w1[0:dk, l, hh * P:(hh + 1) * P],
                                  src[0:dk, :, o:o + (NCMP - 1) * CMP_ST + 1:CMP_ST],
                                  start=(l == 0), stop=(l == CMP_L - 1))
                return last

            pe.wait_ge(w1_in, 16)
            pe.wait_ge(v_pos, 4)
            hidden(5, DQK, kcA, kcB).then_inc(p_hk, 1)
            pe.wait_ge(v_sq, 1)
            for k in range(DT):
                last = mm(pb[:, 4, SEQ:2 * SEQ], ones[:, :], upad[:, k, 0:SEQ], start=(k == 0), stop=(k == DT - 1))
            last.then_inc(p_var, 1)
            pe.wait_ge(a_hk, 1)
            pe.wait_ge(s_small, 64)
            for k in range(2):
                last = mm(pb[0:DQK, 6, 0:GROUPS * NCMP], w2k[:, k, :], hidk[:, k, 0:GROUPS * NCMP],
                          start=(k == 0), stop=(k == 1))
            last.then_inc(p_kc, 1)
            pe.wait_ge(w1_in, 32)
            hidden(7, DV, vcA, vcB).then_inc(p_hv, 1)
            pe.wait_ge(a_hv, 1)
            for g in range(GROUPS):
                for k in range(2):
                    last = mm(pb[0:NCMP, 5, g * DV:(g + 1) * DV], hidv[:, k, g * NCMP:(g + 1) * NCMP], w2v[:, k, :],
                              start=(k == 0), stop=(k == 1))
            last.then_inc(p_vc, 1)

            pe.wait_ge(a_z, DT)
            pe.wait_ge(a_v, 4)
            for j in range(DT):
                landed(T_CO + j)
                if j >= 4:
                    pe.wait_ge(v_zb, j - 3)
                column_tile(j % 4, j % RING, y)

            pe.wait_ge(a_kc, 1)
            pe.wait_ge(a_vc, 1)
            pe.wait_ge(v_zb, DT)
            pe.wait_ge(a_stdc, 1)

            def cmp_scores(gi):
                tt, g = divmod(gi, GROUPS)
                if gi >= 1:
                    pe.wait_ge(v_cs, gi)
                for hh in range(REP):
                    last = mm(pb[:, 4, hh * NCMP:(hh + 1) * NCMP], qT[0:DQK, g * REP + hh, tt * P:(tt + 1) * P],
                              kcT[:, g * NCMP:(g + 1) * NCMP], start=True, stop=True)
                last.then_inc(p_cs, 1)

            def cmp_transposes(gi):
                pe.wait_ge(a_cexp, gi + 1)
                if gi >= 1:
                    pe.wait_ge(a_pct, gi)
                for hh in range(REP):
                    last = nc.tensor.transpose(pb[0:NCMP, 5, hh * P:(hh + 1) * P], Sc[:, hh, :], ident[:, :])
                last.then_inc(p_ct, 1)

            def scores(n):
                tt, h, g, hh, keys = unit_keys(n)
                if n >= 2:
                    pe.wait_ge(v_st, n - 1)
                mm(pb[:, n % 2, 0:2 * keys], qT[0:DQK, h, tt * P:(tt + 1) * P], kT[0:DQK, g, 1:3, 0:keys],
                   start=True, stop=True).then_inc(p_s, 1)

            def transposes(n):
                tt, h, g, hh, keys = unit_keys(n)
                pe.wait_ge(a_exp, 2 * (n + 1))
                if n >= 2:
                    pe.wait_ge(a_pt, n - 1)
                for b in range(2):
                    for kb in range(tt + 1):
                        o = (b * (tt + 1) + kb) * P
                        last = nc.tensor.transpose(pb[:, 2 + n % 2, o:o + P], S[:, n % 2, b, kb * P:(kb + 1) * P],
                                                   ident[:, :])
                last.then_inc(p_t, 1)

            def values(n):
                tt, h, g, hh, keys = unit_keys(n)
                gi = n // REP
                pe.wait_ge(a_pt, n + 1)
                pe.wait_ge(a_pct, gi + 1)
                if gi >= 1 and hh % 2 == 0:
                    pe.wait_ge(v_o, 2 * (gi - 1) + hh // 2 + 1)
                o = (hh % 2) * 3 * DV
                bank = 6 + hh // 2
                mm(pb[:, bank, o:o + DV], PcT[0:NCMP, hh * P:(hh + 1) * P], vcv[:, g * DV:(g + 1) * DV],
                   start=True, stop=True)
                for b in range(2):
                    for kb in range(tt + 1):
                        last = mm(pb[:, bank, o + (1 + b) * DV:o + (2 + b) * DV],
                                  PT[:, n % 2, (b * (tt + 1) + kb) * P:(b * (tt + 1) + kb + 1) * P],
                                  V[:, kb, (b * GROUPS + g) * DV:(b * GROUPS + g + 1) * DV],
                                  start=(kb == 0), stop=(kb == tt))
                last.then_inc(p_o, 1)

            for n in range(NU + 2):
                if n < NU:
                    if n % REP == 0:
                        cmp_scores(n // REP)
                    scores(n)
                    if n % REP == 1:
                        cmp_transposes(n // REP)
                if 1 <= n <= NU:
                    transposes(n - 1)
                if n >= 2:
                    values(n - 2)

            pe.wait_ge(v_at, 2 * GROUPS * TT)
            pe.wait_ge(a_pt, NU)
            pe.wait_ge(a_pct, GROUPS * TT)
            for t in range(TT):
                for jj in range(2):
                    for j in range(4):
                        last = nc.tensor.transpose(pb[:, 2 + 2 * t + jj, j * P:(j + 1) * P],
                                                   attn[:, t, (4 * jj + j) * P:(4 * jj + j + 1) * P], ident[:, :])
                    last.then_inc(p_at, 1)

            wide_bank = (0, 1, 6, 7)
            pe.wait_ge(a_at, 4)
            pe.wait_ge(v_o, 2 * GROUPS * TT)
            for j in range(DT):
                landed(T_AO + j)
                if j >= 4:
                    pe.wait_ge(v_m, j - 3)
                column_tile(wide_bank[j % 4], j % RING, attnT)

            for v in range(4):
                pe.wait_ge(v_row, v + 1)
                if v >= 2:
                    pe.wait_ge(a_row, v - 1)
                for j in range(DT):
                    last = mm(pb[:, 2 + 2 * (v % 2) + j // 4, (j % 4) * P:(j % 4 + 1) * P], wide[:, j, :], ident[:, :],
                              start=True, stop=True)
                last.then_inc(p_row, 1)

            pe.wait_ge(v_m, DT)
            for k in range(DT):
                landed(T_OUT + k)
                for t in range(TT):
                    for hf in range(2):
                        last = mm(pb[:, 6 * t + hf, :], y[:, k, t * P:(t + 1) * P],
                                  ring[:, k % RING, hf * 512:(hf + 1) * 512], start=(k == 0), stop=(k == DT - 1))
                last.then_inc(ring_used, 1)

            pe.wait_ge(v_h2, TT)
            pe.wait_ge(a_row, 4)
            for j in range(DT):
                for t in range(TT):
                    o = (j % 2) * SEQ + t * P
                    last = nc.tensor.transpose(pb[:, 2 + j // 2, o:o + P], h2[:, t, j * P:(j + 1) * P], ident[:, :])
                if j % 2:
                    last.then_inc(p_h2T, 1)
            pe.wait_ge(a_h2T, 4)
            pe.wait_ge(sub_in, 16)
            for m in range(2 * PH + 1):
                if m < 2 * PH:
                    landed(T_WQ + m)
                    if m >= 2:
                        pe.wait_ge(a_q, m - 1)
                    column_tile(m % 2, m % RING, hT)
                if m >= 1:
                    pe.wait_ge(a_q, m)
                    if m >= 3:
                        pe.wait_ge(a_s, m - 2)
                    for t in range(TT):
                        last = mm(pb[:, 2 + (m - 1) % 2, t * NK:(t + 1) * NK], qT[:, m - 1, t * P:(t + 1) * P],
                                  subk[:, m - 1, :], start=True, stop=True)
                    last.then_inc(p_sc, 1)
            pe.wait_ge(ring_used, TILES)
            pe.sem_inc(v_free, CH // 2)

            def expert_chunk(t, b, c, first=False):
                for s in range(CH):
                    pe.wait_ge(v_in[s], c * 16 + 16)
                    pe.wait_ge(a_dg, c * CH + (s + 1))
                    for hf in range(2):
                        last = mm(pb[:, 4 + 2 * t + hf, :], diag[:, b, s, :], vrow(s)[:, hf * 512:(hf + 1) * 512],
                                  start=(first and s == 0), stop=False, skip_group_check=True)
                    last.then_inc(v_free, 1)

            for t in range(TT):
                for b in range(2):
                    expert_chunk(t, b, CPT * t + b, first=(b == 0))
                with pe.Fori(1, CPT // 2) as i:
                    for b in range(2):
                        expert_chunk(t, b, i * 2 + (CPT * t + b))

        @block.scalar
        def _(act):
            fn = nc.scalar.activation

            def turn():
                act.sem_inc(a_turn, 1)

            act.wait_ge(s_c, 16)
            fn(cact, cact, ACT.Silu).then_inc(a_c, 1)
            act.wait_ge(s_x, 16)
            for t in range(TT):
                fn(xs[:, t, :], x[:, t, :], ACT.Square, accum_out=ss[:, t:t + 1]).then_inc(a_ss, 1)
            act.wait_ge(a_ss, TT)
            act.wait_ge(g_const, 4)
            fn(std[:, 0:TT], ss[:, 0:TT], ACT.Sqrt, scale=1.0 / D, bias=eps[:, :]).then_inc(a_std, 1)

            def evac(tile, s, dst, func, rows_=P):
                act.wait_ge(ring_used, tile + (s + 1))
                turn()
                fn(dst, pb[0:rows_, s % 4, 0:SEQ], func).then_inc(a_evac, 1)

            act.wait_ge(v_hT, DT)
            with act.Fori(0, T_MERGE // RING) as r:
                for s in range(RING):
                    if s % 2 == 0:
                        evac(r * RING, s, upad[:, r * 2 + s // 2, PADT:PADT + SEQ], ACT.Copy)
                    else:
                        evac(r * RING, s, y[:, r * 2 + s // 2, :], ACT.Sigmoid)
            act.wait_ge(p_rev, 1)
            fn(revsb, pb[0:HEADS, 4, :], ACT.Copy).then_inc(a_rev, 1)
            act.wait_ge(p_cmpb, 1)
            for t in range(TT):
                o = t * NCMP * HEADS
                last = fn(tbc[:, t, :, :],
                          pb[:, 5, o:o + NCMP * HEADS].rearrange("p (n h) -> p h n", n=NCMP), ACT.Copy)
            last.then_inc(a_cmpb, 1)
            with act.Fori(0, (T_GROUP - T_MERGE) // RING) as r:
                for s in range(RING):
                    evac(r * RING + T_MERGE, s, sig[:, r * RING + s, :], ACT.Sigmoid)
            with act.Fori(0, GROUPS) as g:
                for s in range(REP):
                    evac(g * 8 + T_GROUP, s, qT[0:DQK, g * REP + s, :], ACT.Copy, DQK)
                for s in range(REP, 7):
                    evac(g * 8 + T_GROUP, s, kT[0:DQK, g, s - REP, :], ACT.Copy, DQK)
                evac(g * 8 + T_GROUP, 7, vcT[0:DV, g, :], ACT.Copy, DV)
            act.wait_ge(ring_used, T_CO)
            for t in range(TT):
                fn(V[:, t, :], pb[:, t, :], ACT.Copy).then_inc(a_v, 1)
            for t in range(TT):
                fn(gates[:, t, :, :], pb[:, 2 + t, 0:48], ACT.Sigmoid).then_inc(a_v, 1)
            act.wait_ge(p_hk, 1)
            fn(hidk[:, :, 0:GROUPS * NCMP], pb[:, 5, 0:P].rearrange("p (a b) -> p a b", a=2)[:, :, 0:GROUPS * NCMP],
               ACT.Gelu_apprx_tanh).then_inc(a_hk, 1)
            act.wait_ge(p_kc, 1)
            fn(kcT[:, :], pb[0:DQK, 6, 0:GROUPS * NCMP], ACT.Copy).then_inc(a_kc, 1)
            act.wait_ge(p_var, 1)
            fn(stdc[:, :], pb[:, 4, SEQ:2 * SEQ], ACT.Sqrt, bias=eps[:, :]).then_inc(a_stdc, 1)
            act.wait_ge(v_yn, 1)
            for j in range(DT):
                fn(y[:, j, :], y[:, j, :], ACT.Silu, scale=cols[:, C_LG + j:C_LG + j + 1],
                   bias=cols[:, C_LB + j:C_LB + j + 1]).then_inc(a_z, 1)
            act.wait_ge(p_hv, 1)
            fn(hidv[:, :, 0:GROUPS * NCMP], pb[:, 7, 0:P].rearrange("p (a b) -> p a b", a=2)[:, :, 0:GROUPS * NCMP],
               ACT.Gelu_apprx_tanh).then_inc(a_hv, 1)
            act.wait_ge(p_vc, 1)
            fn(vcv[:, :], pb[0:NCMP, 5, 0:GROUPS * DV], ACT.Copy).then_inc(a_vc, 1)

            def exps(n):
                tt, h, g, hh, keys = unit_keys(n)
                gi = n // REP
                act.wait_ge(v_mx, n + 1)
                if gi >= 2 and hh == 0:
                    act.wait_ge(v_coef, gi - 1)
                for b in range(2):
                    fn(S[:, n % 2, b, 0:keys], S[:, n % 2, b, 0:keys], ACT.Exp, bias=nm[:, n % 2, b:b + 1],
                       accum_out=Z[:, gi % 2, hh, 1 + b:2 + b]).then_inc(a_exp, 1)

            for n in range(NU + 1):
                gi = n // REP
                if n < NU:
                    if n % REP == 0:
                        act.wait_ge(v_csub, gi + 1)
                        fn(Sc[:, :, :], Sc[:, :, :], ACT.Exp).then_inc(a_cexp, 1)
                    exps(n)
                if n >= 1:
                    u = n - 1
                    tt = u // HEADS
                    act.wait_ge(p_t, u + 1)
                    if u >= 2:
                        act.wait_ge(p_o, u - 1)
                    fn(PT[:, u % 2, 0:2 * P * (tt + 1)], pb[:, 2 + u % 2, 0:2 * P * (tt + 1)],
                       ACT.Copy).then_inc(a_pt, 1)
                if n < NU and n % REP == 1:
                    act.wait_ge(p_ct, gi + 1)
                    if gi >= 1:
                        act.wait_ge(p_o, gi * REP)
                    fn(PcT[0:NCMP, :], pb[0:NCMP, 5, :], ACT.Copy).then_inc(a_pct, 1)
            for t in range(TT):
                for jj in range(2):
                    act.wait_ge(p_at, 2 * t + jj + 1)
                    fn(attnT[:, 4 * jj:4 * jj + 4, t * P:(t + 1) * P],
                       pb[:, 2 + 2 * t + jj, :].rearrange("p (j t) -> p j t", j=4), ACT.Copy).then_inc(a_at, 1)
            for v in range(4):
                act.wait_ge(p_row, v + 1)
                fn(rows[:, v, :], pb[:, 2 + 2 * (v % 2):4 + 2 * (v % 2), :].rearrange("p a b -> p (a b)"),
                   ACT.Copy).then_inc(a_row, 1)
            act.wait_ge(ring_used, T_WQ)
            act.wait_ge(p_row, 4)
            for t in range(TT):
                fn(junk, pb[:, 6 * t:6 * t + 2, :].rearrange("p a b -> p (a b)"), ACT.Square,
                   accum_out=ss[:, 2 + t:3 + t]).then_inc(a_ss, 1)
                act.wait_ge(a_ss, TT + t + 1)
            fn(std[:, 2:4], ss[:, 2:4], ACT.Sqrt, scale=1.0 / D, bias=eps[:, :]).then_inc(a_std, 1)
            for t in range(TT):
                act.wait_ge(v_x2, t + 1)
                fn(junk, x[:, t, :], ACT.Square, accum_out=ss[:, 4 + t:5 + t]).then_inc(a_ss, 1)
                act.wait_ge(a_ss, 2 * TT + t + 1)
            fn(std[:, 4:6], ss[:, 4:6], ACT.Sqrt, scale=1.0 / D, bias=eps[:, :]).then_inc(a_std, 1)
            for b in range(4):
                act.wait_ge(p_h2T, b + 1)
                fn(hT[:, 2 * b:2 * b + 2, :], pb[:, 2 + b, :].rearrange("p (a t) -> p a t", a=2),
                   ACT.Copy).then_inc(a_h2T, 1)
            for m in range(2 * PH + 1):
                if m < 2 * PH:
                    act.wait_ge(ring_used, T_WQ + m + 1)
                    fn(qT[:, m, :], pb[:, m % 2, 0:SEQ], ACT.Copy).then_inc(a_q, 1)
                if m >= 1:
                    act.wait_ge(p_sc, m)
                    fn(ssb[:, :, m - 1, :], pb[:, 2 + (m - 1) % 2, 0:TT * NK].rearrange("p (t k) -> p t k", t=TT),
                       ACT.Copy).then_inc(a_s, 1)

            def unit_exp(k):
                act.wait_ge(v_wsub, k + 1)
                fn(wgt[:, SEG * k:SEG * (k + 1), :], wgt[:, SEG * k:SEG * (k + 1), :], ACT.Exp).then_inc(a_wexp, 1)

            unit_exp(0)
            for k in range(UNITS):
                if k + 1 < UNITS:
                    unit_exp(k + 1)
                with act.Fori(0, SEG // 2) as i:
                    for b in range(2):
                        c = i * 2 + (SEG * k + b)
                        act.wait_ge(u_free, c * CH + 2 * CH)
                        fn(gl[:, b, :], dot[:, b, :], ACT.Gelu_apprx_tanh).then_inc(a_gl, 1)
                        act.wait_ge(v_cf, c + 1)
                        for s in range(CH):
                            fn(diag[:, b, s, :], ident[:, :], ACT.Copy, scale=cf[:, b, s:s + 1]).then_inc(a_dg, 1)
            for t in range(TT):
                act.wait_ge(v_free, CH + NE * (t + 1))
                fn(junk, pb[:, 4 + 2 * t:6 + 2 * t, :].rearrange("p a b -> p (a b)"), ACT.Square,
                   accum_out=ss[:, 6 + t:7 + t]).then_inc(a_ss, 1)
                act.wait_ge(a_ss, 3 * TT + t + 1)
                fn(std[:, 6 + t:7 + t], ss[:, 6 + t:7 + t], ACT.Sqrt, scale=1.0 / D, bias=eps[:, :]).then_inc(a_std, 1)

        @block.vector
        def _(dve):
            V_ = nc.vector
            ch = Chain(dve, v_chain)
            dve.sem_inc(u_free, CH)

            def ada_part(i, landed, n, w=adaw):
                for s in range(8):
                    dve.wait_ge(landed[s], n * 16 + 16)
                    V_.tensor_tensor_reduce(out=w[:, s, :], in0=w[:, s, :], in1=cact, scale=1.0, scalar=0.0,
                                            op0=ALU.mult, op1=ALU.add, accum_out=modst[:, s:s + 1]
                                            ).then_inc(ada_used, 1)
                dve.wait_ge(ada_used, i * 8 + 8)
                ch.link(V_.tensor_tensor(mod[:, bass.ds(i * 8, 8)], modst[:, :], cols[:, bass.ds(i * 8 + C_BADA, 8)], ALU.add))

            dve.wait_ge(a_c, 1)
            dve.wait_ge(s_cols, 16)
            ada_part(0, ada_in, 0)
            dve.wait_ge(a_std, 1)
            ch.link(V_.reciprocal(rstd[:, 0:TT], std[:, 0:TT]))
            for t in range(TT):
                V_.tensor_scalar(xs[:, t, :], x[:, t, :], rstd[:, t:t + 1], None, ALU.mult).then_inc(v_xs, 1)
            ada_part(1, ada_in1, 0, adaw1)
            ch.link(V_.scalar_tensor_tensor(out=A1[:, :], in0=mod[:, 8:16], scalar=1.0, in1=cols[:, C_GPM:C_GPM + DT],
                                            op0=ALU.add, op1=ALU.mult))
            for j in range(DT):
                dve.wait_ge(p_xT, j // 2 + 1)
                o = (j % 2) * SEQ
                V_.tensor_scalar(hT[:, j, :], pb[:, 4 + j // 2, o:o + SEQ], A1[:, j:j + 1], mod[:, j:j + 1],
                                 ALU.mult, ALU.add).then_inc(v_hT, 1)

            ch.link(V_.memset(upad[:, :, 0:PADT], 0.0))
            with dve.Fori(0, 2) as r:
                ch.enter(r, 4 * TAPS + 4 - 4)
                for jj in range(4):
                    dve.wait_ge(a_evac, r * 8 + (2 * jj + 2))
                    u = upad[:, r * 4 + jj, PADT:PADT + SEQ]
                    last = V_.tensor_tensor(u, u, y[:, r * 4 + jj, :], ALU.mult)
                    n = ch.add(last)
                dve.wait_ge(v_chain, n)
                for k in range(TAPS):
                    for jj in range(4):
                        j = r * 4 + jj
                        w = cols[:, bass.ds(j * TAPS + (C_CW + k), 1)]
                        if k == 0:
                            ins = V_.tensor_scalar(y[:, j, :], upad[:, j, 0:SEQ], w, cols[:, bass.ds(j + C_CB, 1)],
                                                   ALU.mult, ALU.add)
                        else:
                            dve.wait_ge(v_chain, n - 3 + (jj if k == TAPS - 1 else 0))
                            ins = V_.scalar_tensor_tensor(out=y[:, j, :], in0=upad[:, j, k:k + SEQ], scalar=w,
                                                          in1=y[:, j, :], op0=ALU.mult, op1=ALU.add)
                        if k < TAPS - 1:
                            n = ch.add(ins)
                        elif jj == 3:
                            ins.then_inc(v_y, 1)
                dve.wait_ge(v_y, r + 1)
            ch.leave(2)

            with dve.Fori(2, 6) as i:
                ch.enter(i - 2, 1)
                ada_part(i, ada_more, i - 2)
            ch.leave(4)
            ch.add(V_.tensor_tensor(vec4[:, 0, :], mod[:, 16:24], cols[:, C_GOM:C_GOM + DT], ALU.mult))
            ch.add(V_.scalar_tensor_tensor(out=vec4[:, 1, :], in0=mod[:, 32:40], scalar=1.0,
                                           in1=cols[:, C_GPF:C_GPF + DT], op0=ALU.add, op1=ALU.mult))
            ch.add(V_.tensor_copy(vec4[:, 2, :], mod[:, 24:32]))
            ch.link(V_.tensor_tensor(vec4[:, 3, :], mod[:, 40:48], cols[:, C_GOF:C_GOF + DT], ALU.mult))

            dve.wait_ge(a_evac, T_V)
            dve.wait_ge(s_small, 64)
            dve.wait_ge(v_hT, DT)
            for dst, src, pos, dk, o in ((kcA, kT[0:DQK, :, 0, :], posk, DQK, 0), (kcB, kT[0:DQK, :, 0, :], posk, DQK, CMP_ST),
                                         (vcA, vcT[0:DV, :, :], posv, DV, 0), (vcB, vcT[0:DV, :, :], posv, DV, CMP_ST)):
                V_.tensor_tensor(
                    dst[0:dk].rearrange("p g (c l) -> p g c l", l=CMP_ST),
                    src.rearrange("p g (c l) -> p g c l", l=CMP_ST),
                    pos[:, o:o + CMP_ST].unsqueeze(1).unsqueeze(1).broadcast_to((dk, GROUPS, SEQ // CMP_ST, CMP_ST)),
                    ALU.add).then_inc(v_pos, 1)

            dve.wait_ge(p_mean, 1)
            ch.link(V_.tensor_tensor(y[:, :, :], y[:, :, :],
                                     pb[:, 4, 0:SEQ].unsqueeze(1).broadcast_to((P, DT, SEQ)), ALU.subtract))
            V_.tensor_tensor(upad[:, :, 0:SEQ], y[:, :, :], y[:, :, :], ALU.mult).then_inc(v_sq, 1)
            dve.wait_ge(a_stdc, 1)
            ch.link(V_.reciprocal(stdc[:, :], stdc[:, :]))
            dve.wait_ge(v_sq, 1)
            V_.tensor_tensor(y[:, :, :], y[:, :, :], stdc[:, :].unsqueeze(1).broadcast_to((P, DT, SEQ)),
                             ALU.mult).then_inc(v_yn, 1)
            dve.wait_ge(a_v, 4)
            dve.wait_ge(g_rowok, 1)
            ch.add(V_.tensor_scalar(gates[:, 0, 0, :], gates[:, 0, 0, :], rowok[:, :], None, ALU.mult))
            for j in range(DT):
                dve.wait_ge(ring_used, T_CO + j + 1)
                V_.tensor_tensor(upad[:, j, 0:SEQ], pb[:, j % 4, 0:SEQ], sig[:, DT + j, :], ALU.mult).then_inc(v_zb, 1)

            dve.wait_ge(tb_in, 16)
            dve.wait_ge(a_cmpb, 1)
            dve.wait_ge(p_vc, 1)

            def cmp_logits(gi):
                tt, g = divmod(gi, GROUPS)
                dve.wait_ge(p_cs, gi + 1)
                if gi >= 1:
                    dve.wait_ge(p_ct, gi)
                V_.scalar_tensor_tensor(out=Sc[:, :, :],
                                        in0=pb[:, 4, 0:REP * NCMP].rearrange("p (h n) -> p h n", h=REP),
                                        scalar=SCALE, in1=tbc[:, tt, g * REP:(g + 1) * REP, :],
                                        op0=ALU.mult, op1=ALU.add).then_inc(v_cs, 1)
                dve.wait_ge(v_cs, gi + 1)
                ch.link(V_.tensor_reduce(nmc[:, :], Sc[:, :, :], AX, ALU.max))
                V_.tensor_tensor(Sc[:, :, :], Sc[:, :, :], nmc[:, :].unsqueeze(2).broadcast_to((P, REP, NCMP)),
                                 ALU.subtract).then_inc(v_csub, 1)

            def logits(n):
                tt, h, g, hh, keys = unit_keys(n)
                dve.wait_ge(p_s, n + 1)
                if n >= 2:
                    dve.wait_ge(p_t, n - 1)
                V_.scalar_tensor_tensor(out=S[:, n % 2, :, 0:keys],
                                        in0=pb[:, n % 2, 0:2 * keys].rearrange("p (b t) -> p b t", b=2),
                                        scalar=SCALE,
                                        in1=tb[:, h, SEQ - keys:SEQ].unsqueeze(1).broadcast_to((P, 2, keys)),
                                        op0=ALU.mult, op1=ALU.add).then_inc(v_st, 1)
                dve.wait_ge(v_st, n + 1)
                V_.tensor_reduce(nm[:, n % 2, :], S[:, n % 2, :, 0:keys], AX, ALU.max, negate=True).then_inc(v_mx, 1)

            def combine(gi):
                tt, g = divmod(gi, GROUPS)
                dve.wait_ge(a_exp, 2 * REP * (gi + 1))
                ch.link(V_.reciprocal(rz[:, :, :], Z[:, gi % 2, :, :]))
                V_.tensor_tensor(coef[:, :, :], rz[:, :, :],
                                 gates[:, tt, :, g * REP:(g + 1) * REP].rearrange("p b h -> p h b"),
                                 ALU.mult).then_inc(v_coef, 1)
                dve.wait_ge(v_coef, gi + 1)
                for pr in range(2):
                    dve.wait_ge(p_o, REP * gi + 2 * (pr + 1))
                    V_.tensor_tensor(otmp[:, pr, :].rearrange("p (c d) -> p c d", d=DV),
                                     pb[:, 6 + pr, 0:6 * DV].rearrange("p (c d) -> p c d", d=DV),
                                     coef[:, 2 * pr:2 * pr + 2, :].rearrange("p h b -> p (h b)").unsqueeze(2)
                                     .broadcast_to((P, 6, DV)), ALU.mult).then_inc(v_o, 1)
                for pr in range(2):
                    dve.wait_ge(v_o, 2 * gi + pr + 1)
                    o = (g * REP + 2 * pr) * DV
                    V_.tensor_reduce(attn[:, tt, o:o + 2 * DV].rearrange("p (h d) -> p h d", d=DV),
                                     otmp[:, pr, :].rearrange("p (h b d) -> p h d b", h=2, b=3),
                                     AX, ALU.add).then_inc(v_at, 1)
                dve.wait_ge(v_at, 2 * gi + 2)

            for n in range(NU + 2):
                gi = n // REP
                if n < NU:
                    if n % REP == 0:
                        cmp_logits(gi)
                    logits(n)
                    if n % REP == 1:
                        dve.wait_ge(a_cexp, gi + 1)
                        ch.add(V_.tensor_reduce(Z[:, gi % 2, :, 0], Sc[:, :, :], AX, ALU.add))
                if n % REP == 1 and n > REP:
                    combine(gi - 1)

            wide_bank = (0, 1, 6, 7)

            def row(v):
                if v:
                    dve.wait_ge(p_row, v)
                else:
                    dve.wait_ge(p_t, NU)
                V_.tensor_copy(wide, vec4[:, v, :].unsqueeze(2).broadcast_to((P, DT, P))).then_inc(v_row, 1)

            row(0)
            dve.wait_ge(p_o, NU)
            for j in range(DT):
                dve.wait_ge(ring_used, T_AO + j + 1)
                ch.link(V_.tensor_tensor(tmp[:, 0:SEQ], pb[:, wide_bank[j % 4], 0:SEQ], sig[:, j, :], ALU.mult))
                V_.tensor_tensor(y[:, j, :], tmp[:, 0:SEQ], upad[:, j, 0:SEQ], ALU.add).then_inc(v_m, 1)
                dve.wait_ge(v_m, j + 1)
            for v in range(1, 4):
                row(v)

            dve.wait_ge(a_row, 4)
            dve.wait_ge(a_std, 2)
            ch.link(V_.reciprocal(rstd[:, 2:4], std[:, 2:4]))
            for t in range(TT):
                ch.link(V_.scalar_tensor_tensor(out=tmp, in0=pb[:, 6 * t:6 * t + 2, :].rearrange("p a b -> p (a b)"),
                                                scalar=rstd[:, 2 + t:3 + t], in1=rows[:, 0, :],
                                                op0=ALU.mult, op1=ALU.mult))
                V_.tensor_tensor(x[:, t, :], x[:, t, :], tmp, ALU.add).then_inc(v_x2, 1)
                dve.wait_ge(v_x2, t + 1)
            dve.wait_ge(a_std, 3)
            ch.link(V_.reciprocal(rstd[:, 4:6], std[:, 4:6]))
            for t in range(TT):
                ch.link(V_.scalar_tensor_tensor(out=h2[:, t, :], in0=x[:, t, :], scalar=rstd[:, 4 + t:5 + t],
                                                in1=rows[:, 1, :], op0=ALU.mult, op1=ALU.mult))
                V_.tensor_tensor(h2[:, t, :], h2[:, t, :], rows[:, 2, :], ALU.add).then_inc(v_h2, 1)
            dve.wait_ge(v_h2, TT)

            def top16(n_rows, src, work, vals, idxs):
                for m in range(n_rows):
                    n = ch.add(V_.max(vals(m)[:, 0:8], src(m)))
                dve.wait_ge(v_chain, n)
                for m in range(n_rows):
                    ch.add(V_.max_index(idxs(m)[:, 0:8], vals(m)[:, 0:8], src(m)))
                    n = ch.add(V_.match_replace(work(m), vals(m)[:, 0:8], src(m), -3.0e38))
                dve.wait_ge(v_chain, n)
                for m in range(n_rows):
                    n = ch.add(V_.max(vals(m)[:, 8:16], work(m)))
                dve.wait_ge(v_chain, n)
                for m in range(n_rows):
                    n = ch.add(V_.max_index(idxs(m)[:, 8:16], vals(m)[:, 8:16], work(m)))
                dve.wait_ge(v_chain, n)

            def retrieve(k):
                t, q = divmod(k, CPT // SEG)
                dve.wait_ge(a_s, 4 * q + 4)
                top16(4, lambda m: ssb[:, t, 4 * q + m, :], lambda m: swork[:, m, :],
                      lambda m: v16[:, m, :], lambda m: i16[:, m, :])
                ch.add(V_.tensor_copy(i16f[:, :, :], i16[:, :, :]))
                pair = v16[:, :, :].rearrange("p (h c) k -> p h c k", c=2)
                for h in range(2):
                    n = ch.add(V_.tensor_tensor(cand[:, h, :].rearrange("p (a b) -> p a b", a=TOPK),
                                                pair[:, h, 0, :].unsqueeze(2).broadcast_to((P, TOPK, TOPK)),
                                                pair[:, h, 1, :].unsqueeze(1).broadcast_to((P, TOPK, TOPK)), ALU.add))
                dve.wait_ge(v_chain, n)
                top16(2, lambda h: cand[:, h, :], lambda h: cwork[:, h, :], lambda h: t16[:, h, :],
                      lambda h: p16[:, h * TOPK:(h + 1) * TOPK])
                for half, dst in ((0, e1), (1, e2)):
                    op, by = ((ALU.logical_shift_right, 4), (ALU.bitwise_and, TOPK - 1))[half]
                    ch.link(V_.tensor_single_scalar(pa[:, :], p16[:, :], by, op))
                    ch.link(V_.tensor_copy(paf[:, :], pa[:, :]))
                    ch.link(V_.tensor_tensor(oneh, iota16[:, :].unsqueeze(1).broadcast_to((P, EU, TOPK)),
                                             paf[:, :].unsqueeze(2).broadcast_to((P, EU, TOPK)), ALU.is_equal))
                    sub = i16f[:, :, :].rearrange("p (h c) k -> p h c k", c=2)
                    o4 = oneh.rearrange("p (h e) c -> p h e c", h=2)
                    ch.link(V_.tensor_tensor(o4, o4, sub[:, :, half, :].unsqueeze(2).broadcast_to((P, 2, TOPK, TOPK)),
                                             ALU.mult))
                    ch.link(V_.tensor_reduce(dst[:, :], oneh, AX, ALU.add))
                V_.scalar_tensor_tensor(out=idx[:, SEG * k:SEG * (k + 1), :].rearrange("p a b -> p (a b)"),
                                        in0=e1[:, :], scalar=float(NK), in1=e2[:, :],
                                        op0=ALU.mult, op1=ALU.add).then_inc(v_idx, 1)
                V_.tensor_tensor(weights(k), t16[:, :, :], t16[:, :, 0:1].broadcast_to((P, 2, TOPK)),
                                 ALU.subtract).then_inc(v_wsub, 1)
                dve.wait_ge(v_wsub, k + 1)

            def weights(k):
                return wgt[:, SEG * k:SEG * (k + 1), :].rearrange("p a b -> p (a b)").rearrange(
                    "p (h k) -> p h k", h=2)

            def softmax_sum(k):
                w = weights(k)
                dve.wait_ge(a_wexp, k + 1)
                ch.link(V_.tensor_reduce(wsum[:, :], w, AX, ALU.add))
                ch.link(V_.reciprocal(wsum[:, :], wsum[:, :]))
                ch.link(V_.tensor_tensor(w, w, wsum[:, :].unsqueeze(2).broadcast_to((P, 2, TOPK)), ALU.mult))

            dve.wait_ge(g_const, 4)
            retrieve(0)
            for k in range(UNITS):
                t = k * SEG // CPT
                if k + 1 < UNITS:
                    retrieve(k + 1)
                softmax_sum(k)
                with dve.Fori(0, SEG // 2) as i:
                    for b in range(2):
                        c = i * 2 + (SEG * k + b)
                        for s in range(CH):
                            dve.wait_ge(u_in[s], c * 16 + 16)
                            V_.tensor_tensor_reduce(out=urow[:, s, :], in0=urow[:, s, :], in1=h2[:, t, :], scale=1.0,
                                                    scalar=0.0, op0=ALU.mult, op1=ALU.add,
                                                    accum_out=dot[:, b, s:s + 1]).then_inc(u_free, 1)
                        dve.wait_ge(a_gl, c + 1)
                        V_.tensor_tensor(cf[:, b, :], gl[:, b, :], wgt[:, c, :], ALU.mult).then_inc(v_cf, 1)

            for t in range(TT):
                dve.wait_ge(a_std, 4 + t)
                ch.link(V_.reciprocal(rstd[:, 6 + t:7 + t], std[:, 6 + t:7 + t]))
                ch.link(V_.scalar_tensor_tensor(out=tmp, in0=pb[:, 4 + 2 * t:6 + 2 * t, :].rearrange("p a b -> p (a b)"),
                                                scalar=rstd[:, 6 + t:7 + t], in1=rows[:, 3, :],
                                                op0=ALU.mult, op1=ALU.mult))
                V_.tensor_tensor(x[:, t, :], x[:, t, :], tmp, ALU.add).then_inc(v_out, 1)
                dve.wait_ge(v_out, t + 1)


def bucket(dist):
    exact = BUCKETS // 2
    nf = np.maximum(dist, 1).astype(np.float32)
    big = exact + (np.log(nf / np.float32(exact)) / np.float32(np.log(MAXDIST / exact)) * np.float32(BUCKETS - exact)).astype(np.int32)
    b = np.where(dist < exact, dist, np.minimum(big, BUCKETS - 1))
    return np.where(dist < 0, BUCKETS, b)


def onehot(dist):
    return (bucket(dist)[None] == np.arange(BUCKETS + 1).reshape((-1,) + (1,) * dist.ndim)).astype(np.float32)


def column_tiles(w, width):
    n = w.shape[1] // width
    t = np.zeros((n, P, DT, P), w.dtype)
    t[:, :, :, 0:width] = w.reshape(DT, P, n, width).transpose(2, 1, 0, 3)
    return t.reshape(n, P, D)


def kernel(**inputs):
    import concourse.bacc as _bacc
    from concourse.bass_utils import run_bass_kernel_spmd as _run

    f = {n: np.ascontiguousarray(v) for n, v in inputs.items()}
    w_in = f["w_in"][0]
    sizes = [HEADS * DQK] + [GROUPS * DQK] * 3 + [GROUPS * DV] * 3 + [3 * HEADS, 2 * D, 2 * D]
    at = np.cumsum([0] + sizes)
    q, kc, ks, kw, vc, vs, vw, gn, glu, gm = (w_in[:, at[i]:at[i + 1]] for i in range(10))
    glu_t = column_tiles(glu, P)
    q_t, kc_t, ks_t, kw_t, vc_t = column_tiles(q, DQK), column_tiles(kc, DQK), column_tiles(ks, DQK), column_tiles(kw, DQK), column_tiles(vc, DV)
    vtile = np.zeros((DT, P, D), w_in.dtype)
    vtile[:, :, 0:256] = vs.reshape(DT, P, 256)
    vtile[:, :, 256:512] = vw.reshape(DT, P, 256)
    vtile[:, :, 512:560] = gn.reshape(DT, P, 48)
    stream = [glu_t.reshape(2, DT, P, D).transpose(1, 0, 2, 3).reshape(2 * DT, P, D), column_tiles(gm, P)]
    for g in range(GROUPS):
        stream += [q_t[g * REP:(g + 1) * REP], kc_t[g:g + 1], ks_t[g:g + 1], kw_t[g:g + 1], vc_t[g:g + 1]]
    stream += [vtile, column_tiles(f["w_conv_out"][0], P), column_tiles(f["w_attn_out"][0], P),
               f["w_out"][0].reshape(DT, P, D), column_tiles(f["peer_wq"][0], P)]

    def col(v):
        return v.reshape(-1, P).T

    cols = np.concatenate([col(f[n][0]) for n in ("b_ada", "g_pre_mix", "g_post_mix", "g_pre_ffn", "g_post_ffn",
                                                  "conv_b", "conv_ln_g", "conv_ln_b")]
                          + [f["conv_w"][0, :, 0, :].reshape(TAPS, DT, P).transpose(2, 1, 0).reshape(P, -1)], axis=1)
    j = np.arange(512)
    n = np.arange(NCMP)
    t = np.arange(SEQ)
    arrays = {
        "x": f["x"][0], "c": f["c"][0],
        "w_ada": f["w_ada"][0].T.reshape(48, P, D),
        "w_stream": np.concatenate(stream, axis=0),
        "cols": cols,
        "rel_table": f["rel_table"],
        "onehot_rev": onehot(SEQ - 1 - j),
        "onehot_cmp": onehot(t[None, :] - (n[:, None] * CMP_ST + CMP_L - 1)),
        "w1k": f["cmp_w1k"][0].reshape(CMP_L, DQK, HID).transpose(1, 0, 2),
        "w1v": f["cmp_w1v"][0].reshape(CMP_L, DV, HID).transpose(1, 0, 2),
        "w2k": f["cmp_w2k"][0].reshape(2, P, DQK).transpose(1, 0, 2),
        "w2v": f["cmp_w2v"][0].reshape(2, P, DV).transpose(1, 0, 2),
        "pos_k": f["cmp_pos_k"][0].T, "pos_v": f["cmp_pos_v"][0].T,
        "subkeys": f["peer_subkeys"][0].reshape(2 * PH, NK, P).transpose(2, 0, 1),
        "peer_u": f["peer_u"][0], "peer_v": f["peer_v"][0],
    }
    nc = _bacc.Bacc("TRN2", target_bir_lowering=False, num_devices=1)
    feed, aps = {}, {}
    for name, v in arrays.items():
        v = np.ascontiguousarray(v)
        feed[f"in_{name}"] = v
        aps[name] = nc.dram_tensor(f"in_{name}", v.shape, mybir.dt.from_np(v.dtype), kind="ExternalInput").ap()
    o = nc.dram_tensor("out_y", (SEQ, D), F32, kind="ExternalOutput").ap()
    build(nc, aps, o)
    r = _run(nc, [feed], core_ids=[0])
    return r.results[0]["out_y"].reshape(1, SEQ, D)
```

```python
from contextlib import ExitStack

import numpy as np

import concourse.bass as bass
from concourse import mybir

F32 = mybir.dt.float32
F32R = mybir.dt.float32r
I32 = mybir.dt.int32
U32 = mybir.dt.uint32
ALU = mybir.AluOpType
ACT = mybir.ActivationFunctionType
AX = mybir.AxisListType.X

P = 128
D = 1024
DT = D // P
SEQ = 256
TT = SEQ // P
HEADS = 16
GROUPS = 4
REP = HEADS // GROUPS
DQK = 96
DV = 64
CMP_L = 32
CMP_ST = 16
NCMP = SEQ // CMP_ST - 1
NBLK = SEQ // CMP_ST
NFAR = (P - CMP_L) // CMP_ST + 1
NCG = GROUPS * NBLK - 1
HID = 256
SCALE = DQK ** -0.5
BUCKETS = 32
MAXDIST = 128
TAPS = 31
PADT = TAPS - 1
PH = 8
NK = 128
TOPK = 16
NE = PH * TOPK
REV = 2 * SEQ - 1
EPS = 1e-6
NEG = -1e30

RING = 4
SPLITS = 2
ROUND = 8
CH = 8
CPT = NE // CH
HU = 1
SEG = HU * TOPK // CH
UNITS = TT * CPT // SEG
T_GLU, T_MERGE, T_GROUP, T_V, T_CO, T_AO, T_OUT, T_WQ, TILES = 0, 16, 32, 64, 72, 80, 88, 96, 112

EARLY = 4
T_PLAIN = T_WQ + EARLY
T_REV, T_W1 = 28, 64

M_CHUNK0 = 12

C_BADA, C_GPM, C_GOM, C_GPF, C_GOF, C_CB, C_LG, C_LB, C_CW = 0, 48, 56, 64, 72, 80, 88, 96, 104
NCOLS = C_CW + TAPS * DT
VHALF = (2 * GROUPS * DV + 3 * HEADS) // 2


class Chain:

    def __init__(self, eng, sem):
        self.eng, self.sem, self.n, self.k = eng, sem, 0, 0

    def add(self, ins):
        ins.then_inc(self.sem, 1)
        self.k += 1
        return self.n + self.k

    def link(self, ins):
        self.eng.wait_ge(self.sem, self.add(ins))

    def enter(self, i, per):
        self.base, self.per = self.n + self.k, per
        self.n, self.k = self.base + i * per, 0

    def leave(self, times):
        assert self.k == self.per, self.k
        self.n, self.k = self.base + self.per * times, 0


def build(nc, a, out):
    ctx = ExitStack()
    with ctx:
        def sb(name, shape, dt=F32):
            return ctx.enter_context(nc.sbuf_tensor(name, shape, dt))

        def sem(name):
            return ctx.enter_context(nc.semaphore(name))

        arena = sb("arena", [P, 16, D])
        ring = arena[:, 0:RING, :]
        front = arena[:, 4:8, :].rearrange("p a b -> p (a b)")
        upad_ = front[:, 0:DT * (PADT + SEQ)]
        vcf = front[:, DT * (PADT + SEQ):DT * (PADT + SEQ) + GROUPS * SEQ]
        vcT = vcf.rearrange("p (g t) -> p g t", g=GROUPS)
        adaw = arena[:, 8:16, :]
        adaw0 = arena[:, 0:8, :]
        w1 = arena[:, 8:16, :].rearrange("p a b -> p (a b)").rearrange("p (l n) -> p l n", n=HID)
        early = arena[:, 12:16, :]
        urow = arena[:, 8:16, :]

        x = sb("x", [P, TT, D])
        whi = sb("whi", [P, SPLITS, D], F32R)
        wlo = sb("wlo", [P, SPLITS, D], F32R)
        xhi = sb("xhi", [P, DT, SEQ], F32R)
        xlo = sb("xlo", [P, DT, SEQ], F32R)
        qT = sb("qT", [P, HEADS, SEQ])
        kT_ = sb("kT", [P, GROUPS * 3 * SEQ])
        kT = kT_[:, :].rearrange("p (g b t) -> p g b t", g=GROUPS, b=3)
        subk = kT_[:, 0:2 * PH * NK].rearrange("p (m k) -> p m k", k=NK)
        V = sb("V", [P, TT, 2 * GROUPS * DV])
        gates = sb("gates", [P, TT, 3, HEADS])
        upad = upad_.rearrange("p (j t) -> p j t", j=DT)
        y = sb("y", [P, DT, SEQ])
        yf = y[:, :, :].rearrange("p a b -> p (a b)")
        swork = yf[:, 0:512].rearrange("p (m k) -> p m k", k=NK)
        cand = yf[:, 512:1024].rearrange("p (h c) -> p h c", h=2)
        cwork = yf[:, 1024:1536].rearrange("p (h c) -> p h c", h=2)
        oneh = yf[:, 1536:1536 + 2 * TOPK * TOPK].rearrange("p (u e c) -> p u e c", u=2, c=TOPK)
        sig = sb("sig", [P, 2 * DT, SEQ])
        h2 = sig[:, 0:8, :].rearrange("p a b -> p (a b)").rearrange("p (t d) -> p t d", t=TT)
        tb = arena[:, 8:12, :].rearrange("p a b -> p (a b)").rearrange("p (h t) -> p h t", h=HEADS)
        qf = qT[:, :, :].rearrange("p a b -> p (a b)")
        rows = [qf[:, v * D:(v + 1) * D] for v in range(3)] + [V[:, :, :].rearrange("p a b -> p (a b)")]
        query = qT[:, 0:4, :]
        h2T = qT[:, 4:12, :]
        sc = sb("sc", [P, 4096])
        xs = sc[:, 0:2048].rearrange("p (t d) -> p t d", t=TT)
        ohr = sc[0:BUCKETS + 1, 2048:2560]
        cact = sc[:, 3072:4096]
        kcA, kcB, vcAB = (sc[:, 1024 * i:1024 * i + 1024] for i in range(3))
        attn = xs
        ssb = sc[:, :].rearrange("p (t m k) -> p t m k", t=TT, k=NK)
        S_ = sb("S", [P, 2 * 2 * SEQ])
        S = S_[:, :].rearrange("p (u b t) -> p u b t", u=2, b=2)
        revsb = S_[0:HEADS, 0:512]
        wide = S_[:, :].rearrange("p (j t) -> p j t", j=DT)
        junk = sc[:, 0:1024]
        PT = sb("PT", [P, 2, 512])
        tmp = PT[:, :, :].rearrange("p a b -> p (a b)")
        scaled = [tmp, sc[:, 1024:2048]]
        PcT = sb("PcT", [P, 512])
        htok = PcT[0:NCG, :].rearrange("p (u n) -> p u n", u=2)
        vrows = [arena[:, s, :] for s in range(4, 8)] + [S_[:, :], tmp, kT_[:, 2 * PH * NK:2 * PH * NK + D],
                                                         qf[:, 12 * SEQ:16 * SEQ]]
        cols = sb("cols", [P, NCOLS])
        mod = sb("mod", [P, 48])
        modst = sb("modst", [P, 8])
        A1 = sb("A1", [P, DT])
        vec4 = sb("vec4", [P, 4, DT])
        table = sb("table", [BUCKETS + 1, HEADS])
        posk = sb("posk", [P, CMP_L])
        posv = sb("posv", [P, CMP_ST])
        w2k = sb("w2k", [P, 2, DQK])
        w2v = sb("w2v", [P, 2, DV])
        hidk = sb("hidk", [P, 2, 64])
        hidv = sb("hidv", [P, 2, 64])
        kcT = sb("kcT", [DQK, NCG])
        vcv = sb("vcv", [NCMP, GROUPS * DV])
        tbc = sb("tbc", [P, TT, HEADS, NCMP])
        Sc = sb("Sc", [P, REP, NCMP])
        nmc = sb("nmc", [P, REP])
        nm = sb("nm", [P, 2, 2])
        Z = sb("Z", [P, 2, REP, 3])
        rz = sb("rz", [P, REP, 3])
        coef = sb("coef", [P, REP, 3])
        otmp = sb("otmp", [P, 2, 2 * 3 * DV])
        ident = sb("ident", [P, P])
        ones = sb("ones", [P, P])
        iota16 = sb("iota16", [P, TOPK])
        rowok = sb("rowok", [P, 1])
        eps = sb("eps", [P, 1])
        ss = sb("ss", [P, 8])
        std = sb("std", [P, 8])
        rstd = sb("rstd", [P, 8])
        stdc = sb("stdc", [P, SEQ])
        EU = SEG * CH
        v16 = sb("v16", [P, 2 * HU, TOPK])
        i16 = sb("i16", [P, 2 * HU, TOPK], U32)
        i16f = sb("i16f", [P, 2 * HU, TOPK])
        t16 = sb("t16", [P, HU, TOPK])
        p16 = sb("p16", [P, EU], U32)
        pa = sb("pa", [P, 2, TOPK], U32)
        paf = sb("paf", [P, 2, TOPK])
        e12 = sb("e12", [P, 2, TOPK])
        idx = sb("idx", [P, TT * CPT, CH], I32)
        wgt = sb("wgt", [P, TT * CPT, CH])
        wsum = sb("wsum", [P, HU])
        stage = sb("stage", [P, SEG, CH], I32)
        dot = sb("dot", [P, 2, CH])
        gl = sb("gl", [P, 2, CH])
        cf = sb("cf", [P, 2, CH])
        diag = sig[:, 8:16, :].rearrange("p a b -> p (a b)").rearrange("p (u s c) -> p u s c", u=2, s=CH)
        pb = ctx.enter_context(nc.psum_tensor("pb", [P, 8, 512], F32))

        s_x, s_c, s_cols, s_tbl, s_oh, s_small = (sem(n) for n in
                                                  ("x_in", "c_in", "cols_in", "table_in", "onehot_in", "small_in"))
        ring_in = [sem(f"ring_in{i}") for i in range(RING)]
        ada_in1 = [sem(f"ada_in1_{i}") for i in range(8)]
        ada_in = [sem(f"ada_in{i}") for i in range(8)]
        ada_more = [sem(f"ada_more{i}") for i in range(8)]
        rev_out, tb_in, w1_in, sub_in = sem("rev_out"), sem("tb_in"), sem("w1_in"), sem("sub_in")
        ring_used, ada_used = sem("ring_used"), sem("ada_used")
        w_hi, w_lo, x_hi, x_lo = sem("w_hi"), sem("w_lo"), sem("x_hi"), sem("x_lo")
        v_sc = sem("v_sc")
        early_in = [sem(f"early_in{i}") for i in range(EARLY)]
        g_const, g_rowok, g_chain = sem("g_const"), sem("g_rowok"), sem("g_chain")
        a_c, a_ss, a_std, a_rev = (sem(n) for n in ("a_c", "a_ss", "a_std", "a_rev"))
        a_evac, a_v, a_gk, a_hk, a_kc, a_gv, a_hv, a_vc, a_stdc, a_z = (
            sem(n) for n in ("a_evac", "a_v", "a_gk", "a_hk", "a_kc", "a_gv", "a_hv", "a_vc", "a_stdc", "a_z"))
        p_tk, p_tv, w1v_in = sem("p_tk"), sem("p_tv"), sem("w1v_in")
        a_cexp, a_exp, a_pt, a_pct, a_row, a_h2T, a_q, a_wexp = (
            sem(n) for n in ("a_cexp", "a_exp", "a_pt", "a_pct", "a_row", "a_h2T", "a_q", "a_wexp"))
        a_s = sem("a_s")
        a_turn, a_gl, a_dg = sem("a_turn"), sem("a_gl"), sem("a_dg")
        p_rev, p_xT, p_mean, p_var, p_hk, p_kc, p_hv, p_vc = (
            sem(n) for n in ("p_rev", "p_xT", "p_mean", "p_var", "p_hk", "p_kc",
                             "p_hv", "p_vc"))
        p_cs, p_s, p_t, p_ct, p_o, p_at, p_row, p_h2T, p_sc = (
            sem(n) for n in ("p_cs", "p_s", "p_t", "p_ct", "p_o", "p_at", "p_row", "p_h2T",
                             "p_sc"))
        v_chain, v_xs, v_hT, v_y, v_pos, v_sq, v_yn, v_zb = (
            sem(n) for n in ("v_chain", "v_xs", "v_hT", "v_y", "v_pos", "v_sq", "v_yn", "v_zb"))
        v_cs, v_csub, v_st, v_mx, v_coef, v_o, v_at, v_m, v_row, v_x2, v_h2 = (
            sem(n) for n in ("v_cs", "v_csub", "v_st", "v_mx", "v_coef", "v_o", "v_at", "v_m", "v_row", "v_x2",
                             "v_h2"))
        v_idx, v_wsub, v_cf, v_out = sem("v_idx"), sem("v_wsub"), sem("v_cf"), sem("v_out")
        u_in = [sem(f"u_in{i}") for i in range(CH)]
        v_in = [sem(f"v_in{i}") for i in range(CH)]
        u_free, v_free, g_staged, g_turn = sem("u_free"), sem("v_free"), sem("g_staged"), sem("g_turn")
        o_done = sem("o_done")

        rev_dram = nc.dram_tensor("rev_scratch", (HEADS, P, REV), F32).ap()

        def group_of(gi):
            return divmod(gi, GROUPS)

        def unit_keys(n):
            tt, g = group_of(n // REP)
            return tt, g * REP + n % REP, g, n % REP, P * (tt + 1)

        NU = TT * HEADS

        block = ctx.enter_context(nc.Block())

        @block.sync
        def _(sp):
            sp.dma_start(cact, a["c"].partition_broadcast(P)).then_inc(s_c, 16)
            sp.dma_start(cols[:, :], a["cols"]).then_inc(s_cols, 16)
            sp.dma_start(x[:, :, :], a["x"].rearrange("(t p) d -> p t d", p=P)).then_inc(s_x, 16)
            for s in range(8):
                sp.dma_start(adaw0[:, s, :], a["w_ada"][s]).then_inc(ada_in[s], 16)
            for s in range(8):
                sp.dma_start(adaw[:, s, :], a["w_ada"][8 + s]).then_inc(ada_in1[s], 16)
            sp.dma_start(table[0:BUCKETS, :], a["rel_table"]).then_inc(s_tbl, 16)
            for s in range(RING):
                sp.wait_ge(ada_used, s + 1)
                sp.dma_start(ring[:, s, :], a["w_stream"][s]).then_inc(ring_in[s], 16)
            sp.dma_start(ohr, a["onehot_rev"]).then_inc(s_oh, 16)
            sp.dma_start(posk[:, :], a["pos_k"]).then_inc(s_small, 16)
            sp.dma_start(posv[:, :], a["pos_v"]).then_inc(s_small, 16)
            sp.dma_start(w2k[:, :, :], a["w2k"]).then_inc(s_small, 16)
            sp.dma_start(w2v[:, :, :], a["w2v"]).then_inc(s_small, 16)

            def load(r, s):
                sp.wait_ge(w_lo, (r - 1) * RING + s + 1)
                sp.dma_start(ring[:, s, :], a["w_stream"][r * RING + s]).then_inc(ring_in[s], 16)

            def load_rounds(first, last):
                with sp.Fori(first, last) as r:
                    for s in range(RING):
                        load(r, s)

            load_rounds(1, T_REV // RING)
            sp.wait_ge(a_rev, 1)
            for i in range(8):
                load(T_REV // RING + i // RING, i % RING)
                hs = slice(2 * i, 2 * i + 2)
                sp.dma_start(rev_dram[hs], revsb[hs, 0:REV].unsqueeze(1).broadcast_to((2, P, REV))
                             ).then_inc(rev_out, 16)
            load_rounds(T_REV // RING + 2, T_W1 // RING)
            for tile in range(T_W1, T_W1 + 12):
                load(tile // RING, tile % RING)
                i = tile - T_W1 - 2
                if i == 0:
                    sp.wait_ge(ada_used, 48)
                if 0 <= i < 8:
                    ls = slice(i * CMP_L // 8, (i + 1) * CMP_L // 8)
                    sp.dma_start(w1[:, ls, :], a["w1k"][:, ls, :]).then_inc(w1_in, 16)
            load_rounds(T_W1 // RING + 3, T_AO // RING + 1)
            sp.wait_ge(p_hk, 2)
            for m in range(EARLY):
                sp.dma_start(early[:, m, :], a["w_stream"][T_WQ + m]).then_inc(early_in[m], 16)
            load_rounds(T_AO // RING + 1, T_WQ // RING)
            for s in range(RING):
                sp.wait_ge(w_lo, T_WQ - RING + s + 1)
                sp.dma_start(ring[:, s, :], a["w_stream"][T_PLAIN + s]).then_inc(ring_in[s], 16)
            with sp.Fori(T_PLAIN // RING + 1, TILES // RING) as r:
                for s in range(RING):
                    sp.wait_ge(ring_used, (r - 1) * RING + s + 1)
                    sp.dma_start(ring[:, s, :], a["w_stream"][r * RING + s]).then_inc(ring_in[s], 16)
            for t in range(TT):
                sp.wait_ge(v_out, t + 1)
                sp.dma_start(out[t * P:(t + 1) * P, :], x[:, t, :]).then_inc(o_done, 16)
            sp.wait_ge(o_done, 16 * TT)

        @block.gpsimd
        def _(g):
            g_ch = Chain(g, g_chain)
            g_ch.link(nc.gpsimd.memset(table[BUCKETS:BUCKETS + 1, :], NEG))
            nc.gpsimd.memset(eps[:, :], EPS).then_inc(g_const, 1)
            nc.gpsimd.memset(ones[:, :], 1.0 / D).then_inc(g_const, 1)
            g_ch.link(nc.gpsimd.memset(ident[:, :], 0.0))
            nc.gpsimd.affine_select(out=ident[:, :], in_=ident[:, :], compare_op=ALU.not_equal, fill=1.0, base=0,
                                    pattern=[[-1, P]], channel_multiplier=1).then_inc(g_const, 1)
            nc.gpsimd.iota(iota16[:, :], pattern=[[1, TOPK]], base=0, channel_multiplier=0,
                           allow_small_or_imprecise_dtypes=True).then_inc(g_const, 1)
            nc.gpsimd.memset(tbc[:, 0, :, NFAR:NCMP], NEG).then_inc(g_rowok, 1)
            g_ch.link(nc.gpsimd.memset(rowok[:, :], 1.0))
            nc.gpsimd.affine_select(out=rowok[:, :], in_=rowok[:, :], compare_op=ALU.is_ge, fill=0.0,
                                    base=-(CMP_L - 1), pattern=[[0, 1]], channel_multiplier=1).then_inc(g_rowok, 1)

            def split_lo(slot, tile, n=D, src=ring):
                g.wait_ge(w_hi, tile + 1)
                g.sem_inc(g_turn, 1)
                nc.gpsimd.tensor_tensor(wlo[:, slot % SPLITS, 0:n], src[:, slot % RING, 0:n],
                                        whi[:, slot % SPLITS, 0:n].bitcast(F32), ALU.subtract).then_inc(w_lo, 1)

            def split_rounds(first, last, n=D):
                with g.Fori(first, last) as r:
                    for s in range(ROUND):
                        split_lo(s, r * ROUND + s, n)

            split_rounds(0, T_V // ROUND)
            split_rounds(T_V // ROUND, T_CO // ROUND, 2 * VHALF)
            for s in range(SPLITS):
                split_lo(s, T_CO + s)
            g.wait_ge(p_hk, 1)
            g.dma_start(w1[:, 0:CMP_ST, :], a["w1v"]).then_inc(w1v_in, 16)
            g.wait_ge(rev_out, 128)
            g.wait_ge(p_hv, 1)
            g.dma_start(tb, bass.AP(rev_dram.tensor, P - 1, [[REV - 1, P], [P * REV, HEADS], [1, SEQ]])
                        ).then_inc(tb_in, 16)
            for s in range(SPLITS, ROUND):
                split_lo(s, T_CO + s)
            for s in range(SPLITS):
                split_lo(s, T_AO + s)
            g.wait_ge(p_s, NU)
            g.dma_start(subk, a["subkeys"]).then_inc(sub_in, 16)
            for s in range(SPLITS, ROUND):
                split_lo(s, T_AO + s)
            split_rounds(T_OUT // ROUND, T_WQ // ROUND)
            for m in range(EARLY):
                split_lo(m, T_WQ + m, src=early)
            g.wait_ge(v_st, NU)
            g.wait_ge(v_m, DT)
            with g.Fori(0, UNITS) as k:
                g.wait_ge(v_idx, k + 1)
                g.sem_inc(g_turn, 1)
                for b in range(SEG):
                    c = k * SEG + b
                    nc.gpsimd.tensor_copy(stage[:, b, :], idx[:, c, :]).then_inc(g_staged, 1)
                    g.wait_ge(g_staged, c + 1)
                    g.sem_inc(g_turn, 1)
                    for s in range(CH):
                        g.wait_ge(u_free, c * CH + (s + 1))
                        g.sem_inc(g_turn, 1)
                        nc.gpsimd.indirect_dma_start(
                            out=urow[:, s, :], out_offset=None, in_=a["peer_u"],
                            in_offset=bass.IndirectOffsetOnAxis(ap=stage[:, b, s:s + 1], axis=0),
                        ).then_inc(u_in[s], 16)
                    for s in range(CH):
                        g.wait_ge(v_free, c * CH + (s + 1))
                        g.sem_inc(g_turn, 1)
                        nc.gpsimd.indirect_dma_start(
                            out=vrows[s], out_offset=None, in_=a["peer_v"],
                            in_offset=bass.IndirectOffsetOnAxis(ap=stage[:, b, s:s + 1], axis=0),
                        ).then_inc(v_in[s], 16)

        @block.tensor
        def _(pe):
            mm = nc.tensor.matmul
            pe.sem_inc(v_free, CH)

            pe.wait_ge(g_const, 4)
            pe.wait_ge(v_xs, TT)
            for j in range(DT):
                for t in range(TT):
                    o = (j % 2) * SEQ + t * P
                    last = nc.tensor.transpose(pb[:, 4 + j // 2, o:o + P], xs[:, t, j * P:(j + 1) * P], ident[:, :])
                if j % 2:
                    last.then_inc(p_xT, 1)

            def column_tile(bank, slot, tile, ready=None):
                w = slot % SPLITS
                pe.wait_ge(w_hi, tile + 1)
                for k in range(DT):
                    if ready is not None:
                        pe.wait_ge(x_hi, ready + k + 1)
                    mm(pb[:, bank, 0:SEQ], whi[:, w, k * P:(k + 1) * P], xhi[:, k, :], start=(k == 0), stop=False)
                for k in range(DT):
                    if ready is not None:
                        pe.wait_ge(x_lo, ready + k + 1)
                    mm(pb[:, bank, 0:SEQ], whi[:, w, k * P:(k + 1) * P], xlo[:, k, :], start=False, stop=False)
                pe.wait_ge(w_lo, tile + 1)
                for k in range(DT):
                    last = mm(pb[:, bank, 0:SEQ], wlo[:, w, k * P:(k + 1) * P], xhi[:, k, :],
                              start=False, stop=(k == DT - 1))
                last.then_inc(ring_used, 1)

            def column_round(r, first=False):
                for s in range(ROUND):
                    if not first or s >= 4:
                        pe.wait_ge(a_evac, r * ROUND + (s - 3))
                    column_tile(s % 4, s, r * ROUND + s, ready=0 if first and s == 0 else None)

            column_round(0, first=True)
            pe.wait_ge(s_tbl, 16)
            pe.wait_ge(s_oh, 16)
            mm(pb[0:HEADS, 4, :], table[:, :], ohr, start=True, stop=True).then_inc(p_rev, 1)
            column_round(1)
            with pe.Fori(T_MERGE // ROUND, T_V // ROUND) as r:
                column_round(r)

            def token_tile(k, tile, banks, width):
                w = k % SPLITS
                pe.wait_ge(w_hi, tile + 1)
                for xp, wp in ((xhi, whi), (xlo, whi), (xhi, wlo)):
                    if wp is wlo:
                        pe.wait_ge(w_lo, tile + 1)
                    for t in range(TT):
                        for hf in range(2):
                            last = mm(pb[:, banks[t] + hf, 0:width], xp[:, k, t * P:(t + 1) * P],
                                      wp[:, w, hf * width:(hf + 1) * width],
                                      start=(k == 0 and xp is xhi and wp is whi), stop=(k == DT - 1 and wp is wlo))
                last.then_inc(ring_used, 1)

            pe.wait_ge(a_evac, T_V)
            for k in range(DT):
                token_tile(k, T_V + k, (0, 2), VHALF)

            pe.wait_ge(v_y, 2)
            for k in range(DT):
                last = mm(pb[:, 4, 0:SEQ], ones[:, :], y[:, k, :], start=(k == 0), stop=(k == DT - 1))
            last.then_inc(p_mean, 1)

            pe.wait_ge(w1_in, 128)
            pe.wait_ge(v_pos, 4)
            for l in range(CMP_L):
                src = kcA if l < CMP_ST else kcB
                last = mm(pb[0:NCG, 5, 0:HID], src[:, l:l + (NCG - 1) * CMP_ST + 1:CMP_ST], w1[:, l, :],
                          start=(l == 0), stop=(l == CMP_L - 1))
                if l == CMP_ST - 1:
                    last.then_inc(p_hk, 1)
            last.then_inc(p_hk, 1)
            pe.wait_ge(v_sq, 1)
            for k in range(DT):
                last = mm(pb[:, 4, SEQ:2 * SEQ], ones[:, :], upad[:, k, 0:SEQ], start=(k == 0), stop=(k == DT - 1))
            last.then_inc(p_var, 1)

            def hidden_transposed(u, bank):
                for hh in range(2):
                    last = nc.tensor.transpose(pb[:, bank, hh * 64:hh * 64 + NCG], htok[:, u, hh * P:(hh + 1) * P],
                                               ident[0:NCG, 0:NCG])
                return last

            pe.wait_ge(a_gk, 1)
            hidden_transposed(0, 6).then_inc(p_tk, 1)
            pe.wait_ge(w1v_in, 16)
            for l in range(CMP_ST):
                last = mm(pb[0:NCG, 7, 0:HID], vcAB[:, l:l + (NCG - 1) * CMP_ST + 1:CMP_ST], w1[:, l, :],
                          start=(l == 0), stop=(l == CMP_ST - 1))
            last.then_inc(p_hv, 1)
            pe.wait_ge(a_hk, 1)
            pe.wait_ge(s_small, 64)
            for k in range(2):
                last = mm(pb[0:DQK, 6, 256:256 + NCG], w2k[:, k, :], hidk[:, k, 0:NCG], start=(k == 0), stop=(k == 1))
            last.then_inc(p_kc, 1)

            pe.wait_ge(a_v, 6)
            for j in range(DT):
                if j >= 4:
                    pe.wait_ge(v_zb, j - 3)
                column_tile(j % 4, j, T_CO + j, ready=None if j else DT)
            pe.wait_ge(a_gv, 1)
            hidden_transposed(1, 5).then_inc(p_tv, 1)
            pe.wait_ge(a_hv, 1)
            for g in range(GROUPS):
                for k in range(2):
                    last = mm(pb[0:NCMP, 5, 256 + g * DV:256 + (g + 1) * DV], hidv[:, k, g * NBLK:g * NBLK + NCMP],
                              w2v[:, k, :], start=(k == 0), stop=(k == 1))
            last.then_inc(p_vc, 1)

            pe.wait_ge(a_kc, 1)
            pe.wait_ge(a_vc, 1)
            pe.wait_ge(v_zb, DT)
            pe.wait_ge(a_stdc, 1)

            def cmp_scores(gi):
                tt, g = group_of(gi)
                if gi >= 1:
                    pe.wait_ge(v_cs, gi)
                for hh in range(REP):
                    last = mm(pb[:, 4, hh * NCMP:(hh + 1) * NCMP], qT[0:DQK, g * REP + hh, tt * P:(tt + 1) * P],
                              kcT[:, g * NBLK:g * NBLK + NCMP], start=True, stop=True)
                last.then_inc(p_cs, 1)

            def cmp_transposes(gi):
                pe.wait_ge(a_cexp, gi + 1)
                if gi >= 1:
                    pe.wait_ge(a_pct, gi)
                for hh in range(REP):
                    last = nc.tensor.transpose(pb[0:NCMP, 5, hh * P:(hh + 1) * P], Sc[:, hh, :], ident[:, :])
                last.then_inc(p_ct, 1)

            def scores(n):
                tt, h, g, hh, keys = unit_keys(n)
                if n >= 2:
                    pe.wait_ge(v_st, n - 1)
                mm(pb[:, n % 2, :], qT[:, h, tt * P:(tt + 1) * P], kT[:, g, 1:3, :],
                   start=True, stop=True).then_inc(p_s, 1)

            def transposes(n):
                tt, h, g, hh, keys = unit_keys(n)
                pe.wait_ge(a_exp, 2 * (n + 1))
                if n >= 2:
                    pe.wait_ge(a_pt, n - 1)
                for b in range(2):
                    for kb in range(tt + 1):
                        o = (b * (tt + 1) + kb) * P
                        last = nc.tensor.transpose(pb[:, 2 + n % 2, o:o + P], S[:, n % 2, b, kb * P:(kb + 1) * P],
                                                   ident[:, :])
                last.then_inc(p_t, 1)

            def values(n):
                tt, h, g, hh, keys = unit_keys(n)
                gi = n // REP
                pe.wait_ge(a_pt, n + 1)
                pe.wait_ge(a_pct, gi + 1)
                if gi >= 1 and hh % 2 == 0:
                    pe.wait_ge(v_o, 2 * (gi - 1) + hh // 2 + 1)
                o = (hh % 2) * 3 * DV
                bank = 6 + hh // 2
                mm(pb[:, bank, o:o + DV], PcT[0:NCMP, hh * P:(hh + 1) * P], vcv[:, g * DV:(g + 1) * DV],
                   start=True, stop=True)
                for b in range(2):
                    for kb in range(tt + 1):
                        last = mm(pb[:, bank, o + (1 + b) * DV:o + (2 + b) * DV],
                                  PT[:, n % 2, (b * (tt + 1) + kb) * P:(b * (tt + 1) + kb + 1) * P],
                                  V[:, kb, (b * GROUPS + g) * DV:(b * GROUPS + g + 1) * DV],
                                  start=(kb == 0), stop=(kb == tt))
                last.then_inc(p_o, 1)

            for n in range(NU + 2):
                if n < NU:
                    if n % REP == 0:
                        cmp_scores(n // REP)
                    scores(n)
                    if n % REP == 1:
                        cmp_transposes(n // REP)
                if 1 <= n <= NU:
                    transposes(n - 1)
                if n >= 2:
                    values(n - 2)

            pe.wait_ge(v_at, 2 * GROUPS * TT)
            pe.wait_ge(a_pt, NU)
            pe.wait_ge(a_pct, GROUPS * TT)
            for t in range(TT):
                for jj in range(2):
                    for j in range(4):
                        last = nc.tensor.transpose(pb[:, 2 + 2 * t + jj, j * P:(j + 1) * P],
                                                   attn[:, t, (4 * jj + j) * P:(4 * jj + j + 1) * P], ident[:, :])
                    last.then_inc(p_at, 1)

            wide_bank = (0, 1, 6, 7)
            pe.wait_ge(x_lo, 2 * DT + 4)
            pe.wait_ge(v_o, 2 * GROUPS * TT)
            for j in range(DT):
                if j >= 4:
                    pe.wait_ge(v_m, j - 3)
                column_tile(wide_bank[j % 4], j, T_AO + j)

            def row(v):
                pe.wait_ge(v_row, v + 1)
                if v >= 2:
                    pe.wait_ge(a_row, v - 1)
                for j in range(DT):
                    last = mm(pb[:, 2 + 2 * (v % 2) + j // 4, (j % 4) * P:(j % 4 + 1) * P], wide[:, j, :], ident[:, :],
                              start=True, stop=True)
                last.then_inc(p_row, 1)

            for v in range(2):
                row(v)

            for k in range(DT):
                pe.wait_ge(x_lo, 2 * DT + 4 + k + 1)
                token_tile(k, T_OUT + k, (0, 6), 512)
            for v in range(2, 4):
                row(v)

            pe.wait_ge(v_h2, TT)
            pe.wait_ge(a_row, 4)
            for j in range(DT):
                for t in range(TT):
                    o = (j % 2) * SEQ + t * P
                    last = nc.tensor.transpose(pb[:, 2 + j // 2, o:o + P], h2[:, t, j * P:(j + 1) * P], ident[:, :])
                if j % 2:
                    last.then_inc(p_h2T, 1)
            def expert_chunk(t, b, c, first=False):
                for s in range(CH):
                    pe.wait_ge(v_in[s], c * 16 + 16)
                    pe.wait_ge(a_dg, c * CH + (s + 1))
                    for hf in range(2):
                        last = mm(pb[:, 4 + 2 * t + hf, :], diag[:, b, s, :], vrows[s][:, hf * 512:(hf + 1) * 512],
                                  start=(first and s == 0), stop=False, skip_group_check=True)
                    last.then_inc(v_free, 1)

            pe.wait_ge(x_lo, 3 * DT + 8)
            pe.wait_ge(sub_in, 16)
            def subkey_scores(m):
                pe.wait_ge(a_q, m + 1)
                if m >= 2:
                    pe.wait_ge(a_s, m - 1)
                for t in range(TT):
                    last = mm(pb[:, 2 + m % 2, t * NK:(t + 1) * NK], query[:, m % 4, t * P:(t + 1) * P],
                              subk[:, m, :], start=True, stop=True)
                last.then_inc(p_sc, 1)

            for m in range(2 * PH + 1):
                if m == 2:
                    subkey_scores(m - 1)
                if m < 2 * PH:
                    if m >= 2:
                        pe.wait_ge(a_q, m - 1)
                    if T_WQ + m < T_PLAIN:
                        column_tile(m % 2, m, T_WQ + m)
                    else:
                        pe.wait_ge(ring_in[m % RING], 16 * ((T_WQ + m - EARLY) // RING + 1))
                        if T_WQ + m == T_PLAIN:
                            pe.wait_ge(a_h2T, 4)
                        for k in range(DT):
                            last = mm(pb[:, m % 2, 0:SEQ], ring[:, m % RING, k * P:(k + 1) * P], h2T[:, k, :],
                                      start=(k == 0), stop=(k == DT - 1))
                        last.then_inc(ring_used, 1)
                if m >= 1 and m != 2:
                    subkey_scores(m - 1)
                if m == M_CHUNK0:
                    expert_chunk(0, 0, 0, first=True)

            for t in range(TT):
                for b in range(2):
                    if t or b:
                        expert_chunk(t, b, CPT * t + b, first=(b == 0))
                with pe.Fori(1, CPT // 2) as i:
                    for b in range(2):
                        expert_chunk(t, b, i * 2 + (CPT * t + b))

        @block.scalar
        def _(act):
            fn = nc.scalar.activation

            def turn():
                act.sem_inc(a_turn, 1)

            act.wait_ge(s_c, 16)
            fn(cact, cact, ACT.Silu).then_inc(a_c, 1)
            act.wait_ge(s_x, 16)
            for t in range(TT):
                fn(xs[:, t, :], x[:, t, :], ACT.Square, accum_out=ss[:, t:t + 1]).then_inc(a_ss, 1)
            act.wait_ge(a_ss, TT)
            act.wait_ge(g_const, 4)
            fn(std[:, 0:TT], ss[:, 0:TT], ACT.Sqrt, scale=1.0 / D, bias=eps[:, :]).then_inc(a_std, 1)

            def evac(tile, s, dst, func):
                act.wait_ge(ring_used, tile + (s + 1))
                turn()
                fn(dst, pb[:, s % 4, 0:SEQ], func).then_inc(a_evac, 1)

            def split_hi(slot, tile, n=D):
                if isinstance(tile, int) and tile >= T_WQ:
                    src = early
                    act.wait_ge(early_in[slot % RING], 16)
                else:
                    src = ring
                    act.wait_ge(ring_in[slot % RING], tile_landed(slot, tile))
                if not isinstance(tile, int) or tile >= SPLITS:
                    act.wait_ge(ring_used, tile + (1 - SPLITS))
                turn()
                fn(whi[:, slot % SPLITS, 0:n], src[:, slot % RING, 0:n], ACT.Copy).then_inc(w_hi, 1)

            def tile_landed(slot, tile):
                return (tile - slot % RING) * (16 // RING) + 16

            split_hi(0, 0)
            split_hi(1, 1)
            for j in range(DT):
                act.wait_ge(v_hT, j + 1)
                fn(xhi[:, j, :], y[:, j, :], ACT.Copy).then_inc(x_hi, 1)

            def ada_load(i, s):
                act.wait_ge(ada_used, i * 8 + (s - 7))
                turn()
                act.dma_start(adaw[:, s, :], a["w_ada"][i * 8 + s]).then_inc(ada_more[s], 16)

            with act.Fori(0, T_MERGE // ROUND) as r:
                for s in range(ROUND):
                    split_hi(s + SPLITS, r * ROUND + (s + SPLITS))
                    if s % 2 == 0:
                        evac(r * ROUND, s, upad[:, r * 4 + s // 2, PADT:PADT + SEQ], ACT.Copy)
                    else:
                        evac(r * ROUND, s, y[:, r * 4 + s // 2, :], ACT.Sigmoid)
                    ada_load(r + 2, s)
            act.wait_ge(p_rev, 1)
            fn(revsb, pb[0:HEADS, 4, :], ACT.Copy).then_inc(a_rev, 1)
            with act.Fori(0, (T_GROUP - T_MERGE) // ROUND) as r:
                for s in range(ROUND):
                    split_hi(s + SPLITS, r * ROUND + (s + SPLITS + T_MERGE))
                    evac(r * ROUND + T_MERGE, s, sig[:, r * ROUND + s, :], ACT.Sigmoid)
            for g in range(GROUPS):
                for s in range(ROUND):
                    split_hi(s + SPLITS, g * ROUND + (s + SPLITS + T_GROUP))
                    if s < REP:
                        evac(g * ROUND + T_GROUP, s, qT[:, g * REP + s, :], ACT.Copy)
                    elif s < ROUND - 1:
                        evac(g * ROUND + T_GROUP, s, kT[:, g, s - REP, :], ACT.Copy)
                    else:
                        evac(g * ROUND + T_GROUP, s, vcT[:, g, :], ACT.Copy)
                    i = g * ROUND + s
                    if i < 8:
                        ada_load(4, i)
                    elif 20 <= i < 28:
                        ada_load(5, i - 20)
            for s in range(ROUND):
                split_hi(s + SPLITS, T_V + s + SPLITS, 2 * VHALF if s + SPLITS < ROUND else D)
            act.wait_ge(ring_used, T_CO)
            for t in range(TT):
                fn(V[:, t, 0:VHALF], pb[:, 2 * t, 0:VHALF], ACT.Copy).then_inc(a_v, 1)
                fn(V[:, t, VHALF:512], pb[:, 2 * t + 1, 0:512 - VHALF], ACT.Copy).then_inc(a_v, 1)
            for t in range(TT):
                fn(gates[:, t, :, :], pb[:, 2 * t + 1, 512 - VHALF:VHALF], ACT.Sigmoid).then_inc(a_v, 1)
            act.wait_ge(p_hk, 2)
            fn(htok[:, 0, :], pb[0:NCG, 5, 0:HID], ACT.Gelu_apprx_tanh).then_inc(a_gk, 1)
            act.wait_ge(p_var, 1)
            fn(stdc[:, :], pb[:, 4, SEQ:2 * SEQ], ACT.Sqrt, bias=eps[:, :]).then_inc(a_stdc, 1)
            act.wait_ge(p_tk, 1)
            fn(hidk[:, :, 0:NCG], pb[:, 6, 0:P].rearrange("p (a b) -> p a b", a=2)[:, :, 0:NCG],
               ACT.Copy).then_inc(a_hk, 1)
            act.wait_ge(v_yn, 1)
            for j in range(DT):
                fn(y[:, j, :], y[:, j, :], ACT.Silu, scale=cols[:, C_LG + j:C_LG + j + 1],
                   bias=cols[:, C_LB + j:C_LB + j + 1]).then_inc(a_z, 1)
                act.wait_ge(a_z, j + 1)
                fn(xhi[:, j, :], y[:, j, :], ACT.Copy).then_inc(x_hi, 1)
            act.wait_ge(p_kc, 1)
            fn(kcT[:, :], pb[0:DQK, 6, 256:256 + NCG], ACT.Copy).then_inc(a_kc, 1)
            act.wait_ge(p_hv, 1)
            fn(htok[:, 1, :], pb[0:NCG, 7, 0:HID], ACT.Gelu_apprx_tanh).then_inc(a_gv, 1)
            for s in range(ROUND):
                split_hi(s + SPLITS, T_CO + s + SPLITS)
            act.wait_ge(p_tv, 1)
            fn(hidv[:, :, 0:NCG], pb[:, 5, 0:P].rearrange("p (a b) -> p a b", a=2)[:, :, 0:NCG],
               ACT.Copy).then_inc(a_hv, 1)
            act.wait_ge(p_vc, 1)
            fn(vcv[:, :], pb[0:NCMP, 5, 256:256 + GROUPS * DV], ACT.Copy).then_inc(a_vc, 1)

            def exps(n):
                tt, h, g, hh, keys = unit_keys(n)
                gi = n // REP
                act.wait_ge(v_mx, n + 1)
                if gi >= 2 and hh == 0:
                    act.wait_ge(v_coef, 2 * (gi - 1))
                for b in range(2):
                    fn(S[:, n % 2, b, 0:keys], S[:, n % 2, b, 0:keys], ACT.Exp, bias=nm[:, n % 2, b:b + 1],
                       accum_out=Z[:, gi % 2, hh, 1 + b:2 + b]).then_inc(a_exp, 1)

            for n in range(NU + 1):
                gi = n // REP
                if n < NU:
                    if n % REP == 0:
                        act.wait_ge(v_csub, gi + 1)
                        fn(Sc[:, :, :], Sc[:, :, :], ACT.Exp).then_inc(a_cexp, 1)
                    exps(n)
                if n >= 1:
                    u = n - 1
                    tt = group_of(u // REP)[0]
                    act.wait_ge(p_t, u + 1)
                    if u >= 2:
                        act.wait_ge(p_o, u - 1)
                    fn(PT[:, u % 2, 0:2 * P * (tt + 1)], pb[:, 2 + u % 2, 0:2 * P * (tt + 1)],
                       ACT.Copy).then_inc(a_pt, 1)
                if n < NU and n % REP == 1:
                    act.wait_ge(p_ct, gi + 1)
                    if gi >= 1:
                        act.wait_ge(p_o, gi * REP)
                    fn(PcT[0:NCMP, :], pb[0:NCMP, 5, :], ACT.Copy).then_inc(a_pct, 1)
            for t in range(TT):
                for jj in range(2):
                    act.wait_ge(p_at, 2 * t + jj + 1)
                    fn(xhi[:, 4 * jj:4 * jj + 4, t * P:(t + 1) * P],
                       pb[:, 2 + 2 * t + jj, :].rearrange("p (j t) -> p j t", j=4), ACT.Copy).then_inc(x_hi, 1)
            for s in range(ROUND):
                split_hi(s + SPLITS, T_AO + s + SPLITS)
            act.wait_ge(ring_used, T_OUT)
            for j in range(DT):
                act.wait_ge(v_m, j + 1)
                fn(xhi[:, j, :], y[:, j, :], ACT.Copy).then_inc(x_hi, 1)

            def row(v):
                act.wait_ge(p_row, v + 1)
                fn(rows[v], pb[:, 2 + 2 * (v % 2):4 + 2 * (v % 2), :].rearrange("p a b -> p (a b)"),
                   ACT.Copy).then_inc(a_row, 1)

            for v in range(2):
                row(v)
            for s in range(ROUND):
                split_hi(s + SPLITS, T_OUT + s + SPLITS)
            act.wait_ge(ring_used, T_WQ)
            act.wait_ge(p_row, 2)
            for t in range(TT):
                if t:
                    act.wait_ge(v_sc, 1)
                fn(junk, pb[:, 6 * t:6 * t + 2, :].rearrange("p a b -> p (a b)"), ACT.Square,
                   accum_out=ss[:, 2 + t:3 + t]).then_inc(a_ss, 1)
                act.wait_ge(a_ss, TT + t + 1)
            fn(std[:, 2:4], ss[:, 2:4], ACT.Sqrt, scale=1.0 / D, bias=eps[:, :]).then_inc(a_std, 1)
            for v in range(2, 4):
                row(v)
            for t in range(TT):
                act.wait_ge(v_x2, t + 1)
                fn(junk, x[:, t, :], ACT.Square, accum_out=ss[:, 4 + t:5 + t]).then_inc(a_ss, 1)
                act.wait_ge(a_ss, 2 * TT + t + 1)
            fn(std[:, 4:6], ss[:, 4:6], ACT.Sqrt, scale=1.0 / D, bias=eps[:, :]).then_inc(a_std, 1)
            for b in range(4):
                act.wait_ge(p_h2T, b + 1)
                fn(xhi[:, 2 * b:2 * b + 2, :], pb[:, 2 + b, :].rearrange("p (a t) -> p a t", a=2),
                   ACT.Copy).then_inc(x_hi, 1)
            for b in range(4):
                act.wait_ge(x_lo, 3 * DT + 4 + b + 1)
                fn(h2T[:, 2 * b:2 * b + 2, :], pb[:, 2 + b, :].rearrange("p (a t) -> p a t", a=2),
                   ACT.Copy).then_inc(a_h2T, 1)
            def unit_exp(k):
                act.wait_ge(v_wsub, k + 1)
                fn(wgt[:, SEG * k:SEG * (k + 1), :], wgt[:, SEG * k:SEG * (k + 1), :], ACT.Exp).then_inc(a_wexp, 1)

            def coefficients(c, b):
                act.wait_ge(u_free, c * CH + 2 * CH)
                fn(gl[:, b, :], dot[:, b, :], ACT.Gelu_apprx_tanh).then_inc(a_gl, 1)
                act.wait_ge(v_cf, c + 1)
                for s in range(CH):
                    fn(diag[:, b, s, :], ident[:, :], ACT.Copy, scale=cf[:, b, s:s + 1]).then_inc(a_dg, 1)

            def score_out(m):
                act.wait_ge(p_sc, m + 1)
                fn(ssb[:, :, m, :], pb[:, 2 + m % 2, 0:TT * NK].rearrange("p (t k) -> p t k", t=TT),
                   ACT.Copy).then_inc(a_s, 1)

            for m in range(2 * PH + 1):
                if m == 2:
                    score_out(m - 1)
                if m < 2 * PH:
                    if T_WQ + m + SPLITS < T_PLAIN:
                        split_hi(m + SPLITS, T_WQ + m + SPLITS)
                    act.wait_ge(ring_used, T_WQ + m + 1)
                    fn(query[:, m % 4, :], pb[:, m % 2, 0:SEQ], ACT.Copy).then_inc(a_q, 1)
                if m >= 1 and m != 2:
                    score_out(m - 1)
                if m == M_CHUNK0 - 4:
                    unit_exp(0)
                if m == M_CHUNK0 - 1:
                    coefficients(0, 0)

            for k in range(UNITS):
                for b in range(SEG):
                    if b == 0 and k + 1 < UNITS:
                        unit_exp(k + 1)
                    if k or b:
                        coefficients(SEG * k + b, b)
            for t in range(TT):
                act.wait_ge(v_free, CH + NE * (t + 1))
                fn(junk, pb[:, 4 + 2 * t:6 + 2 * t, :].rearrange("p a b -> p (a b)"), ACT.Square,
                   accum_out=ss[:, 6 + t:7 + t]).then_inc(a_ss, 1)
                act.wait_ge(a_ss, 3 * TT + t + 1)
                fn(std[:, 6 + t:7 + t], ss[:, 6 + t:7 + t], ACT.Sqrt, scale=1.0 / D, bias=eps[:, :]).then_inc(a_std, 1)

        @block.vector
        def _(dve):
            V_ = nc.vector
            ch = Chain(dve, v_chain)
            dve.sem_inc(u_free, CH)

            def ada_part(i, landed, n, w=adaw):
                for s in range(8):
                    dve.wait_ge(landed[s], n * 16 + 16)
                    V_.tensor_tensor_reduce(out=w[:, s, :], in0=w[:, s, :], in1=cact, scale=1.0, scalar=0.0,
                                            op0=ALU.mult, op1=ALU.add, accum_out=modst[:, s:s + 1]
                                            ).then_inc(ada_used, 1)
                dve.wait_ge(ada_used, i * 8 + 8)
                ch.link(V_.tensor_tensor(mod[:, bass.ds(i * 8, 8)], modst[:, :], cols[:, bass.ds(i * 8 + C_BADA, 8)], ALU.add))

            dve.wait_ge(a_c, 1)
            dve.wait_ge(s_cols, 16)
            ada_part(0, ada_in, 0, adaw0)
            dve.wait_ge(a_std, 1)
            ch.link(V_.reciprocal(rstd[:, 0:TT], std[:, 0:TT]))
            for t in range(TT):
                V_.tensor_scalar(xs[:, t, :], x[:, t, :], rstd[:, t:t + 1], None, ALU.mult).then_inc(v_xs, 1)
            ada_part(1, ada_in1, 0)

            def split_x(j, n):
                dve.wait_ge(x_hi, n + 1)
                V_.tensor_tensor(xlo[:, j, :], y[:, j, :], xhi[:, j, :].bitcast(F32), ALU.subtract).then_inc(x_lo, 1)

            ch.link(V_.scalar_tensor_tensor(out=A1[:, :], in0=mod[:, 8:16], scalar=1.0, in1=cols[:, C_GPM:C_GPM + DT],
                                            op0=ALU.add, op1=ALU.mult))
            for j in range(DT):
                dve.wait_ge(p_xT, j // 2 + 1)
                o = (j % 2) * SEQ
                V_.tensor_scalar(y[:, j, :], pb[:, 4 + j // 2, o:o + SEQ], A1[:, j:j + 1], mod[:, j:j + 1],
                                 ALU.mult, ALU.add).then_inc(v_hT, 1)
                if j:
                    split_x(j - 1, j - 1)
            split_x(DT - 1, DT - 1)

            ch.link(V_.memset(upad[:, :, 0:PADT], 0.0))
            ada_part(2, ada_more, 0)
            with dve.Fori(0, 2) as r:
                ch.enter(r, 4 * TAPS + 4 - 4 + 1)
                for jj in range(4):
                    dve.wait_ge(a_evac, r * 8 + (2 * jj + 2))
                    u = upad[:, r * 4 + jj, PADT:PADT + SEQ]
                    last = V_.tensor_tensor(u, u, y[:, r * 4 + jj, :], ALU.mult)
                    n = ch.add(last)
                dve.wait_ge(v_chain, n)
                for k in range(TAPS):
                    for jj in range(4):
                        j = r * 4 + jj
                        w = cols[:, bass.ds(j * TAPS + (C_CW + k), 1)]
                        if k == 0:
                            ins = V_.tensor_scalar(y[:, j, :], upad[:, j, 0:SEQ], w, cols[:, bass.ds(j + C_CB, 1)],
                                                   ALU.mult, ALU.add)
                        else:
                            dve.wait_ge(v_chain, n - 3 + (jj if k == TAPS - 1 else 0))
                            ins = V_.scalar_tensor_tensor(out=y[:, j, :], in0=upad[:, j, k:k + SEQ], scalar=w,
                                                          in1=y[:, j, :], op0=ALU.mult, op1=ALU.add)
                        if k < TAPS - 1:
                            n = ch.add(ins)
                        elif jj == 3:
                            ins.then_inc(v_y, 1)
                dve.wait_ge(v_y, r + 1)
                ada_part(r + 3, ada_more, r + 1)
            ch.leave(2)
            ada_part(5, ada_more, 3)
            ch.add(V_.tensor_tensor(vec4[:, 0, :], mod[:, 16:24], cols[:, C_GOM:C_GOM + DT], ALU.mult))
            ch.add(V_.scalar_tensor_tensor(out=vec4[:, 1, :], in0=mod[:, 32:40], scalar=1.0,
                                           in1=cols[:, C_GPF:C_GPF + DT], op0=ALU.add, op1=ALU.mult))
            ch.add(V_.tensor_copy(vec4[:, 2, :], mod[:, 24:32]))
            ch.link(V_.tensor_tensor(vec4[:, 3, :], mod[:, 40:48], cols[:, C_GOF:C_GOF + DT], ALU.mult))

            dve.wait_ge(a_evac, T_V)
            dve.wait_ge(s_small, 64)
            dve.wait_ge(v_hT, DT)

            def blocks(v):
                return v.rearrange("p (c l) -> p c l", l=CMP_ST)

            for dst, half in ((kcA, 0), (kcB, 1)):
                V_.tensor_tensor(dst.rearrange("p (g c l) -> p g c l", g=GROUPS, l=CMP_ST),
                                 kT[:, :, 0, :].rearrange("p g (c l) -> p g c l", l=CMP_ST),
                                 posk[:, half * CMP_ST:(half + 1) * CMP_ST].unsqueeze(1).unsqueeze(1).broadcast_to(
                                     (P, GROUPS, NBLK, CMP_ST)), ALU.add).then_inc(v_pos, 1)
            n = GROUPS * NBLK
            V_.tensor_tensor(blocks(vcAB[0:DV, :]), blocks(vcf[0:DV, :]),
                             posv[0:DV, :].unsqueeze(1).broadcast_to((DV, n, CMP_ST)), ALU.add).then_inc(v_pos, 1)
            V_.tensor_tensor(blocks(vcAB[DV:P, 0:(n - 1) * CMP_ST]), blocks(vcf[DV:P, CMP_ST:]),
                             posv[DV:P, :].unsqueeze(1).broadcast_to((DV, n - 1, CMP_ST)), ALU.add).then_inc(v_pos, 1)

            dve.wait_ge(p_mean, 1)
            ch.link(V_.tensor_tensor(y[:, :, :], y[:, :, :],
                                     pb[:, 4, 0:SEQ].unsqueeze(1).broadcast_to((P, DT, SEQ)), ALU.subtract))
            V_.tensor_tensor(upad[:, :, 0:SEQ], y[:, :, :], y[:, :, :], ALU.mult).then_inc(v_sq, 1)
            dve.wait_ge(a_stdc, 1)
            ch.link(V_.reciprocal(stdc[:, :], stdc[:, :]))
            dve.wait_ge(v_sq, 1)
            V_.tensor_tensor(y[:, :, :], y[:, :, :], stdc[:, :].unsqueeze(1).broadcast_to((P, DT, SEQ)),
                             ALU.mult).then_inc(v_yn, 1)
            for j in range(DT):
                split_x(j, DT + j)
            dve.wait_ge(a_v, 6)
            dve.wait_ge(g_rowok, 2)
            ch.add(V_.tensor_scalar(gates[:, 0, 0, :], gates[:, 0, 0, :], rowok[:, :], None, ALU.mult))
            for j in range(DT):
                dve.wait_ge(ring_used, T_CO + j + 1)
                V_.tensor_tensor(upad[:, j, 0:SEQ], pb[:, j % 4, 0:SEQ], sig[:, DT + j, :], ALU.mult).then_inc(v_zb, 1)

            dve.wait_ge(tb_in, 16)
            dve.wait_ge(g_rowok, 2)
            for tt, n in ((0, NFAR), (1, NCMP)):
                o = P - tt * P + CMP_L - 1
                ch.link(V_.tensor_copy(tbc[:, tt, :, 0:n], tb[:, :, o:o + (n - 1) * CMP_ST + 1:CMP_ST]))
            dve.wait_ge(p_vc, 1)

            def cmp_logits(gi):
                tt, g = group_of(gi)
                dve.wait_ge(p_cs, gi + 1)
                if gi >= 1:
                    dve.wait_ge(p_ct, gi)
                V_.scalar_tensor_tensor(out=Sc[:, :, :],
                                        in0=pb[:, 4, 0:REP * NCMP].rearrange("p (h n) -> p h n", h=REP),
                                        scalar=SCALE, in1=tbc[:, tt, g * REP:(g + 1) * REP, :],
                                        op0=ALU.mult, op1=ALU.add).then_inc(v_cs, 1)
                dve.wait_ge(v_cs, gi + 1)
                ch.link(V_.tensor_reduce(nmc[:, :], Sc[:, :, :], AX, ALU.max))
                V_.tensor_tensor(Sc[:, :, :], Sc[:, :, :], nmc[:, :].unsqueeze(2).broadcast_to((P, REP, NCMP)),
                                 ALU.subtract).then_inc(v_csub, 1)

            def logits(n):
                tt, h, g, hh, keys = unit_keys(n)
                dve.wait_ge(p_s, n + 1)
                if n >= 2:
                    dve.wait_ge(p_t, n - 1)
                V_.scalar_tensor_tensor(out=S[:, n % 2, :, 0:keys],
                                        in0=pb[:, n % 2, :].rearrange("p (b t) -> p b t", b=2)[:, :, 0:keys],
                                        scalar=SCALE,
                                        in1=tb[:, h, SEQ - keys:SEQ].unsqueeze(1).broadcast_to((P, 2, keys)),
                                        op0=ALU.mult, op1=ALU.add).then_inc(v_st, 1)
                dve.wait_ge(v_st, n + 1)
                V_.tensor_reduce(nm[:, n % 2, :], S[:, n % 2, :, 0:keys], AX, ALU.max, negate=True).then_inc(v_mx, 1)

            def combine(gi, pr):
                tt, g = group_of(gi)
                hs = slice(2 * pr, 2 * pr + 2)
                o = g * REP + 2 * pr
                c = 2 * gi + pr + 1
                dve.wait_ge(a_exp, 2 * REP * gi + 4 * (pr + 1))
                ch.link(V_.reciprocal(rz[:, hs, :], Z[:, gi % 2, hs, :]))
                V_.tensor_tensor(coef[:, hs, :], rz[:, hs, :], gates[:, tt, :, o:o + 2].rearrange("p b h -> p h b"),
                                 ALU.mult).then_inc(v_coef, 1)
                dve.wait_ge(v_coef, c)
                dve.wait_ge(p_o, REP * gi + 2 * (pr + 1))
                V_.tensor_tensor(otmp[:, pr, :].rearrange("p (c d) -> p c d", d=DV),
                                 pb[:, 6 + pr, 0:6 * DV].rearrange("p (c d) -> p c d", d=DV),
                                 coef[:, hs, :].rearrange("p h b -> p (h b)").unsqueeze(2).broadcast_to((P, 6, DV)),
                                 ALU.mult).then_inc(v_o, 1)
                dve.wait_ge(v_o, c)
                V_.tensor_reduce(attn[:, tt, o * DV:(o + 2) * DV].rearrange("p (h d) -> p h d", d=DV),
                                 otmp[:, pr, :].rearrange("p (h b d) -> p h d b", h=2, b=3),
                                 AX, ALU.add).then_inc(v_at, 1)
                dve.wait_ge(v_at, c)

            for n in range(NU + 2):
                gi = n // REP
                if n < NU:
                    if n % REP == 0:
                        cmp_logits(gi)
                    logits(n)
                    if n % REP == 1:
                        dve.wait_ge(a_cexp, gi + 1)
                        ch.add(V_.tensor_reduce(Z[:, gi % 2, :, 0], Sc[:, :, :], AX, ALU.add))
                if n % REP == 1 and n > REP:
                    combine(gi - 1, 1)
                if n % REP == 3:
                    combine(gi, 0)

            wide_bank = (0, 1, 6, 7)

            def row(v):
                if v:
                    dve.wait_ge(p_row, v)
                else:
                    dve.wait_ge(p_t, NU)
                V_.tensor_copy(wide, vec4[:, v, :].unsqueeze(2).broadcast_to((P, DT, P))).then_inc(v_row, 1)

            for t in range(TT):
                for jj in range(2):
                    dve.wait_ge(x_hi, 2 * DT + 2 * t + jj + 1)
                    part = (slice(None), slice(4 * jj, 4 * jj + 4), slice(t * P, (t + 1) * P))
                    V_.tensor_tensor(xlo[part], pb[:, 2 + 2 * t + jj, :].rearrange("p (j t) -> p j t", j=4),
                                     xhi[part].bitcast(F32), ALU.subtract).then_inc(x_lo, 1)
            row(0)
            dve.wait_ge(p_o, NU)
            for j in range(DT):
                dve.wait_ge(ring_used, T_AO + j + 1)
                ch.link(V_.tensor_tensor(tmp[:, 0:SEQ], pb[:, wide_bank[j % 4], 0:SEQ], sig[:, j, :], ALU.mult))
                V_.tensor_tensor(y[:, j, :], tmp[:, 0:SEQ], upad[:, j, 0:SEQ], ALU.add).then_inc(v_m, 1)
                dve.wait_ge(v_m, j + 1)
            row(1)
            for j in range(DT):
                split_x(j, 2 * DT + 4 + j)
            for v in range(2, 4):
                row(v)

            dve.wait_ge(ring_used, T_WQ)
            dve.wait_ge(a_row, 1)
            for t in (1, 0):
                if t == 0:
                    dve.wait_ge(a_ss, TT + 1)
                V_.tensor_tensor(scaled[t], pb[:, 6 * t:6 * t + 2, :].rearrange("p a b -> p (a b)"), rows[0],
                                 ALU.mult).then_inc(v_sc, 1)
            dve.wait_ge(v_sc, 2)
            dve.wait_ge(a_std, 2)
            ch.link(V_.reciprocal(rstd[:, 2:4], std[:, 2:4]))
            for t in range(TT):
                V_.scalar_tensor_tensor(out=x[:, t, :], in0=scaled[t], scalar=rstd[:, 2 + t:3 + t], in1=x[:, t, :],
                                        op0=ALU.mult, op1=ALU.add).then_inc(v_x2, 1)
            dve.wait_ge(a_row, 4)
            for t in range(TT):
                dve.wait_ge(v_x2, t + 1)
                V_.tensor_tensor(scaled[t], x[:, t, :], rows[1], ALU.mult).then_inc(v_sc, 1)
            dve.wait_ge(v_sc, 2 + TT)
            dve.wait_ge(a_std, 3)
            ch.link(V_.reciprocal(rstd[:, 4:6], std[:, 4:6]))
            for t in range(TT):
                V_.scalar_tensor_tensor(out=h2[:, t, :], in0=scaled[t], scalar=rstd[:, 4 + t:5 + t], in1=rows[2],
                                        op0=ALU.mult, op1=ALU.add).then_inc(v_h2, 1)
            dve.wait_ge(v_h2, TT)
            for b in range(4):
                dve.wait_ge(x_hi, 3 * DT + 4 + b + 1)
                V_.tensor_tensor(xlo[:, 2 * b:2 * b + 2, :], pb[:, 2 + b, :].rearrange("p (a t) -> p a t", a=2),
                                 xhi[:, 2 * b:2 * b + 2, :].bitcast(F32), ALU.subtract).then_inc(x_lo, 1)

            def top16(n_rows, src, work, vals, idxs):
                for m in range(n_rows):
                    n = ch.add(V_.max(vals(m)[:, 0:8], src(m)))
                dve.wait_ge(v_chain, n)
                for m in range(n_rows):
                    ch.add(V_.max_index(idxs(m)[:, 0:8], vals(m)[:, 0:8], src(m)))
                    n = ch.add(V_.match_replace(work(m), vals(m)[:, 0:8], src(m), -3.0e38))
                dve.wait_ge(v_chain, n)
                for m in range(n_rows):
                    n = ch.add(V_.max(vals(m)[:, 8:16], work(m)))
                dve.wait_ge(v_chain, n)
                for m in range(n_rows):
                    n = ch.add(V_.max_index(idxs(m)[:, 8:16], vals(m)[:, 8:16], work(m)))
                dve.wait_ge(v_chain, n)

            def retrieve(k):
                t, q = divmod(k, CPT // SEG)
                dve.wait_ge(a_s, 2 * HU * (q + 1))
                top16(2 * HU, lambda m: ssb[:, t, 2 * HU * q + m, :], lambda m: swork[:, m, :],
                      lambda m: v16[:, m, :], lambda m: i16[:, m, :])
                ch.add(V_.tensor_copy(i16f[:, :, :], i16[:, :, :]))
                pair = v16[:, :, :].rearrange("p (h c) k -> p h c k", c=2)
                for h in range(HU):
                    n = ch.add(V_.tensor_tensor(cand[:, h, :].rearrange("p (a b) -> p a b", a=TOPK),
                                                pair[:, h, 0, :].unsqueeze(2).broadcast_to((P, TOPK, TOPK)),
                                                pair[:, h, 1, :].unsqueeze(1).broadcast_to((P, TOPK, TOPK)), ALU.add))
                dve.wait_ge(v_chain, n)
                top16(HU, lambda h: cand[:, h, :], lambda h: cwork[:, h, :], lambda h: t16[:, h, :],
                      lambda h: p16[:, h * TOPK:(h + 1) * TOPK])
                ch.add(V_.tensor_single_scalar(pa[:, 0, :], p16[:, :], 4, ALU.logical_shift_right))
                ch.link(V_.tensor_single_scalar(pa[:, 1, :], p16[:, :], TOPK - 1, ALU.bitwise_and))
                ch.link(V_.tensor_copy(paf[:, :, :], pa[:, :, :]))
                ch.link(V_.tensor_tensor(oneh, iota16[:, :].unsqueeze(1).unsqueeze(1).broadcast_to((P, 2, TOPK, TOPK)),
                                         paf[:, :, :].unsqueeze(3).broadcast_to((P, 2, TOPK, TOPK)), ALU.is_equal))
                ch.link(V_.tensor_tensor(oneh, oneh, i16f[:, :, :].unsqueeze(2).broadcast_to((P, 2, TOPK, TOPK)),
                                         ALU.mult))
                ch.link(V_.tensor_reduce(e12[:, :, :], oneh, AX, ALU.add))
                V_.scalar_tensor_tensor(out=idx[:, SEG * k:SEG * (k + 1), :].rearrange("p a b -> p (a b)"),
                                        in0=e12[:, 0, :], scalar=float(NK), in1=e12[:, 1, :],
                                        op0=ALU.mult, op1=ALU.add).then_inc(v_idx, 1)
                V_.tensor_tensor(weights(k), t16[:, :, :], t16[:, :, 0:1].broadcast_to((P, HU, TOPK)),
                                 ALU.subtract).then_inc(v_wsub, 1)
                dve.wait_ge(v_wsub, k + 1)

            def weights(k):
                return wgt[:, SEG * k:SEG * (k + 1), :].rearrange("p a b -> p (a b)").rearrange(
                    "p (h k) -> p h k", h=HU)

            def softmax_sum(k):
                w = weights(k)
                dve.wait_ge(a_wexp, k + 1)
                ch.link(V_.tensor_reduce(wsum[:, :], w, AX, ALU.add))
                ch.link(V_.reciprocal(wsum[:, :], wsum[:, :]))
                ch.link(V_.tensor_tensor(w, w, wsum[:, :].unsqueeze(2).broadcast_to((P, HU, TOPK)), ALU.mult))

            dve.wait_ge(g_const, 4)
            retrieve(0)
            for k in range(UNITS):
                t = k * SEG // CPT
                if k + 1 < UNITS:
                    retrieve(k + 1)
                for b in range(SEG):
                    c = SEG * k + b
                    for s in range(CH):
                        dve.wait_ge(u_in[s], c * 16 + 16)
                        V_.tensor_tensor_reduce(out=urow[:, s, :], in0=urow[:, s, :], in1=h2[:, t, :], scale=1.0,
                                                scalar=0.0, op0=ALU.mult, op1=ALU.add,
                                                accum_out=dot[:, b, s:s + 1]).then_inc(u_free, 1)
                    if b == 0:
                        softmax_sum(k)
                    dve.wait_ge(a_gl, c + 1)
                    V_.tensor_tensor(cf[:, b, :], gl[:, b, :], wgt[:, c, :], ALU.mult).then_inc(v_cf, 1)

            for t in range(TT):
                dve.wait_ge(a_ss, 3 * TT + t + 1)
                ch.link(V_.tensor_tensor(scaled[1], pb[:, 4 + 2 * t:6 + 2 * t, :].rearrange("p a b -> p (a b)"),
                                         rows[3], ALU.mult))
                dve.wait_ge(a_std, 4 + t)
                ch.link(V_.reciprocal(rstd[:, 6 + t:7 + t], std[:, 6 + t:7 + t]))
                V_.scalar_tensor_tensor(out=x[:, t, :], in0=scaled[1], scalar=rstd[:, 6 + t:7 + t], in1=x[:, t, :],
                                        op0=ALU.mult, op1=ALU.add).then_inc(v_out, 1)
                dve.wait_ge(v_out, t + 1)


def bucket(dist):
    exact = BUCKETS // 2
    nf = np.maximum(dist, 1).astype(np.float32)
    big = exact + (np.log(nf / np.float32(exact)) / np.float32(np.log(MAXDIST / exact)) * np.float32(BUCKETS - exact)).astype(np.int32)
    b = np.where(dist < exact, dist, np.minimum(big, BUCKETS - 1))
    return np.where(dist < 0, BUCKETS, b)


def onehot(dist):
    return (bucket(dist)[None] == np.arange(BUCKETS + 1).reshape((-1,) + (1,) * dist.ndim)).astype(np.float32)


def column_tiles(w, width):
    n = w.shape[1] // width
    t = np.zeros((n, P, DT, P), w.dtype)
    t[:, :, :, 0:width] = w.reshape(DT, P, n, width).transpose(2, 1, 0, 3)
    return t.reshape(n, P, D)


def rows128(v):
    return np.concatenate([v, np.zeros((P - v.shape[0],) + v.shape[1:], v.dtype)], axis=0)


def kernel(**inputs):
    import concourse.bacc as _bacc
    from concourse.bass_utils import run_bass_kernel_spmd as _run

    f = {n: np.ascontiguousarray(v) for n, v in inputs.items()}
    w_in = f["w_in"][0]
    sizes = [HEADS * DQK] + [GROUPS * DQK] * 3 + [GROUPS * DV] * 3 + [3 * HEADS, 2 * D, 2 * D]
    at = np.cumsum([0] + sizes)
    q, kc, ks, kw, vc, vs, vw, gn, glu, gm = (w_in[:, at[i]:at[i + 1]] for i in range(10))
    vc2 = np.tile(vc.reshape(D, GROUPS, 1, DV), (1, 1, 2, 1)).reshape(D, GROUPS * P)
    glu_t = column_tiles(glu, P)
    q_t, kc_t, ks_t, kw_t, vc_t = column_tiles(q, DQK), column_tiles(kc, DQK), column_tiles(ks, DQK), column_tiles(kw, DQK), column_tiles(vc2, P)
    vtile = np.zeros((DT, P, D), w_in.dtype)
    vtile[:, :, 0:256] = vs.reshape(DT, P, 256)
    vtile[:, :, 256:512] = vw.reshape(DT, P, 256)
    vtile[:, :, 512:560] = gn.reshape(DT, P, 48)
    stream = [glu_t.reshape(2, DT, P, D).transpose(1, 0, 2, 3).reshape(2 * DT, P, D), column_tiles(gm, P)]
    for g in range(GROUPS):
        stream += [q_t[g * REP:(g + 1) * REP], kc_t[g:g + 1], ks_t[g:g + 1], kw_t[g:g + 1], vc_t[g:g + 1]]
    stream += [vtile, column_tiles(f["w_conv_out"][0], P), column_tiles(f["w_attn_out"][0], P),
               f["w_out"][0].reshape(DT, P, D), column_tiles(f["peer_wq"][0], P)]

    def col(v):
        return v.reshape(-1, P).T

    cols = np.concatenate([col(f[n][0]) for n in ("b_ada", "g_pre_mix", "g_post_mix", "g_pre_ffn", "g_post_ffn",
                                                  "conv_b", "conv_ln_g", "conv_ln_b")]
                          + [f["conv_w"][0, :, 0, :].reshape(TAPS, DT, P).transpose(2, 1, 0).reshape(P, -1)], axis=1)
    j = np.arange(512)
    arrays = {
        "x": f["x"][0], "c": f["c"][0],
        "w_ada": f["w_ada"][0].T.reshape(48, P, D),
        "w_stream": np.concatenate(stream, axis=0),
        "cols": cols,
        "rel_table": f["rel_table"],
        "onehot_rev": onehot(SEQ - 1 - j),
        "w1k": rows128(f["cmp_w1k"][0].reshape(CMP_L, DQK, HID).transpose(1, 0, 2)),
        "w1v": f["cmp_w1v"][0].reshape(2, CMP_ST, DV, HID).transpose(0, 2, 1, 3).reshape(P, CMP_ST, HID),
        "w2k": f["cmp_w2k"][0].reshape(2, P, DQK).transpose(1, 0, 2),
        "w2v": f["cmp_w2v"][0].reshape(2, P, DV).transpose(1, 0, 2),
        "pos_k": rows128(f["cmp_pos_k"][0].T),
        "pos_v": f["cmp_pos_v"][0].reshape(2, CMP_ST, DV).transpose(0, 2, 1).reshape(P, CMP_ST),
        "subkeys": f["peer_subkeys"][0].reshape(2 * PH, NK, P).transpose(2, 0, 1),
        "peer_u": f["peer_u"][0], "peer_v": f["peer_v"][0],
    }
    nc = _bacc.Bacc("TRN2", target_bir_lowering=False, num_devices=1)
    feed, aps = {}, {}
    for name, v in arrays.items():
        v = np.ascontiguousarray(v)
        feed[f"in_{name}"] = v
        aps[name] = nc.dram_tensor(f"in_{name}", v.shape, mybir.dt.from_np(v.dtype), kind="ExternalInput").ap()
    o = nc.dram_tensor("out_y", (SEQ, D), F32, kind="ExternalOutput").ap()
    build(nc, aps, o)
    r = _run(nc, [feed], core_ids=[0])
    return r.results[0]["out_y"].reshape(1, SEQ, D)
```
